# Optimizing a Trainium2 kernel written in Bass

```python
import math
import jax, jax.numpy as jnp
from jax import lax
import numpy as np

D_MODEL = 1024
BATCH = 1
SEQ = 512
DEPTH = 2
DEC_BATCH = 8
DEC_SEQ = 8
PAST_LEN = 2048
PAGE_SIZE = 128

N_EVEN = (DEPTH + 1) // 2
N_ODD = DEPTH // 2
RMS_EPS = 1e-6
D_A = D_MODEL // 2
POOL_WINDOWS = (2, 4, 8, 16)
POOL_GROUP = D_A // len(POOL_WINDOWS)
POOL_HIST = max(POOL_WINDOWS) - 1
H_B = 4
HD_B = 64
D_B = H_B * 2 * HD_B
Q_BLOCK = 128
D_C = D_MODEL // 2
CONV_W = 3
D_WINDOWS = ((128, 1), (512, 4), (2048, 16))
H_DG = 8
HD_D = 64
D_DG = H_DG * HD_D
D_FF = 4 * D_MODEL
D_IN_AB = D_A + 3 * D_B
D_IN_CD = 3 * D_C + 3 * len(D_WINDOWS) * D_DG
D_MIX_AB = D_A + D_B
D_MIX_CD = D_C + D_DG

kernel_name = "hybrid_pool_diffattn_shortconv_dilated_step"

def rmsnorm(x, g):
    xf = x.astype(jnp.float32)
    y = xf * lax.rsqrt(jnp.mean(xf * xf, axis=-1, keepdims=True) + RMS_EPS)
    return (y * g.astype(jnp.float32)).astype(x.dtype)

def mlp(h, w_up, w_down):
    return jnp.square(jax.nn.relu(h @ w_up)) @ w_down

def pool_mix(u, hist, pos0, a_mix, a_scale):
    B, T, _ = u.shape
    ext = jnp.concatenate([hist.astype(u.dtype), u], axis=1)
    cs = jnp.pad(jnp.cumsum(ext.astype(jnp.float32), axis=1), ((0, 0), (1, 0), (0, 0)))
    end = cs[:, POOL_HIST + 1:POOL_HIST + 1 + T]
    pos = pos0 + jnp.arange(T)
    means = []
    for gi, w in enumerate(POOL_WINDOWS):
        sl = slice(gi * POOL_GROUP, (gi + 1) * POOL_GROUP)
        start = cs[:, POOL_HIST + 1 - w:POOL_HIST + 1 - w + T, sl]
        cnt = jnp.minimum(pos + 1, w).astype(jnp.float32)[None, :, None]
        means.append((end[..., sl] - start) / cnt)
    p = (jnp.concatenate(means, axis=-1) - u.astype(jnp.float32)).reshape(B, T, len(POOL_WINDOWS), POOL_GROUP)
    y = jnp.einsum('btgc,gcd->btgd', p, a_mix.astype(jnp.float32)).reshape(B, T, D_A) * a_scale.astype(jnp.float32)
    return y.astype(u.dtype), ext[:, -POOL_HIST:]

def short_conv(z, hist, w):
    T = z.shape[1]
    ext = jnp.concatenate([hist.astype(z.dtype), z], axis=1)
    y = ext[:, 0:T] * w[0]
    for j in range(1, CONV_W):
        y = y + ext[:, j:j + T] * w[j]
    return y, ext[:, -(CONV_W - 1):]

def diff_attn_core(q, ks, vs, masks, lam, lam_init, subln_g):
    B, Tq = q.shape[:2]
    logits = jnp.concatenate([jnp.einsum('bqhmd,bkhmd->bhmqk', q, k) for k in ks], axis=-1).astype(jnp.float32) * (HD_B ** -0.5)
    logits = jnp.where(jnp.concatenate(masks, axis=-1), logits, -jnp.inf)
    p = jax.nn.softmax(logits, axis=-1)
    a = p[:, :, 0] - lam * p[:, :, 1]
    o = None
    off = 0
    for v in vs:
        n = v.shape[1]
        part = jnp.einsum('bhqk,bkhe->bqhe', a[..., off:off + n].astype(v.dtype), v)
        o = part if o is None else o + part
        off += n
    o = rmsnorm(o, subln_g) * (1.0 - lam_init)
    return o.reshape(B, Tq, D_B)

def diff_attn_prompt(q, k, v, lam, lam_init, subln_g):
    B, S = q.shape[:2]
    nb = S // Q_BLOCK
    qb = jnp.moveaxis(q.reshape(B, nb, Q_BLOCK, H_B, 2, HD_B), 1, 0)
    qpos = jnp.arange(S).reshape(nb, Q_BLOCK)
    kpos = jnp.arange(S)

    def blk(args):
        qi, pi = args
        return diff_attn_core(qi, [k], [v], [kpos[None, :] <= pi[:, None]], lam, lam_init, subln_g)

    o = lax.map(blk, (qb, qpos))
    return jnp.moveaxis(o, 0, 1).reshape(B, S, D_B)

def dilated_prompt(q, k, v, dil, nback):
    B, S, H, E = q.shape
    L = S // dil
    nb = -(-L // nback)
    Lp = nb * nback

    def streams(a):
        a = a.reshape(B, L, dil, H, E).transpose(0, 2, 1, 3, 4)
        return jnp.pad(a, ((0, 0), (0, 0), (0, Lp - L), (0, 0), (0, 0))).reshape(B, dil, nb, nback, H, E)

    def with_prev(a):
        prev = jnp.pad(a, ((0, 0), (0, 0), (1, 0), (0, 0), (0, 0), (0, 0)))[:, :, :-1]
        return jnp.concatenate([prev, a], axis=3)

    qb = streams(q)
    kc = with_prev(streams(k))
    vc = with_prev(streams(v))
    logits = jnp.einsum('brnqhe,brnkhe->brnhqk', qb, kc).astype(jnp.float32) * (HD_D ** -0.5)
    qi = jnp.arange(nback)[:, None]
    kk = jnp.arange(2 * nback)[None, :]
    dist = qi - kk + nback
    band = (dist >= 0) & (dist <= nback)
    valid = (jnp.arange(nb)[:, None, None] * nback + kk[None] - nback) >= 0
    mask = band[None] & valid
    logits = jnp.where(mask[:, None], logits, -jnp.inf)
    lse = jax.nn.logsumexp(logits, axis=-1)
    p = jnp.exp(logits - lse[..., None])
    o = jnp.einsum('brnhqk,brnkhe->brnqhe', p.astype(v.dtype), vc)
    o = o.reshape(B, dil, Lp, H, E)[:, :, :L].transpose(0, 2, 1, 3, 4).reshape(B, S, H, E)
    lse = jnp.moveaxis(lse, -1, 3).reshape(B, dil, Lp, H)[:, :, :L].transpose(0, 2, 1, 3).reshape(B, S, H)
    return o, lse

def dilated_sample(q, k_ext, v_ext, dil, nback):
    B, T = q.shape[:2]
    Lb = k_ext.shape[1] - T
    idx = Lb + jnp.arange(T)[:, None] - dil * jnp.arange(nback + 1)[None, :]
    valid = idx >= 0
    idx = jnp.maximum(idx, 0)
    kg = k_ext[:, idx]
    vg = v_ext[:, idx]
    logits = jnp.einsum('bqhe,bqkhe->bhqk', q, kg).astype(jnp.float32) * (HD_D ** -0.5)
    logits = jnp.where(valid, logits, -jnp.inf)
    lse = jax.nn.logsumexp(logits, axis=-1)
    p = jnp.exp(logits - lse[..., None])
    o = jnp.einsum('bhqk,bqkhe->bqhe', p.astype(v_ext.dtype), vg)
    return o, jnp.moveaxis(lse, 1, 2)

def even_mixer(h, w_in, w_out, a_mix, a_scale, b_lam, b_subln_g, lam_init, pool_hist, pos0, kv_past):
    B, T, _ = h.shape
    proj = h @ w_in
    u = proj[..., :D_A]
    q = proj[..., D_A:D_A + D_B].reshape(B, T, H_B, 2, HD_B)
    k_flat = proj[..., D_A + D_B:D_A + 2 * D_B].reshape(B, T, H_B, 2 * HD_B)
    v = proj[..., D_A + 2 * D_B:].reshape(B, T, H_B, 2 * HD_B)
    k = k_flat.reshape(B, T, H_B, 2, HD_B)
    a_out, new_hist = pool_mix(u, pool_hist, pos0, a_mix, a_scale)
    lf = b_lam.astype(jnp.float32)
    lam = jnp.exp(jnp.sum(lf[0] * lf[1])) - jnp.exp(jnp.sum(lf[2] * lf[3])) + lam_init
    if kv_past is None:
        o_b = diff_attn_prompt(q, k, v, lam, lam_init, b_subln_g)
    else:
        P = kv_past.shape[1]
        k_past = kv_past[:, :, 0].reshape(B, P, H_B, 2, HD_B).astype(k.dtype)
        v_past = kv_past[:, :, 1].astype(v.dtype)
        masks = [jnp.ones((T, P), bool), jnp.tril(jnp.ones((T, T), bool))]
        o_b = diff_attn_core(q, [k_past, k], [v_past, v], masks, lam, lam_init, b_subln_g)
    y = jnp.concatenate([a_out, o_b], axis=-1) @ w_out
    return y, new_hist, jnp.stack([k_flat, v], axis=2)

def odd_mixer(h, w_in, w_out, conv_w, conv_hist, d_bufs):
    B, T, _ = h.shape
    proj = h @ w_in
    b_gate = proj[..., :D_C]
    c_gate = proj[..., D_C:2 * D_C]
    hc = proj[..., 2 * D_C:3 * D_C]
    cv, new_conv = short_conv(c_gate * hc, conv_hist, conv_w)
    c_out = b_gate * cv
    outs, lses, new_bufs = [], [], []
    for g, (win, dil) in enumerate(D_WINDOWS):
        off = 3 * D_C + 3 * g * D_DG
        q = proj[..., off:off + D_DG].reshape(B, T, H_DG, HD_D)
        kv = proj[..., off + D_DG:off + 3 * D_DG].reshape(B, T, 2, H_DG, HD_D)
        nback = win // dil
        if d_bufs is None:
            o, lse = dilated_prompt(q, kv[:, :, 0], kv[:, :, 1], dil, nback)
            new_bufs.append(kv[:, T - min(win, T):])
        else:
            ext = jnp.concatenate([d_bufs[g].astype(kv.dtype), kv], axis=1)
            o, lse = dilated_sample(q, ext[:, :, 0], ext[:, :, 1], dil, nback)
            new_bufs.append(ext[:, T:])
        outs.append(o)
        lses.append(lse)
    wg = jax.nn.softmax(jnp.stack(lses, axis=0), axis=0)
    o_d = jnp.einsum('gbth,gbthe->bthe', wg.astype(h.dtype), jnp.stack(outs, axis=0)).reshape(B, T, D_DG)
    y = jnp.concatenate([c_out, o_d], axis=-1) @ w_out
    return y, new_conv, new_bufs

def setup_inputs(seed: int = 0) -> dict:
    key = jax.random.key(seed)
    ks = jax.random.split(key, 24)
    f32 = jnp.float32
    n_pages = PAST_LEN // PAGE_SIZE
    n_pool = (DEC_BATCH * n_pages * 5) // 4

    def nrm(k, shape, scale=1.0):
        return jax.random.normal(k, shape, f32) * scale

    page_table = jax.random.permutation(ks[0], n_pool)[:DEC_BATCH * n_pages].reshape(DEC_BATCH, n_pages).astype(jnp.int32)
    d_bufs = [nrm(ks[1 + g], (N_ODD, DEC_BATCH, min(w, PAST_LEN), 2, H_DG, HD_D)) for g, (w, _) in enumerate(D_WINDOWS)]
    return {
        'x_prompt': nrm(ks[4], (BATCH, SEQ, D_MODEL)),
        'x_sample': nrm(ks[5], (DEC_BATCH, DEC_SEQ, D_MODEL)),
        'state_a_pool': nrm(ks[6], (N_EVEN, DEC_BATCH, POOL_HIST, D_A)),
        'cache_b_kv': nrm(ks[7], (N_EVEN, n_pool, PAGE_SIZE, 2, H_B, 2 * HD_B)),
        'state_c_conv': nrm(ks[8], (N_ODD, DEC_BATCH, CONV_W - 1, D_C)),
        'cache_d0_kv': d_bufs[0],
        'cache_d1_kv': d_bufs[1],
        'cache_d2_kv': d_bufs[2],
        'page_table': page_table,
        'norm_mix_g': 1.0 + nrm(ks[9], (DEPTH, D_MODEL), 0.05),
        'norm_mlp_g': 1.0 + nrm(ks[10], (DEPTH, D_MODEL), 0.05),
        'norm_out_g': 1.0 + nrm(ks[11], (D_MODEL,), 0.05),
        'w_in_ab': nrm(ks[12], (N_EVEN, D_MODEL, D_IN_AB), D_MODEL ** -0.5),
        'w_out_ab': nrm(ks[13], (N_EVEN, D_MIX_AB, D_MODEL), D_MIX_AB ** -0.5),
        'a_mix': nrm(ks[14], (N_EVEN, len(POOL_WINDOWS), POOL_GROUP, POOL_GROUP), POOL_GROUP ** -0.5),
        'a_scale': 1.0 + nrm(ks[15], (N_EVEN, D_A), 0.1),
        'b_lam': nrm(ks[16], (N_EVEN, 4, HD_B), 0.1),
        'b_subln_g': 1.0 + nrm(ks[17], (N_EVEN, 2 * HD_B), 0.05),
        'w_in_cd': nrm(ks[18], (N_ODD, D_MODEL, D_IN_CD), D_MODEL ** -0.5),
        'w_out_cd': nrm(ks[19], (N_ODD, D_MIX_CD, D_MODEL), D_MIX_CD ** -0.5),
        'c_conv_w': nrm(ks[20], (N_ODD, CONV_W, D_C), CONV_W ** -0.5),
        'w_up': nrm(ks[21], (DEPTH, D_MODEL, D_FF), D_MODEL ** -0.5),
        'w_down': nrm(ks[22], (DEPTH, D_FF, D_MODEL), D_FF ** -0.5),
    }

def reference(x_prompt, x_sample, state_a_pool, cache_b_kv, state_c_conv, cache_d0_kv, cache_d1_kv, cache_d2_kv, page_table,
              norm_mix_g, norm_mlp_g, norm_out_g, w_in_ab, w_out_ab, a_mix, a_scale, b_lam, b_subln_g,
              w_in_cd, w_out_cd, c_conv_w, w_up, w_down):
    Bp = x_prompt.shape[0]
    Bs = x_sample.shape[0]
    past_len = page_table.shape[1] * cache_b_kv.shape[2]
    d_caches = (cache_d0_kv, cache_d1_kv, cache_d2_kv)
    xp, xs = x_prompt, x_sample
    pool_p, pool_s, bkv_p, bkv_s, conv_p, conv_s = [], [], [], [], [], []
    dbuf_p = [[] for _ in D_WINDOWS]
    dbuf_s = [[] for _ in D_WINDOWS]
    for layer in range(DEPTH):
        i = layer // 2
        hp = rmsnorm(xp, norm_mix_g[layer])
        hs = rmsnorm(xs, norm_mix_g[layer])
        if layer % 2 == 0:
            lam_init = 0.8 - 0.6 * math.exp(-0.3 * layer)
            kv_past = cache_b_kv[i][page_table].reshape(Bs, past_len, 2, H_B, 2 * HD_B)
            zero_hist = jnp.zeros((Bp, POOL_HIST, D_A), xp.dtype)
            yp, hist_p, kvp = even_mixer(hp, w_in_ab[i], w_out_ab[i], a_mix[i], a_scale[i], b_lam[i], b_subln_g[i],
                                         lam_init, zero_hist, 0, None)
            ys, hist_s, kvs = even_mixer(hs, w_in_ab[i], w_out_ab[i], a_mix[i], a_scale[i], b_lam[i], b_subln_g[i],
                                         lam_init, state_a_pool[i], past_len, kv_past)
            pool_p.append(hist_p)
            pool_s.append(hist_s)
            bkv_p.append(kvp)
            bkv_s.append(kvs)
        else:
            zero_conv = jnp.zeros((Bp, CONV_W - 1, D_C), xp.dtype)
            yp, cvp, bufs_p = odd_mixer(hp, w_in_cd[i], w_out_cd[i], c_conv_w[i], zero_conv, None)
            ys, cvs, bufs_s = odd_mixer(hs, w_in_cd[i], w_out_cd[i], c_conv_w[i], state_c_conv[i],
                                        [c[i] for c in d_caches])
            conv_p.append(cvp)
            conv_s.append(cvs)
            for g in range(len(D_WINDOWS)):
                dbuf_p[g].append(bufs_p[g])
                dbuf_s[g].append(bufs_s[g])
        xp = xp + yp
        xs = xs + ys
        xp = xp + mlp(rmsnorm(xp, norm_mlp_g[layer]), w_up[layer], w_down[layer])
        xs = xs + mlp(rmsnorm(xs, norm_mlp_g[layer]), w_up[layer], w_down[layer])
    y_prompt = rmsnorm(xp, norm_out_g)
    y_sample = rmsnorm(xs, norm_out_g)
    return (y_prompt, y_sample,
            jnp.stack(pool_p), jnp.stack(pool_s),
            jnp.stack(bkv_p), jnp.stack(bkv_s),
            jnp.stack(conv_p), jnp.stack(conv_s),
            jnp.stack(dbuf_p[0]), jnp.stack(dbuf_s[0]),
            jnp.stack(dbuf_p[1]), jnp.stack(dbuf_s[1]),
            jnp.stack(dbuf_p[2]), jnp.stack(dbuf_s[2]))


_drawn_inputs = setup_inputs


def setup_inputs(seed=0):
    import zlib

    import numpy as np

    out = dict(_drawn_inputs(seed))
    spreads = {}
    factors = {}
    for name, (base, spread) in spreads.items():
        noise = np.random.default_rng([zlib.crc32(name.encode()), seed]).standard_normal(out[name].shape)
        drawn = base * np.exp(spread * noise) if base else spread * noise
        out[name] = __import__('jax').numpy.asarray(drawn.astype(out[name].dtype))
    for name, factor in factors.items():
        out[name] = (out[name] * factor).astype(out[name].dtype)
    return out
```

```python
from contextlib import ExitStack, contextmanager

import numpy as np
import concourse.bass as bass
from concourse import mybir

F32 = mybir.dt.float32
F32R = mybir.dt.float32r
I32 = mybir.dt.int32
ALU = mybir.AluOpType
ACT = mybir.ActivationFunctionType
AX = mybir.AxisListType
ds = bass.ds

P = 128
D = 1024
KT_N = D // P
SEQ, NB, TS = 512, 8, 8
NS = NB * TS
N = SEQ + NS
NH = N // 2
EPS = 1e-6
LAM_INIT = 0.8 - 0.6
NEG = -1e30
PAST, PAGE = 2048, 128
NPAGES = PAST // PAGE
WIN, DIL = (128, 512, 2048), (1, 4, 16)
FF = 4 * D

T_AB, T_OA, T_M0 = 0, 16, 24
T_CD = T_M0 + 64
T_OC = T_CD + 48
T_M1 = T_OC + 8
T_END = T_M1 + 64

C = {}
_at = 0
for _n, _w in (("ident", 128), ("ones", 128), ("causal", 128), ("prev", 128), ("g2m", 128), ("rm2", 8), ("rm1", 4),
               ("k01", 4), ("g0m", 8), ("selfm", 360), ("sel", 32), ("halfm", 2), ("m01", 2), ("rtab", 16),
               ("sel8", 512)):
    C[_n] = (_at, _w)
    _at += _w
NC_ = (_at + 7) // 8 * 8


def constants():
    c = np.zeros((P, NC_), np.float32)

    def put(name, a):
        c[:a.shape[0], C[name][0]:C[name][0] + C[name][1]] = a

    i = np.arange(P)
    put("ident", np.eye(P))
    put("ones", np.ones((P, P)))
    put("causal", np.where(i[None] <= i[:, None], 0, NEG))
    put("prev", np.where(i[None] >= i[:, None], 0, NEG))
    r, l = i // 32, i % 32
    put("g2m", np.where((r[:, None] == r[None]) & (l[None] <= l[:, None]), 0, NEG))
    real = (i % 32) < 16
    t, half = i % 8, (i % 32) // 8
    put("rm2", np.where(real[:, None] & (t[:, None] != np.arange(8)[None]), NEG, 0))
    put("rm1", np.where(real[:, None] & (t[:, None] % 4 != np.arange(4)[None]), NEG, 0))
    put("k01", np.where(real[:, None] & (t[:, None] == np.arange(4)[None] + 4), NEG, 0))
    put("g0m", np.where(real[:, None] & (np.arange(8)[None] < t[:, None]), NEG, 0))
    sm = np.zeros((P, 3, 15, 8), np.float32)
    sm[real] = NEG
    for g in range(3):
        for row in i[real]:
            for t2 in range(8):
                if t2 <= t[row] and (t[row] - t2) % DIL[g] == 0:
                    sm[row, g, 7, t2] = 0
    put("selfm", sm.reshape(P, 360))
    sel = np.zeros((P, 32), np.float32)
    for row in i[real]:
        sel[row, (row // 32) * 8 + t[row]] = 1
    put("sel", sel)
    put("halfm", (half[:, None] == np.arange(2)[None]) & real[:, None])
    put("m01", (half[:, None] == np.arange(2)[None]) & real[:, None])
    put("rtab", np.broadcast_to(1.0 / (1.0 + np.arange(16)), (P, 16)))
    s8 = np.zeros((8, 4, P), np.float32)
    for h in range(8):
        s8[h, h % 4, 64 * (h // 4):64 * (h // 4) + 64] = 1
    put("sel8", s8.reshape(8, 512))
    return c


class Tally:

    def __init__(self):
        self.n, self.terms = 0, []

    def add(self, k=1):
        self.n += k
        return self.now()

    def now(self):
        v = self.n
        for reg, k in self.terms:
            v = reg * k + v
        return v

    @contextmanager
    def loop(self, reg, per, first, end):
        start = self.n
        self.n = start - first * per
        self.terms.append((reg, per))
        inner = self.n
        yield
        self.terms.pop()
        assert self.n - inner == per, (self.n - inner, per)
        self.n = start + per * (end - first)


def build(nc, a):
    with ExitStack() as ctx:
        sem = lambda name: ctx.enter_context(nc.semaphore(name))

        pp = [ctx.enter_context(nc.psum_tensor(f"pp{i}", [P, 1024], F32)) for i in range(4)]
        bank = [pp[i // 2][:, 512 * (i % 2):512 * (i % 2) + 512] for i in range(8)]
        halves = [pp[i][:, :].rearrange("p (h c) -> p h c", h=2)[:, :, 0:NH] for i in range(4)]
        acc = pp[0:2]
        acc_h = halves[0:2]

        base = nc.sbuf_base
        total = (nc.sbuf_usable_end - base) // 32 * 8 - 16
        ctx.enter_context(nc.sbuf_tensor("whole_map", [P, total], F32))
        base = (base + 31) // 32 * 32

        def at(name, word, words, dt=F32):
            assert word + words <= total, (name, word + words, total)
            return nc.alloc_sbuf_tensor_at(name, [P, words], dt, offset=base + 4 * word)

        def tiles(t, n, first=0):
            return t[:, first * N:(first + n) * N].rearrange("p (k n) -> p k n", n=N)

        W_X, W_A, W_B = 0, KT_N * N, 3 * KT_N * N
        W_RAW = W_B + 2 * KT_N * N
        W_W = W_RAW + 4096
        W_PROJ = W_W + 4096
        W_TMP = W_PROJ + 16 * N
        W_CONST = W_TMP + 6 * N
        W_G = W_CONST + NC_
        W_S = W_G + 64
        x = at("x", W_X, KT_N * N)
        a_hi, a_lo = at("a_hi", W_A, KT_N * N, F32R), at("a_lo", W_A + KT_N * N, KT_N * N, F32R)
        b_hi, b_lo = at("b_hi", W_B, KT_N * N, F32R), at("b_lo", W_B + KT_N * N, KT_N * N, F32R)
        xk = tiles(x, 8)
        ahk, alk, bhk, blk = (tiles(t, 8) for t in (a_hi, a_lo, b_hi, b_lo))
        raw = [at(f"raw{i}", W_RAW + 2048 * i, 2048) for i in range(2)]
        whi = [at(f"whi{i}", W_W + 1024 * i, 1024, F32R) for i in range(2)]
        wlo = [at(f"wlo{i}", W_W + 2048 + 1024 * i, 1024, F32R) for i in range(2)]
        raw_v = [t[:, :].rearrange("p (k j n) -> p k j n", k=KT_N, j=2) for t in raw]
        whi_v = [t[:, :].rearrange("p (k n) -> p k n", k=KT_N) for t in whi]
        wlo_v = [t[:, :].rearrange("p (k n) -> p k n", k=KT_N) for t in wlo]
        proj = at("proj", W_PROJ, 16 * N)
        pk = tiles(proj, 16)
        rnorm = at("rnorm", W_TMP, N)
        r_h = rnorm[:, :].rearrange("p (h c) -> p h c", h=2)
        zbuf = at("zbuf", W_TMP + N, 2 * N)
        sqbuf = at("sqbuf", W_TMP + 3 * N, 2 * N)
        sqsum = at("sqsum", W_TMP + 5 * N, N)
        dummy = at("dummy", total - 8, 1)
        con = at("con", W_CONST, NC_)
        gains = at("gains", W_G, 64)
        cc = lambda n: con[:, C[n][0]:C[n][0] + C[n][1]]
        ident, ones = cc("ident"), cc("ones")
        G_MIX, G_MLP, G_OUT, G_SCALE, G_CONV, G_SUBLN = 0, 16, 32, 40, 44, 56

        W_AX = W_A + 4 * 2048
        W_BH, W_BL = W_B + 4 * N, W_B + KT_N * N + 4 * N
        W_V, W_K, W_Q, W_E = W_S, W_S + 2048, W_S + 3072, W_S + 6144
        W_QST = W_S + 7168
        W_STAT = W_TMP + 3 * N
        x_tok = at("x_tok", W_PROJ, 5 * D)[:, :].rearrange("p (t d) -> p t d", d=D)
        gain_rows = at("gain_rows", W_S, P)
        kring = [at(f"kring{i}", W_A + 2048 * i, 2048) for i in range(2)]
        vring = [at(f"vring{i}", W_A + 4096 + 2048 * i, 2048) for i in range(2)]
        kring_v = [t[:, :].rearrange("p (g f) -> p g f", g=4) for t in kring]
        vring_v = [t[:, :].rearrange("p (g f) -> p g f", g=4) for t in vring]
        v_all = at("v_all", W_V, 2048)[:, :].rearrange("p (c f) -> p c f", c=4)
        k_tok = [at(f"k_tok{i}", W_K + 512 * i, 512) for i in range(2)]
        qkv_s = at("qkv_s", W_Q, 3072)[:, :].rearrange("p (g w) -> p g w", g=3)
        q_s = qkv_s[:, :, 0:256].rearrange("p g (i n) -> p g i n", i=4)
        k_s = qkv_s[:, :, 256:512].rearrange("p g (i n) -> p g i n", i=4)
        v_s = qkv_s[:, :, 512:1024]
        e2 = [at(f"e{i}", W_E + 512 * i, 512) for i in range(2)]
        q_st = at("q_st", W_QST, 384)[:, :].rearrange("p (g i c) -> p g i c", g=3, i=4)
        neglam = at("neglam", W_QST + 384, 2)
        pages = nc.alloc_sbuf_tensor_at("pages", [1, P], I32, offset=base + 4 * (W_Q + 2928))
        lam_in = at("lam_in", W_E, 256)
        lam_t = at("lam_t", W_E + 256, 132)
        pt_l0 = [at(f"pt_l0{i}", W_AX + 512 * i, 512) for i in range(2)]
        pt_l1 = [at(f"pt_l1{i}", W_PROJ + 12 * N + 512 * i, 512) for i in range(2)]
        hist_tok = at("hist_tok", W_STAT, 512)
        a_mix = at("a_mix", W_STAT + 640, 512)
        stat0 = at("stat0", W_STAT + 512, 128)
        e4 = [[e2[0], e2[1]], [at("e4a", W_BL, 512), at("e4b", W_BL + 512, 512)]]
        kt_l0 = at("kt_l0", W_BL, 2048)
        o_feat0 = at("o_feat0", W_BH, 4 * N)
        orun0 = at("orun0", W_V, 1024)
        pool_a = at("pool_a", W_Q + 1024, 2 * 528)[:, :].rearrange("p (i c) -> p i c", i=2)
        pool_s = at("pool_s", W_Q + 1024 + 1056, 2 * 184)[:, :].rearrange("p (i b c) -> p i b c", i=2, b=NB)
        hist_f = at("hist_f", W_Q + 1024 + 1056 + 368, 480)[:, :].rearrange("p (g b c) -> p g b c", g=4, b=NB)
        conv_tok = at("conv_tok", W_STAT, 512)
        stat1 = at("stat1", W_STAT + 512, 640)
        cv = at("cv", W_V, 2 * N)
        zext = at("zext", W_V + 2 * N, 320)[:, :].rearrange("p (k b c) -> p k b c", k=4, b=NB)
        kt_l1 = at("kt_l1", W_PROJ, 2048)
        orun1 = at("orun1", W_PROJ + 2048, 1024)
        o_g = [at("o_g0", W_BH, 4 * N), at("o_g1", W_BL, 4 * N), at("o_g2", W_PROJ + 8 * N, 4 * N)]
        nm = [at(f"nm{g}", W_V + 512 * g, 512) for g in range(3)]
        sm = [at(f"sm{g}", W_V + 1536 + 512 * g, 512) for g in range(3)]
        y_feat = at("y_feat", W_A, KT_N * N)
        y_tok = at("y_tok", W_PROJ, 5 * D)[:, :].rearrange("p (t d) -> p t d", d=D)

        neg0 = stat0[:, 0:4].rearrange("p (u m) -> p u m", u=2)
        sum0 = stat0[:, 4:8].rearrange("p (u m) -> p u m", u=2)
        rs0 = stat0[:, 8:12].rearrange("p (u m) -> p u m", u=2)
        S_NEG, S_TMP, S_ALPHA, S_SUM, S_RUN, S_REC, S_COMB = 0, 5, 6, 12, 18, 26, 34
        neg1 = stat1[:, 320:416].rearrange("p (g c h) -> p g c h", g=3, c=4)
        sum1 = stat1[:, 416:512].rearrange("p (g c h) -> p g c h", g=3, c=4)
        negp = stat1[:, 512:544].rearrange("p (c h) -> p c h", c=4)
        sump = stat1[:, 544:576].rearrange("p (c h) -> p c h", c=4)
        samp = [at("samp0", W_STAT, 512), at("samp1", W_STAT, 512)]

        s_const, s_x, s_gain, s_lam, s_hist, s_page = (sem(n) for n in
            ("const_loaded", "x_loaded", "gains_loaded", "lam_loaded", "hist_loaded", "pages_loaded"))
        raw_loaded = [sem(f"raw_loaded{i}") for i in range(2)]
        whi_ready, wlo_ready = sem("whi_ready"), sem("wlo_ready")
        tile_done, acc_free = sem("tile_done"), sem("acc_free")
        ahi_ready, a_ready = sem("ahi_ready"), sem("a_ready")
        bhi_ready, b_ready = sem("bhi_ready"), sem("b_ready")
        xsq_ready, sqs_done = sem("xsq_ready"), sem("sqs_done")
        ms_ready, v_ready, sqrt_ready = sem("ms_ready"), sem("v_ready"), sem("sqrt_ready")
        gain_ps, gain_ready, xt_ps, x_ready = sem("gain_ps"), sem("gain_ready"), sem("xt_ps"), sem("x_ready")
        sq_up = sem("sq_up")
        dve_step, pool_step = sem("dve_step"), sem("pool_step")
        lam_e, lam_d = sem("lam_e"), sem("lam_d")
        outs = [sem(f"outs{i}") for i in range(4)]
        tk_ps, tv_ps, tk_done, tv_done = (sem(n) for n in ("tk_ps", "tv_ps", "tk_done", "tv_done"))
        kout = [sem(f"kout{i}") for i in range(2)]
        vout = sem("vout")
        q_scaled, qs_saved = sem("q_scaled"), sem("qs_saved")
        hist_ps, hist_done, rows_ps, rows_done, rows_out = (sem(n) for n in
            ("hist_ps", "hist_done", "rows_ps", "rows_done", "rows_out"))
        pm_ready, mix_ps = sem("pm_ready"), sem("mix_ps")
        p0_s, p0_m, p0_e, p0_a, p0_t, p0_at, p0_pv, p0_o = (sem(f"p0_{n}") for n in
            ("s", "m", "e", "a", "t", "at", "pv", "o"))
        p1_s, p1_m, p1_e, p1_t, p1_pt, p1_pv, p1_o = (sem(f"p1_{n}") for n in
            ("s", "m", "e", "t", "pt", "pv", "o"))
        sub_sq, sub_ms, sub_v, sub_r, sub_t = (sem(f"sub_{n}") for n in ("sq", "ms", "v", "r", "t"))
        SS = []
        for L in range(2):
            SS.append({n: sem(f"sa{L}_{n}") for n in
                       ("k0", "k1", "v0", "v1", "q", "kt_ps", "kt_a", "kt_d", "s", "neg", "e", "pt_ps", "pt",
                        "o_ps", "o", "fin", "fin_ps", "fin_d")})
        cb_t, cb_d, cb_x, cb_e, cb_c, cb_ps, cb_u = (sem(f"cb_{n}") for n in ("t", "d", "x", "e", "c", "ps", "u"))
        y_ready, yt_ps, yt_done = sem("y_ready"), sem("yt_ps"), sem("yt_done")
        q_zero = sem("q_zero")

        def tok_cols(v, g, c):
            if g == 0:
                return v[:, 128 * c:128 * c + 128]
            if g == 1:
                return v.rearrange("p (l r) -> p r l", r=4)[:, c, :]
            return v.rearrange("p (l c r) -> p c r l", c=4, r=4)[:, c, :, :]

        def proj_cols(v, g, c):
            return tok_cols(v, g if g < 2 else 0, c)

        units1, items1 = [[], [], []], []
        for g in range(3):
            for c in range(4):
                for quad in range(2):
                    parts = [(c, ("causal", "causal", "g2m")[g])] + ([(c - 1, "prev")] if g == 0 and c else [])
                    u = []
                    for kc, mask in parts:
                        u.append(len(items1))
                        items1.append((g, c, quad, kc, mask))
                    units1[g].append((c, quad, u))
        UNIT_OF = {it: 8 * g + s for g in range(3) for s, u in enumerate(units1[g]) for it in u[2]}
        BLK = [dict(pages=(4, 4, 4, 4), groups=(0, 0, 0, 0), new=1, mask=(None,) * 4),
               dict(pages=(4, 4, 4, 1), groups=(2, 2, 1, 0), new=3, mask=("rm2a", "rm2b", "rm1", "g0m"))]
        for b_ in BLK:
            b_["pn"] = sum(b_["pages"])
            b_["pa"] = sum((n + 1) // 2 for n in b_["pages"])
            b_["pd"] = b_["pn"] - b_["pa"]

        stored = [not (T == 1 and c < 3) for T in range(4) for c in range(5)]
        V_STORES = [sum(stored[0:5 * T + 5]) for T in range(4)]
        K_BEFORE = [sum(stored[j] for j in range(n % 2, n, 2)) for n in range(22)]
        K_STORES = (K_BEFORE[20], K_BEFORE[21])

        block = ctx.enter_context(nc.Block())

        @block.sync
        def _(sp):
            sp.dma_start(con[:, :], a["consts"]).then_inc(s_const, 16)
            sp.dma_start(x_tok[:, 0:4, :], a["x_prompt"][0].rearrange("(t p) d -> p t d", p=P)).then_inc(s_x, 16)
            sp.dma_start(x_tok[0:NS, 4, :], a["x_sample"].rearrange("b t d -> (b t) d")).then_inc(s_x, 16)

            def unit(w, col, n, slot, wait=True):
                if wait:
                    sp.wait_ge(wlo_ready, 2 * n - 2)
                sp.dma_start(raw_v[slot].rearrange("p k j n -> p k (j n)"),
                             w.rearrange("(k p) n -> p k n", p=P)[:, :, ds(col, 256)]).then_inc(raw_loaded[slot], 16)

            def matrix(w, t0, n_tiles, first=0):
                if n_tiles // 4 - first == 1:
                    for s in range(2):
                        unit(w, 512 * first + 256 * s, t0 // 2 + 2 * first + s, s)
                    return
                with sp.Fori(first, n_tiles // 4) as i:
                    for s in range(2):
                        unit(w, i * 512 + 256 * s, i * 2 + t0 // 2 + s, s)

            def mlp_weights(L, t0):
                up, down = a["w_up"][L], a["w_down"][L].rearrange("(c k) n -> c k n", c=4)
                with sp.Fori(0, 4) as c:
                    with sp.Fori(0, 2) as i:
                        for s in range(2):
                            unit(up, c * 1024 + i * 512 + 256 * s, c * 8 + i * 2 + t0 // 2 + s, s)
                    with sp.Fori(0, 2) as i:
                        for s in range(2):
                            sp.wait_ge(wlo_ready, (c * 8 + i * 2 + (t0 // 2 + 4 + s)) * 2 - 2)
                            sp.dma_start(raw_v[s].rearrange("p k j n -> p k (j n)"),
                                         down[ds(c, 1), :, ds(i * 512 + 256 * s, 256)]
                                         .rearrange("o (k p) n -> p (o k) n", p=P)).then_inc(raw_loaded[s], 16)

            def cache_blocks(L):
                B, S = BLK[L], SS[L]

                def load(b, i, first):
                    slot, np_ = i % 2, B["pages"][i]
                    if i >= 2:
                        k_val, v_val = b * B["pn"] + 4 * (i - 2) + B["pages"][i - 2], b * 5 + (i - 2) + 1
                    else:
                        k_val = b * B["pn"] + (4 * (i + 2) + B["pages"][i + 2] - B["pn"])
                        v_val = b * 5 + (i + 2 + 1 - 5)
                    if L == 0:
                        page = [sp.value_load(pages[0:1, ds(b * 16 + (4 * i + p), 1)], min_val=0,
                                              max_val=a["cache_b_kv"].shape[1] - 1) for p in range(4)]
                    for kv, ring in ((0, kring_v), (1, vring_v)):
                        if kv == 0 and (i >= 2 or not first):
                            sp.wait_ge(S["kt_ps"], k_val)
                        if kv == 1 and (i >= 2 or not first):
                            sp.wait_ge(S["o_ps"], v_val)
                        done = S[("k", "v")[kv] + str(slot)]
                        if L == 0:
                            for p in range(4):
                                sp.dma_start(ring[slot][:, p, :],
                                             a["cache_b_kv"][0][ds(page[p], 1)].rearrange("o t v h e -> (o t) v (h e)")
                                             [:, kv, :]).then_inc(done, 16)
                        else:
                            g = B["groups"][i]
                            src = a[f"cache_d{g}_kv"][0][ds(b, 1)].rearrange(
                                "o (i s) v h e -> (o i) s v (h e)", s=DIL[g])
                            first_s = 4 * i if g == 2 else 0
                            sp.dma_start(ring[slot][:, 0:np_, :],
                                         src[:, first_s:first_s + np_, kv, :]).then_inc(done, 16)

                for i in range(4):
                    load(0, i, True)
                with sp.Fori(1, NB) as b:
                    for i in range(4):
                        load(b, i, False)

            def store_tokens(T, out_p, out_s, g):
                for c in range(5):
                    n = 5 * T + c
                    for kv, done in ((0, tk_done), (1, tv_done)):
                        if not stored[n]:
                            continue
                        sp.wait_ge(done, n + 1)
                        if c < 4:
                            src = k_tok[n % 2][:, :] if kv == 0 else v_all[:, c, :]
                            v = out_p[0, 0].rearrange("t v h e -> t v (h e)")[:, kv, :]
                            if T == 0:
                                dst = v[P * c:P * c + P, :]
                            elif g == 0:
                                dst = v
                            elif g == 1:
                                dst = v.rearrange("(l r) f -> r l f", r=4)[c]
                            else:
                                dst = v.rearrange("(l c r) f -> c r l f", c=4, r=4)[c]
                        else:
                            src = k_tok[n % 2][0:NS, :] if kv == 0 else v_s[0:NS, g, :]
                            v = out_s[0].rearrange("b t v h e -> b t v (h e)")
                            dst = v[:, v.shape[1] - TS:, kv, :]
                        sp.dma_start(dst, src).then_inc(kout[n % 2] if kv == 0 else vout, 16)

            w_ab, w_oa = a["w_in_ab"][0], a["w_out_ab"][0]
            unit(w_ab, 0, 0, 0, wait=False)
            unit(w_ab, 256, 1, 1, wait=False)
            for m, n in enumerate(("norm_mix_g", "norm_mlp_g")):
                sp.dma_start(gain_rows[16 * m:16 * m + 16, :],
                             a[n].rearrange("l (k p) -> (l k) p", p=P)).then_inc(s_gain, 16)
            sp.dma_start(gain_rows[32:40, :], a["norm_out_g"].rearrange("(k p) -> k p", p=P)).then_inc(s_gain, 16)
            sp.dma_start(gain_rows[40:44, :], a["a_scale"][0].rearrange("(k p) -> k p", p=P)).then_inc(s_gain, 16)
            sp.dma_start(gain_rows[44:56, :], a["c_conv_w"][0].rearrange("j (k p) -> (j k) p", p=P)).then_inc(s_gain, 16)
            sp.dma_start(gain_rows[56:57, :], a["b_subln_g"]).then_inc(s_gain, 16)
            sp.dma_start(lam_in[:, :], a["b_lam"][0].rearrange("a d -> (a d)").partition_broadcast(P)).then_inc(s_lam, 16)
            sp.dma_start(hist_tok[0:120, :], a["state_a_pool"][0].rearrange("b t c -> (b t) c")).then_inc(s_hist, 16)
            sp.dma_start(a_mix[:, :].rearrange("p (g d) -> p g d", g=4),
                         a["a_mix"][0].rearrange("g c d -> c g d")).then_inc(s_hist, 16)
            sp.dma_start(pages[0:1, :], a["page_table"].rearrange("(o b) n -> o (b n)", o=1)).then_inc(s_page, 16)
            matrix(w_ab, T_AB, 16, first=1)
            unit(w_oa, 0, T_OA // 2, 0)
            unit(w_oa, 256, T_OA // 2 + 1, 1)
            sp.wait_ge(rows_done, 1)
            sp.dma_start(a["new_pool_prompt"][0, 0], e2[0][49:64, :]).then_inc(rows_out, 16)
            sp.dma_start(a["new_pool_sample"][0][:, 7:15, :], e2[0][NS:P, :]).then_inc(rows_out, 16)
            store_tokens(0, a["new_bkv_prompt"], a["new_bkv_sample"], 0)
            sp.wait_ge(s_page, 16)
            sp.wait_ge(tile_done, T_AB + 16)
            cache_blocks(0)
            unit(w_oa, 512, T_OA // 2 + 2, 0)
            unit(w_oa, 768, T_OA // 2 + 3, 1)
            mlp_weights(0, T_M0)
            w_cd, w_oc = a["w_in_cd"][0], a["w_out_cd"][0]
            unit(w_cd, 0, T_CD // 2, 0)
            unit(w_cd, 256, T_CD // 2 + 1, 1)
            sp.wait_ge(b_ready, 8 + 32)
            sp.dma_start(conv_tok[0:16, :], a["state_c_conv"][0].rearrange("b t c -> (b t) c")).then_inc(s_hist, 16)
            for g, (first, end) in enumerate(((1, 7), (7, 10), (10, 12))):
                with sp.Fori(first, end) as i:
                    for s in range(2):
                        unit(w_cd, i * 512 + 256 * s, i * 2 + T_CD // 2 + s, s)
                if g == 0:
                    sp.wait_ge(rows_done, 2)
                    sp.dma_start(a["new_conv_prompt"][0, 0], e2[0][NS - 2:NS, :]).then_inc(rows_out, 16)
                    for j in range(2):
                        sp.dma_start(a["new_conv_sample"][0][:, j, :], e2[0][NS + 6 + j:P:8, :]).then_inc(rows_out, 16)
                if g == 2:
                    unit(w_oc, 0, T_OC // 2, 0)
                    unit(w_oc, 256, T_OC // 2 + 1, 1)
                store_tokens(1 + g, a[f"new_d{g}_prompt"], a[f"new_d{g}_sample"], g)
            sp.wait_ge(tile_done, T_CD + 48)
            cache_blocks(1)
            unit(w_oc, 512, T_OC // 2 + 2, 0)
            unit(w_oc, 768, T_OC // 2 + 3, 1)
            mlp_weights(1, T_M1)

            for t in range(5):
                sp.wait_ge(yt_done, t + 1)
                if t < 4:
                    sp.dma_start(a["y_prompt"][0, P * t:P * t + P, :], y_tok[:, t, :]).then_inc(outs[2], 16)
                else:
                    sp.dma_start(a["y_sample"].rearrange("b t d -> (b t) d"), y_tok[0:NS, t, :]).then_inc(outs[2], 16)
            sp.wait_ge(outs[2], 80)
            sp.wait_ge(rows_out, 80)
            sp.wait_ge(vout, 16 * V_STORES[3])
            for i in range(2):
                sp.wait_ge(kout[i], 16 * K_STORES[i])

        @block.tensor
        def _(pe):
            def dense(group, n_groups, m_hi, m_lo, ready, ready_base, hook=None, peel=False):

                def four(G, first):
                    for q in range(4):
                        s = q % 2
                        pe.wait_ge(wlo_ready, G * 4 + (q + 1))
                        pe.wait_ge(acc_free, G * 4 + (q + 1))
                        for k in range(KT_N):
                            if first and q == 0:
                                pe.wait_ge(ready, ready_base + (k + 1))
                            for n, (w, m) in enumerate(((whi_v, m_hi), (whi_v, m_lo), (wlo_v, m_hi))):
                                for h in range(2):
                                    last = pe.matmul(acc_h[s][:, h, :], w[s][:, k, :], m[:, k, NH * h:NH * h + NH],
                                                     start=(k == 0 and n == 0), stop=(k == KT_N - 1 and n == 2))
                        last.then_inc(tile_done, 1)
                        if hook and first and q == 0:
                            hook()

                done = 0
                if peel or n_groups == 1:
                    four(group(0), True)
                    done = 1
                if n_groups - done == 1:
                    four(group(done), done == 0)
                elif n_groups > done:
                    with pe.Fori(done, n_groups) as i:
                        four(group(i), done == 0)

            def mean_square(f):
                def go():
                    pe.wait_ge(sqs_done, 8 * (f + 1))
                    for h in range(2):
                        last = pe.matmul(halves[2][:, h, :], ones, sqsum[:, NH * h:NH * h + NH], start=True, stop=True)
                    last.then_inc(ms_ready, 1)
                return go

            def mlp(L, t0):
                G0, fa, fb = t0 // 4, 8 * (1 + 2 * L), (8, 48)[L]
                dense(lambda i: i + G0, 2, ahk, alk, a_ready, fa, hook=mean_square(1 + 2 * L), peel=True)
                dense(lambda i: i + (G0 + 2), 2, bhk, blk, b_ready, fb)
                with pe.Fori(1, 4) as c:
                    dense(lambda i: c * 4 + (i + G0), 2, ahk, alk, a_ready, fa)
                    dense(lambda i: c * 4 + (i + (G0 + 2)), 2, bhk, blk, b_ready, c * 8 + fb)

            def token_major(T, kb, g):
                for c in range(5):
                    for kv, (ps, done, bk) in enumerate(((tk_ps, tk_done, bank[6]), (tv_ps, tv_done, bank[7]))):
                        if T or c:
                            pe.wait_ge(done, 5 * T + c)
                        rows = P if c < 4 else NS
                        for i in range(4):
                            tile = kb + 4 * kv + i
                            src = proj_cols(pk[:, tile, 0:SEQ], g, c) if c < 4 else pk[:, tile, SEQ:N]
                            last = pe.transpose(bk[0:rows, P * i:P * i + P], src, ident)
                        last.then_inc(ps, 1)

            def rows_of(tile0):
                for i in range(4):
                    last = pe.transpose(bank[7][:, P * i:P * i + P], pk[:, tile0 + i, N - P:N], ident)
                last.then_inc(rows_ps, 1)

            def sample_attention(L, pt):
                B, S = BLK[L], SS[L]
                kt = (kt_l0, kt_l1)[L][:, :].rearrange("p (i g n) -> p i g n", i=4, g=4)
                with pe.Fori(0, NB) as b:
                    for i in range(6):
                        if i < 4:
                            pe.wait_ge(S[f"k{i % 2}"], (b * 2 + (i // 2 + 1)) * (64 if L == 0 else 16))
                            for p in range(B["pages"][i]):
                                if p % 2 == 0:
                                    pe.wait_ge(S["kt_a"], b * B["pa"] + (2 * i + p // 2))
                                else:
                                    pe.wait_ge(S["kt_d"], b * B["pd"] + (2 * i + p // 2))
                                for t in range(4):
                                    last = pe.transpose(bank[p % 2][:, P * t:P * t + P],
                                                        kring_v[i % 2][:, p, P * t:P * t + P], ident)
                                last.then_inc(S["kt_ps"], 1)
                        if i >= 1:
                            j = i - 1
                            pe.wait_ge(S["e"], b * 5 + (j + 1))
                            pe.wait_ge(S["pt"], b * 5 + (j - 1 if j >= 2 else 0))
                            n = B["pages"][j] if j < 4 else B["new"]
                            w = P if j < 4 else NS
                            for p in range(n):
                                last = pe.transpose(bank[4 + j % 2][:, P * p:P * p + P],
                                                    e2[j % 2][:, w * p:w * p + P], ident)
                            last.then_inc(S["pt_ps"], 1)
                        if i < 5:
                            pe.wait_ge(S["e"], b * 5 + (i - 1 if i >= 2 else 0))
                            if i == 0:
                                pe.wait_ge(S["q"], b * 2 + 2)
                            sb = bank[2 + i % 2]
                            if i < 4:
                                np_, g = B["pages"][i], B["groups"][i]
                                pe.wait_ge(S["kt_a"], b * B["pa"] + (2 * i + (np_ + 1) // 2))
                                pe.wait_ge(S["kt_d"], b * B["pd"] + (2 * i + np_ // 2))
                                for t in range(4):
                                    last = pe.matmul(sb[32 * t:32 * t + 32, 0:P * np_], q_st[:, g, t, :],
                                                     kt[:, t, 0:np_, :], start=True, stop=True)
                            else:
                                for g in range(B["new"]):
                                    for t in range(4):
                                        last = pe.matmul(sb[32 * t:32 * t + 32, NS * g:NS * g + NS],
                                                         q_st[:, g, t, :], k_s[:, g, t, :], start=True, stop=True)
                            last.then_inc(S["s"], 1)
                        if i >= 1:
                            j = i - 1
                            if j == 4:
                                pe.wait_ge(tv_done, (5, 20)[L])
                            pe.wait_ge(S["pt"], b * 5 + (j + 1))
                            pe.wait_ge(S["o"], b * 5 + (j - 1 if j >= 2 else 0))
                            ob = bank[6 + j % 2]
                            if j < 4:
                                pe.wait_ge(S[f"v{j % 2}"], (b * 2 + (j // 2 + 1)) * (64 if L == 0 else 16))
                            n, w = (B["pages"][j], P) if j < 4 else (B["new"], NS)
                            for p in range(n):
                                v = vring_v[j % 2][:, p, :] if j < 4 else v_s[0:NS, p, :]
                                for t in range(4):
                                    last = pe.matmul(ob[32 * t:32 * t + 32, 0:P],
                                                     pt[j % 2][0:w, P * p + 32 * t:P * p + 32 * t + 32],
                                                     v[:, P * t:P * t + P], start=(p == 0), stop=(p == n - 1))
                            last.then_inc(S["o_ps"], 1)

            def sample_finish(L, orun, stat):
                S = SS[L]
                comb = stat[:, S_COMB:S_COMB + 256].rearrange("p (b c) -> p b c", b=NB)
                pe.wait_ge(S["fin"], 1)
                for b in range(NB):
                    last = pe.matmul(bank[0][:, 32 * b:32 * b + 32], orun[:, P * b:P * b + P], comb[:, b, :],
                                     start=True, stop=True)
                last.then_inc(S["fin_ps"], 1)

            pe.wait_ge(s_const, 16)
            pe.wait_ge(s_gain, 96)
            pe.transpose(bank[7][:, 0:57], gain_rows[0:57, :], ident[0:57, 0:57]).then_inc(gain_ps, 1)
            pe.wait_ge(s_x, 32)
            for k in range(KT_N):
                if k >= 2:
                    pe.wait_ge(x_ready, k - 1)
                for t in range(5):
                    rows = P if t < 4 else NS
                    last = pe.transpose(acc[k % 2][:, P * t:P * t + rows], x_tok[0:rows, t, P * k:P * k + P],
                                        ident[0:rows, 0:rows])
                last.then_inc(xt_ps, 1)

            pe.wait_ge(x_ready, 8)
            dense(lambda i: i, 4, ahk, alk, a_ready, 0, hook=mean_square(0), peel=True)
            pe.wait_ge(acc_free, 2 + T_AB + 16)
            pe.wait_ge(s_hist, 32)
            for i in range(4):
                last = pe.transpose(bank[6][:, P * i:P * i + 120], hist_tok[0:120, P * i:P * i + P],
                                    ident[0:120, 0:120])
            last.then_inc(hist_ps, 1)
            rows_of(0)
            pe.wait_ge(hist_done, 1)
            pe.wait_ge(rows_done, 1)
            token_major(0, 8, 0)

            pe.wait_ge(q_scaled, 1)
            for s in range(16 + 2):
                if s < 16:
                    h, qt = s // 4, s % 4
                    if s >= 2:
                        pe.wait_ge(p0_e, s - 1)
                    for m in range(2):
                        last = pe.matmul(bank[2 * (s % 2) + m][:, 0:P * (qt + 1)],
                                         pk[64 * m:64 * m + 64, 4 + h, P * qt:P * qt + P],
                                         pk[64 * m:64 * m + 64, 8 + h, 0:P * (qt + 1)], start=True, stop=True)
                    last.then_inc(p0_s, 1)
                if s >= 2:
                    n = s - 2
                    h, qt = n // 4, n % 4
                    pe.wait_ge(p0_at, n + 1)
                    if n == 0:
                        pe.wait_ge(tk_done, 5)
                        pe.wait_ge(tv_done, 5)
                    if n >= 2:
                        pe.wait_ge(p0_o, n - 1)
                    for kb in range(qt + 1):
                        last = pe.matmul(bank[6 + n % 2][:, 0:P], v_all[:, kb, P * h:P * h + P],
                                         pt_l0[n % 2][:, P * kb:P * kb + P], start=(kb == 0), stop=(kb == qt))
                    last.then_inc(p0_pv, 1)
                if 1 <= s <= 16:
                    n = s - 1
                    qt = n % 4
                    pe.wait_ge(p0_a, n + 1)
                    if n >= 2:
                        pe.wait_ge(p0_at, n - 1)
                    for kb in range(qt + 1):
                        last = pe.transpose(bank[4 + n % 2][:, P * kb:P * kb + P],
                                            e4[n % 2][0][:, P * kb:P * kb + P], ident)
                    last.then_inc(p0_t, 1)

            for g in range(4):
                pe.wait_ge(pm_ready, g + 1)
                pe.wait_ge(p0_e, 16)
                if g >= 2:
                    pe.wait_ge(b_ready, g - 1)
                for h in range(2):
                    last = pe.matmul(acc_h[g % 2][:, h, :], a_mix[:, P * g:P * g + P],
                                     pk[:, g, NH * h:NH * h + NH], start=True, stop=True)
                last.then_inc(mix_ps, 1)
            pe.wait_ge(b_ready, 4)
            pe.wait_ge(p0_o, 16)

            sample_attention(0, pt_l0)
            sample_finish(0, orun0, samp[0])

            for h in range(4):
                pe.wait_ge(sub_sq, h + 1)
                if h >= 2:
                    pe.wait_ge(sub_v, h - 1)
                for f in range(2):
                    last = pe.matmul(halves[1 + h % 2][:, f, :], ones, zbuf[:, N * (h % 2) + NH * f:N * (h % 2) + NH * f + NH],
                                     start=True, stop=True)
                last.then_inc(sub_ms, 1)
            pe.wait_ge(sub_v, 4)
            pe.wait_ge(SS[0]["fin_d"], 1)
            dense(lambda i: i + T_OA // 4, 2, bhk, blk, b_ready, 0)
            mlp(0, T_M0)

            dense(lambda i: i + T_CD // 4, 3, ahk, alk, a_ready, 16, hook=mean_square(2), peel=True)
            pe.wait_ge(acc_free, 2 + T_CD + 12)
            pe.wait_ge(s_hist, 48)
            for i in range(4):
                last = pe.transpose(bank[6][:, 16 * i:16 * i + 16], conv_tok[0:16, P * i:P * i + P], ident[0:16, 0:16])
            last.then_inc(hist_ps, 1)
            pe.wait_ge(pm_ready, 5)
            rows_of(4)
            for g in range(3):
                dense(lambda i: i + (T_CD // 4 + 3 + 3 * g), 3, ahk, alk, a_ready, 16)
                pe.wait_ge(acc_free, 2 + T_CD + 12 * (g + 2))
                if g == 0:
                    pe.wait_ge(hist_done, 2)
                    pe.wait_ge(rows_done, 2)
                else:
                    pe.wait_ge(p1_o, 4 * g)
                token_major(1 + g, 4, g)
                pe.wait_ge(q_scaled, 2 + g)
                for s in range(8 + 2):
                    if s < 8:
                        c, quad, its = units1[g][s]
                        for it in its:
                            if it >= 4:
                                pe.wait_ge(p1_e, it - 3)
                            kc = items1[it][3]
                            for hh in range(4):
                                t, r = hh, 64 * quad
                                last = pe.matmul(bank[it % 4][:, P * hh:P * hh + P],
                                                 proj_cols(pk[r:r + 64, t, 0:SEQ], g, c),
                                                 proj_cols(pk[r:r + 64, 4 + t, 0:SEQ], g, kc), start=True, stop=True)
                            last.then_inc(p1_s, 1)
                    if s >= 2:
                        u = 8 * g + s - 2
                        c, quad, its = units1[g][s - 2]
                        pe.wait_ge(p1_pt, its[-1] + 1)
                        if s == 2:
                            pe.wait_ge(tk_done, 5 * (2 + g))
                            pe.wait_ge(tv_done, 5 * (2 + g))
                        if u >= 4 and quad == 0:
                            pe.wait_ge(p1_o, u // 2 - 1)
                        for hh in range(4):
                            head, r = 2 * hh + quad, 64 * quad
                            for n, it in enumerate(its):
                                last = pe.matmul(bank[6 + u // 2 % 2][r:r + 64, P * hh:P * hh + P],
                                                 v_all[:, items1[it][3], 64 * head:64 * head + 64],
                                                 pt_l1[it % 2][:, P * hh:P * hh + P],
                                                 start=(n == 0), stop=(n == len(its) - 1))
                        last.then_inc(p1_pv, 1)
                    if 1 <= s <= 8:
                        for it in units1[g][s - 1][2]:
                            pe.wait_ge(p1_e, it + 1)
                            if it >= 2:
                                pe.wait_ge(p1_pt, it - 1)
                            for hh in range(4):
                                last = pe.transpose(bank[4 + it % 2][:, P * hh:P * hh + P],
                                                    e2[it % 2][:, P * hh:P * hh + P], ident)
                            last.then_inc(p1_t, 1)

            pe.wait_ge(p1_o, 12)
            pe.wait_ge(cb_t, 1)
            for n, src in enumerate((neg1, sum1)):
                for g in range(3):
                    for c in range(4):
                        last = pe.transpose(bank[3 * n + g][0:8, P * c:P * c + P], src[:, g, c, :], ident)
            last.then_inc(cb_d, 1)
            pe.wait_ge(cb_c, 1)
            for t in range(4):
                for g in range(3):
                    n = 3 * t + g
                    if n >= 6:
                        pe.wait_ge(cb_u, n // 3 - 1)
                    last = pe.matmul(bank[n % 6][:, :], cc("sel8")[0:8, P * t:P * t + P], nm[g][0:8, :],
                                     start=True, stop=True)
                last.then_inc(cb_ps, 1)
            pe.wait_ge(cb_u, 4)

            sample_attention(1, pt_l1)
            sample_finish(1, orun1, samp[1])
            pe.wait_ge(SS[1]["fin_d"], 1)
            dense(lambda i: i + T_OC // 4, 2, bhk, blk, b_ready, 40)
            mlp(1, T_M1)

            mean_square(4)()
            for t in range(5):
                rows = P if t < 4 else NS
                pe.wait_ge(y_ready, 8)
                if t >= 2:
                    pe.wait_ge(yt_done, t - 1)
                for k in range(KT_N):
                    last = pe.transpose(acc[t % 2][0:rows, P * k:P * k + P], y_feat[:, N * k + P * t:N * k + P * t + rows],
                                        ident)
                last.then_inc(yt_ps, 1)

        @block.vector
        def _(dve):
            steps = Tally()

            def link(ins):
                ins.then_inc(dve_step, 1)
                dve.wait_ge(dve_step, steps.add())

            def split_lo(G, q):
                j = q % 2
                dve.wait_ge(whi_ready, G * 4 + (q + 1))
                dve.tensor_tensor(wlo_v[j], raw_v[q // 2][:, :, j, :], whi_v[j].bitcast(F32),
                                  ALU.subtract).then_inc(wlo_ready, 1)

            def dense(group, n_groups, evac, post=None, peel=False, hook=None, static=False, last=False):
                def four(G, i):
                    for q in range(4):
                        dve.wait_ge(tile_done, G * 4 + (q + 1))
                        if hook and q == 0 and isinstance(i, int) and i == 0:
                            hook()
                        evac(G, i, q)
                        if not (last and q >= 2 and i == n_groups - 1):
                            split_lo(*((G, q + 2) if q < 2 else (G + 1, q - 2)))
                        if post:
                            post(G, i, q)
                done = 0
                while done < n_groups and (static or n_groups - done == 1 or (peel and done == 0)):
                    four(group(done), done)
                    done += 1
                if done < n_groups:
                    with dve.Fori(done, n_groups) as i:
                        four(group(i), i)

            def rms(f):
                def go():
                    dve.wait_ge(ms_ready, f + 1)
                    dve.tensor_scalar(r_h, halves[2], 1.0 / D, EPS, ALU.mult, ALU.add).then_inc(v_ready, 1)
                    dve.wait_ge(sqrt_ready, f + 1)
                    link(dve.reciprocal(rnorm[:, :], rnorm[:, :]))
                return go

            def to_proj(tile0=0):
                def evac(G, i, q):
                    dst = proj[:, ds(i * (4 * N) + (tile0 + q) * N, N)].rearrange("p (h c) -> p h c", h=2)
                    dve.tensor_tensor(dst, acc_h[q % 2], r_h, ALU.mult).then_inc(acc_free, 1)
                return evac

            def to_proj_streams():
                L0 = NH // 16

                def evac(G, i, q):
                    dst = proj[:, ds(i * (4 * N) + q * N, N)]
                    dp = dst[:, 0:SEQ].rearrange("p (r l) -> p r l", r=16)
                    rl = lambda v: v.rearrange("p (l r) -> p r l", r=16)
                    a0, a1 = acc_h[q % 2][:, 0, :], acc_h[q % 2][:, 1, :]
                    dve.tensor_tensor(dp[:, :, 0:L0], rl(a0), rl(rnorm[:, 0:NH]), ALU.mult)
                    dve.tensor_tensor(dp[:, :, L0:32], rl(a1[:, 0:SEQ - NH]), rl(rnorm[:, NH:SEQ]), ALU.mult)
                    dve.tensor_tensor(dst[:, SEQ:N], a1[:, SEQ - NH:NH], rnorm[:, SEQ:N], ALU.mult).then_inc(acc_free, 1)
                return evac

            def up(G, i, q):
                j = q % 2
                z = zbuf[:, N * j:N * j + N]
                dve.tensor_tensor(z.rearrange("p (h c) -> p h c", h=2), acc_h[j], r_h, ALU.mult).then_inc(acc_free, 1)
                dve.wait_ge(acc_free, G * 4 + (q + 3))
                dve.scalar_tensor_tensor(out=sqbuf[:, N * j:N * j + N], in0=z, scalar=0.0, in1=z, op0=ALU.max,
                                         op1=ALU.mult).then_inc(sq_up, 1)

            def up_post(b0):
                def post(G, i, q):
                    dve.wait_ge(bhi_ready, b0 + i * 4 + (q + 1))
                    at_ = ds(i * (4 * N) + q * N, N)
                    dve.tensor_tensor(b_lo[:, at_], sqbuf[:, N * (q % 2):N * (q % 2) + N], b_hi[:, at_].bitcast(F32),
                                      ALU.subtract).then_inc(b_ready, 1)
                return post

            def down(G, i, q):
                xt = x[:, ds(i * (4 * N) + q * N, N)].rearrange("p (h c) -> p h c", h=2)
                dve.tensor_tensor(xt, xt, acc_h[q % 2], ALU.add).then_inc(acc_free, 1)

            def fin_post(f, gcol):
                def post(G, i, q):
                    k = 4 * i + q
                    dve.wait_ge(ahi_ready, 8 * f + k + 1)
                    dve.scalar_tensor_tensor(out=alk[:, k, :], in0=xk[:, k, :], scalar=gains[:, gcol + k:gcol + k + 1],
                                             in1=ahk[:, k, :].bitcast(F32), op0=ALU.mult,
                                             op1=ALU.subtract).then_inc(a_ready, 1)
                return post

            def mlp(L, t0):
                G0, fb = t0 // 4, (8, 48)[L]
                dense(lambda i: i + G0, 2, up, up_post(fb), peel=True, hook=rms(1 + 2 * L))
                dense(lambda i: i + (G0 + 2), 2, down)
                with dve.Fori(1, 3) as c:
                    dense(lambda i: c * 4 + (i + G0), 2, up, up_post(c * 8 + fb))
                    dense(lambda i: c * 4 + (i + (G0 + 2)), 2, down)
                dense(lambda i: i + (G0 + 12), 2, up, up_post(24 + fb))
                if L == 0:
                    dense(lambda i: i + (G0 + 14), 2, down, fin_post(2, G_MIX + 8), static=True)
                else:
                    dense(lambda i: i + (G0 + 14), 2, down, static=True, last=True)

            def token_major(T, g):
                for c in range(5):
                    dve.wait_ge(tv_ps, 5 * T + c + 1)
                    if c == 0 and T:
                        dve.wait_ge(vout, 16 * V_STORES[T - 1])
                    dst, rows = (v_all[:, c, :], P) if c < 4 else (v_s[0:NS, g, :], NS)
                    dve.tensor_copy(dst, bank[7][0:rows, :]).then_inc(tv_done, 1)

            def sample_attention(L, orun, stat):
                B, S = BLK[L], SS[L]
                kt = (kt_l0, kt_l1)[L][:, :].rearrange("p (i g n) -> p i g n", i=4, g=4)
                neg = lambda i: stat[:, S_NEG + i:S_NEG + i + 1]
                tmp = stat[:, S_TMP:S_TMP + 1]
                ob, run = stat[:, 300:428], stat[:, 510:511]
                n_links = (10, 15)[L]
                with dve.Fori(0, NB) as b, steps.loop(b, n_links, 0, NB):
                    for i in range(6):
                        if i < 4:
                            for p in range(1, B["pages"][i], 2):
                                dve.wait_ge(S["kt_ps"], b * B["pn"] + (4 * i + p + 1))
                                dve.wait_ge(S["s"], b * 5 + i)
                                dve.tensor_copy(kt[:, :, p, :], bank[1].rearrange("p (i n) -> p i n", i=4)
                                                ).then_inc(S["kt_d"], 1)
                        if i < 5:
                            dve.wait_ge(S["s"], b * 5 + (i + 1))
                            sb = bank[2 + i % 2]
                            w = P * B["pages"][i] if i < 4 else NS * B["new"]
                            if i < 4 and B["mask"][i]:
                                m, np_ = B["mask"][i], B["pages"][i]
                                sv = sb[:, 0:w].rearrange("p (g n) -> p g n", n=P)
                                if m == "g0m":
                                    link(dve.tensor_tensor(sb[:, 0:8], sb[:, 0:8], cc("g0m"), ALU.add))
                                else:
                                    rm = {"rm2a": cc("rm2")[:, 0:4], "rm2b": cc("rm2")[:, 4:8], "rm1": cc("rm1")}[m]
                                    link(dve.tensor_tensor(sv, sv, rm.unsqueeze(2).broadcast_to([P, 4, P]), ALU.add))
                                    if m == "rm1":
                                        link(dve.tensor_tensor(sv[:, :, 0], sv[:, :, 0], cc("k01"), ALU.add))
                            if i == 4:
                                sv = sb[:, 0:w].rearrange("p (g n) -> p g n", n=NS)
                                mv = cc("selfm").rearrange("p (g n) -> p g n", g=3)
                                link(dve.tensor_tensor(sv, sv, mv[:, 0:B["new"], ds(b * (-8) + 56, NS)], ALU.add))
                            if i == 0:
                                dve.tensor_reduce(neg(0), sb[:, 0:w], AX.X, ALU.max, negate=True).then_inc(S["neg"], 1)
                            else:
                                link(dve.tensor_reduce(tmp, sb[:, 0:w], AX.X, ALU.max, negate=True))
                                dve.wait_ge(S["neg"], b * 5 + i)
                                dve.tensor_tensor(neg(i), tmp, neg(i - 1), ALU.min).then_inc(S["neg"], 1)
                        if i >= 1:
                            j = i - 1
                            al = stat[:, S_ALPHA + j:S_ALPHA + j + 1]
                            su = stat[:, S_SUM + j:S_SUM + j + 1]
                            dve.wait_ge(S["o_ps"], b * 5 + (j + 1))
                            pv = bank[6 + j % 2][:, 0:P]
                            rdst = run if j < 4 else stat[:, ds(b + S_RUN, 1)]
                            odst = ob if j < 4 else orun[:, ds(b * P, P)]
                            if j == 0:
                                link(dve.tensor_copy(run, su))
                                dve.tensor_copy(ob, pv).then_inc(S["o"], 1)
                            else:
                                ins = dve.scalar_tensor_tensor(out=rdst, in0=run, scalar=al, in1=su, op0=ALU.mult,
                                                               op1=ALU.add)
                                link(ins)
                                dve.wait_ge(S["o"], b * 5 + j)
                                dve.scalar_tensor_tensor(out=odst, in0=ob, scalar=al, in1=pv, op0=ALU.mult,
                                                         op1=ALU.add).then_inc(S["o"], 1)

            def sample_finish(L, orun, stat, o_feat):
                S = SS[L]
                rec = stat[:, S_REC:S_REC + 8]
                comb = stat[:, S_COMB:S_COMB + 256].rearrange("p (b c) -> p b c", b=NB)
                dve.wait_ge(S["o"], 5 * NB)
                link(dve.reciprocal(rec, stat[:, S_RUN:S_RUN + 8]))
                if L == 0:
                    link(dve.tensor_scalar(rec, rec, neglam[:, 1:2], None, ALU.mult))
                else:
                    ov = orun[:, :].rearrange("p (b e) -> p b e", b=NB)
                    for hf in range(2):
                        o2 = ov[:, :, 64 * hf:64 * hf + 64]
                        link(dve.tensor_scalar(o2, o2, cc("halfm")[:, hf:hf + 1], None, ALU.mult))
                dve.tensor_tensor(comb, cc("sel").unsqueeze(1).broadcast_to([P, NB, 32]),
                                  rec.unsqueeze(2).broadcast_to([P, NB, 32]), ALU.mult).then_inc(S["fin"], 1)
                dve.wait_ge(S["fin_ps"], 1)
                for t in range(4):
                    last = dve.tensor_copy(o_feat[:, t, SEQ:N].rearrange("p (b t) -> p b t", b=NB),
                                           bank[0][:, 0:256].rearrange("p (b i t) -> p b i t", b=NB, i=4)[:, :, t, :])
                last.then_inc(S["fin_d"], 1)

            dve.wait_ge(gain_ps, 1)
            dve.tensor_copy(gains[:, 0:57], bank[7][:, 0:57]).then_inc(gain_ready, 1)
            dve.wait_ge(s_const, 16)
            dve.tensor_scalar(dummy[:, :], cc("ones")[:, 0:1], 1.0, None, ALU.mult).then_inc(acc_free, 2)
            split_lo(0, 0)
            split_lo(0, 1)
            for k in range(KT_N + 1):
                if k < KT_N:
                    dve.wait_ge(xt_ps, k + 1)
                    dve.tensor_copy(xk[:, k, :], acc[k % 2][:, 0:N]).then_inc(x_ready, 1)
                if k >= 1:
                    fin_post(0, G_MIX)(0, 0, k - 1)

            dve.wait_ge(s_lam, 16)
            lv = lam_in[:, :].rearrange("p (m s d) -> p m s d", m=2, s=2)
            lt = lam_t[:, 0:128].rearrange("p (m d) -> p m d", m=2)
            link(dve.tensor_tensor(lt, lv[:, :, 0, :], lv[:, :, 1, :], ALU.mult))
            dve.tensor_reduce(lam_t[:, 128:130], lt, AX.X, ALU.add).then_inc(lam_d, 1)
            dve.wait_ge(lam_e, 1)
            link(dve.tensor_tensor(neglam[:, 0:1], lam_t[:, 131:132], lam_t[:, 130:131], ALU.subtract))
            link(dve.tensor_scalar(neglam[:, 0:1], neglam[:, 0:1], -LAM_INIT, None, ALU.add))
            link(dve.scalar_tensor_tensor(out=neglam[:, 1:2], in0=cc("m01")[:, 1:2], scalar=neglam[:, 0:1],
                                          in1=cc("m01")[:, 0:1], op0=ALU.mult, op1=ALU.add))

            dense(lambda i: i, 4, to_proj(), peel=True, hook=rms(0))
            dve.wait_ge(acc_free, 2 + T_AB + 16)
            dve.tensor_scalar(proj[:, 4 * N:8 * N], proj[:, 4 * N:8 * N], 0.125, None, ALU.mult).then_inc(q_scaled, 1)
            dve.wait_ge(hist_ps, 1)
            dve.tensor_copy(hist_f.rearrange("p g b c -> p g (b c)"),
                            bank[6].rearrange("p (g w) -> p g w", g=4)[:, :, 0:120]).then_inc(hist_done, 1)
            dve.wait_ge(rows_ps, 1)
            dve.tensor_copy(e2[0][:, :], bank[7]).then_inc(rows_done, 1)
            token_major(0, 0)

            dve.wait_ge(rows_out, 32)
            dve.wait_ge(q_scaled, 1)
            for s in range(16 + 2):
                if s < 16:
                    qt, u = s % 4, s % 2
                    nk = P * (qt + 1)
                    dve.wait_ge(p0_s, s + 1)
                    sv = pp[u][:, :].rearrange("p (m n) -> p m n", m=2)
                    diag = sv[:, :, P * qt:P * qt + P]
                    link(dve.tensor_tensor(diag, diag, cc("causal").unsqueeze(1).broadcast_to([P, 2, P]), ALU.add))
                    dve.tensor_reduce(neg0[:, u, :], sv[:, :, 0:nk], AX.X, ALU.max, negate=True).then_inc(p0_m, 1)
                if 1 <= s <= 16:
                    n, u = s - 1, (s - 1) % 2
                    nk = P * (n % 4 + 1)
                    dve.wait_ge(p0_e, n + 1)
                    link(dve.reciprocal(rs0[:, u, :], sum0[:, u, :]))
                    link(dve.tensor_scalar(rs0[:, u, 1:2], rs0[:, u, 1:2], neglam[:, 0:1], None, ALU.mult))
                    e0, e1 = e4[u][0][:, 0:nk], e4[u][1][:, 0:nk]
                    link(dve.tensor_scalar(e0, e0, rs0[:, u, 0:1], None, ALU.mult))
                    dve.scalar_tensor_tensor(out=e0, in0=e1, scalar=rs0[:, u, 1:2], in1=e0, op0=ALU.mult,
                                             op1=ALU.add).then_inc(p0_a, 1)
                if s >= 2:
                    n = s - 2
                    h, qt = n // 4, n % 4
                    dve.wait_ge(p0_pv, n + 1)
                    dve.tensor_copy(o_feat0[:, N * h + P * qt:N * h + P * qt + P], bank[6 + n % 2][:, 0:P]
                                    ).then_inc(p0_o, 1)

            for g in range(4):
                dve.wait_ge(bhi_ready, g + 1)
                dve.scalar_tensor_tensor(out=blk[:, g, :].rearrange("p (h c) -> p h c", h=2), in0=acc_h[g % 2],
                                         scalar=gains[:, G_SCALE + g:G_SCALE + g + 1],
                                         in1=bhk[:, g, :].bitcast(F32).rearrange("p (h c) -> p h c", h=2),
                                         op0=ALU.mult, op1=ALU.subtract).then_inc(b_ready, 1)

            of0 = tiles(o_feat0, 4)
            sample_attention(0, orun0, samp[0])
            sample_finish(0, orun0, samp[0], of0)

            dve.wait_ge(p0_o, 16)
            for h in range(4):
                dve.wait_ge(sub_ms, h + 1)
                t1 = sqbuf[:, N * (h % 2):N * (h % 2) + N]
                t1h = t1.rearrange("p (h c) -> p h c", h=2)
                dve.tensor_scalar(t1h, halves[1 + h % 2], 1.0 / P, EPS, ALU.mult, ALU.add).then_inc(sub_v, 1)
                dve.wait_ge(sub_r, h + 1)
                link(dve.reciprocal(t1, t1))
                link(dve.scalar_tensor_tensor(out=t1, in0=of0[:, h, :], scalar=gains[:, G_SUBLN:G_SUBLN + 1], in1=t1,
                                              op0=ALU.mult, op1=ALU.mult))
                dve.tensor_scalar(t1, t1, 1.0 - LAM_INIT, None, ALU.mult).then_inc(sub_t, 1)
                dve.wait_ge(bhi_ready, 5 + h)
                dve.tensor_tensor(blk[:, 4 + h, :], t1, bhk[:, 4 + h, :].bitcast(F32), ALU.subtract).then_inc(b_ready, 1)

            dense(lambda i: i + T_OA // 4, 2, down, fin_post(1, G_MLP), static=True)
            mlp(0, T_M0)

            dense(lambda i: i + T_CD // 4, 3, to_proj(), peel=True, hook=rms(2))
            dve.wait_ge(acc_free, 2 + T_CD + 12)
            link(dve.tensor_tensor(proj[:, 4 * N:8 * N], proj[:, 4 * N:8 * N], proj[:, 8 * N:12 * N], ALU.mult))
            dve.wait_ge(hist_ps, 2)
            dve.tensor_copy(zext[:, :, :, 0:2], bank[6][:, 0:64].rearrange("p (k b c) -> p k b c", k=4, b=NB)
                            ).then_inc(hist_done, 1)
            dve.wait_ge(hist_done, 2)
            for k in range(4):
                link(dve.tensor_copy(zext[:, k, :, 2:10], pk[:, 4 + k, SEQ:N].rearrange("p (b c) -> p b c", b=NB)))
            dve.tensor_copy(dummy[:, :], cc("ones")[:, 0:1]).then_inc(pm_ready, 1)
            for k in range(4):
                w = [gains[:, G_CONV + 4 * j + k:G_CONV + 4 * j + k + 1] for j in range(3)]
                z, y = pk[:, 4 + k, :], cv[:, N * (k % 2):N * (k % 2) + N]
                ys = y[:, SEQ:N].rearrange("p (b c) -> p b c", b=NB)
                if k >= 2:
                    dve.wait_ge(b_ready, 40 + k - 1)
                link(dve.tensor_scalar(y, z, w[2], None, ALU.mult))
                for j in (1, 0):
                    d = 2 - j
                    dve.scalar_tensor_tensor(out=ys, in0=zext[:, k, :, j:j + 8], scalar=w[j], in1=ys, op0=ALU.mult,
                                             op1=ALU.add)
                    link(dve.scalar_tensor_tensor(out=y[:, d:SEQ], in0=z[:, 0:SEQ - d], scalar=w[j], in1=y[:, d:SEQ],
                                                  op0=ALU.mult, op1=ALU.add))
                dve.tensor_tensor(y, y, pk[:, k, :], ALU.mult).then_inc(sub_t, 1)
                dve.wait_ge(bhi_ready, 40 + k + 1)
                dve.tensor_tensor(blk[:, k, :], y, bhk[:, k, :].bitcast(F32), ALU.subtract).then_inc(b_ready, 1)
            dve.wait_ge(rows_ps, 2)
            dve.tensor_copy(e2[0][:, :], bank[7]).then_inc(rows_done, 1)

            for g in range(3):
                if g:
                    dve.wait_ge(qs_saved, 2 * (g + 1))
                dense(lambda i: i + (T_CD // 4 + 3 + 3 * g), 3, to_proj() if g < 2 else to_proj_streams())
                dve.wait_ge(acc_free, 2 + T_CD + 12 * (g + 2))
                dve.tensor_scalar(proj[:, 0:4 * N], proj[:, 0:4 * N], 0.125, None, ALU.mult).then_inc(q_scaled, 1)
                token_major(1 + g, g)
                if g == 0:
                    dve.wait_ge(rows_out, 80)
                for s in range(8 + 2):
                    if s < 8:
                        c, quad, its = units1[g][s]
                        for n, it in enumerate(its):
                            mask = items1[it][4]
                            dve.wait_ge(p1_s, it + 1)
                            sv = bank[it % 4].rearrange("p (h n) -> p h n", h=4)
                            link(dve.tensor_tensor(sv, sv, cc(mask).unsqueeze(1).broadcast_to([P, 4, P]), ALU.add))
                            dst = neg1[:, g, c, 4 * quad:4 * quad + 4] if n == 0 else negp[:, c, 4 * quad:4 * quad + 4]
                            ins = dve.tensor_reduce(dst, sv, AX.X, ALU.max, negate=True)
                            if n < len(its) - 1 or n == 1:
                                link(ins)
                            else:
                                ins.then_inc(p1_m, 1)
                        if len(its) == 2:
                            d = neg1[:, g, c, 4 * quad:4 * quad + 4]
                            dve.tensor_tensor(d, d, negp[:, c, 4 * quad:4 * quad + 4], ALU.min).then_inc(p1_m, 1)
                    if s >= 2 and s % 2:
                        u = 8 * g + s - 2
                        dve.wait_ge(p1_pv, u + 1)
                        src = bank[6 + u // 2 % 2].rearrange("p (i n) -> p i n", i=4)
                        og = tiles(o_g[g], 4)
                        for i in range(4):
                            dst, sr = tok_cols(og[:, i, 0:SEQ], g, units1[g][s - 2][0]), src[:, i, :]
                            if g == 2:
                                sr = sr.rearrange("p (r l) -> p r l", r=4)
                            last = dve.tensor_copy(dst, sr)
                        last.then_inc(p1_o, 1)

            dve.wait_ge(p1_e, len(items1))
            dve.wait_ge(p1_o, 12)
            s0 = sum1[:, 0, 1:4, :]
            dve.tensor_tensor(s0, s0, sump[:, 1:4, :], ALU.add).then_inc(cb_t, 1)
            dve.wait_ge(cb_d, 1)
            dve.wait_ge(vout, 16 * V_STORES[3])
            for i in range(2):
                dve.wait_ge(kout[i], 16 * K_STORES[i])
            for n, dst in enumerate((nm, sm)):
                for g in range(3):
                    src = bank[3 * n + g][0:8, :].rearrange("p (c n) -> p c n", c=4)
                    for c in range(4):
                        d, s_ = tok_cols(dst[g][0:8, :], g, c), src[:, c, :]
                        if g == 2:
                            s_ = s_.rearrange("p (r l) -> p r l", r=4)
                        last = dve.tensor_copy(d, s_)
            link(last)
            low = e2[0][0:8, :]
            link(dve.tensor_tensor(low, nm[0][0:8, :], nm[1][0:8, :], ALU.min))
            link(dve.tensor_tensor(low, low, nm[2][0:8, :], ALU.min))
            for g in range(3):
                last = dve.tensor_tensor(nm[g][0:8, :], low, nm[g][0:8, :], ALU.subtract)
            last.then_inc(cb_x, 1)
            dve.wait_ge(cb_e, 3)
            for g in range(3):
                last = dve.tensor_tensor(sm[g][0:8, :], sm[g][0:8, :], nm[g][0:8, :], ALU.mult)
            link(last)
            link(dve.tensor_tensor(low, sm[0][0:8, :], sm[1][0:8, :], ALU.add))
            link(dve.tensor_tensor(low, low, sm[2][0:8, :], ALU.add))
            link(dve.reciprocal(low, low))
            for g in range(3):
                last = dve.tensor_tensor(nm[g][0:8, :], nm[g][0:8, :], low, ALU.mult)
            last.then_inc(cb_c, 1)
            of1 = tiles(o_g[0], 4)
            for t in range(4):
                dve.wait_ge(cb_ps, t + 1)
                for g in range(3):
                    o = tiles(o_g[g], 4)[:, t, 0:SEQ]
                    last = dve.tensor_tensor(o, o, bank[(3 * t + g) % 6][:, :], ALU.mult)
                last.then_inc(cb_u, 1)
                dve.wait_ge(cb_u, t + 1)
                o = of1[:, t, 0:SEQ]
                link(dve.tensor_tensor(o, o, tiles(o_g[1], 4)[:, t, 0:SEQ], ALU.add))
                link(dve.tensor_tensor(o, o, tiles(o_g[2], 4)[:, t, 0:SEQ], ALU.add))

            dve.wait_ge(qs_saved, 8)
            sample_attention(1, orun1, samp[1])
            sample_finish(1, orun1, samp[1], of1)
            dve.wait_ge(SS[1]["fin_d"], 1)
            for t in range(4):
                t1 = sqbuf[:, N * (t % 2):N * (t % 2) + N]
                if t == 0:
                    dve.wait_ge(SS[1]["fin_ps"], 1)
                dve.tensor_copy(t1, of1[:, t, :]).then_inc(sub_t, 1)
                dve.wait_ge(bhi_ready, 45 + t)
                dve.tensor_tensor(blk[:, 4 + t, :], t1, bhk[:, 4 + t, :].bitcast(F32), ALU.subtract).then_inc(b_ready, 1)

            dense(lambda i: i + T_OC // 4, 2, down, fin_post(3, G_MLP + 8), static=True)
            mlp(1, T_M1)

            rms(4)()
            for k in range(KT_N):
                dve.scalar_tensor_tensor(out=y_feat[:, N * k:N * k + N], in0=xk[:, k, :],
                                         scalar=gains[:, G_OUT + k:G_OUT + k + 1], in1=rnorm[:, :], op0=ALU.mult,
                                         op1=ALU.mult).then_inc(y_ready, 1)
            for t in range(1, 5, 2):
                dve.wait_ge(yt_ps, t + 1)
                dve.wait_ge(yt_done, t)
                dve.tensor_copy(y_tok[:, t, :], acc[t % 2][:, :]).then_inc(yt_done, 1)

        @block.scalar
        def _(act):
            def split_hi(G, q, free=True):
                j = q % 2
                if j == 0:
                    act.wait_ge(raw_loaded[q // 2], G * 16 + 16)
                act.activation(whi_v[j], raw_v[q // 2][:, :, j, :], ACT.Copy).then_inc(whi_ready, 1)

            def dense(group, n_groups, post=None, peel=False, hook=None, static=False, last=False):
                def four(G, i):
                    for q in range(4):
                        act.wait_ge(tile_done, G * 4 + (q + 1))
                        if not (last and q >= 2 and i == n_groups - 1):
                            split_hi(*((G, q + 2) if q < 2 else (G + 1, q - 2)))
                        if hook and q == 0 and isinstance(i, int) and i == 0:
                            hook()
                        if post:
                            post(G, i, q)
                done = 0
                while done < n_groups and (static or n_groups - done == 1 or (peel and done == 0)):
                    four(group(done), done)
                    done += 1
                if done < n_groups:
                    with act.Fori(done, n_groups) as i:
                        four(group(i), i)

            def root(f):
                def go():
                    act.wait_ge(v_ready, f + 1)
                    act.activation(rnorm[:, :], rnorm[:, :], ACT.Sqrt).then_inc(sqrt_ready, 1)
                return go

            def up_post(s0, b0):
                def post(G, i, q):
                    act.wait_ge(sq_up, s0 + i * 4 + (q + 1))
                    act.activation(b_hi[:, ds(i * (4 * N) + q * N, N)], sqbuf[:, N * (q % 2):N * (q % 2) + N],
                                   ACT.Copy).then_inc(bhi_ready, 1)
                return post

            def fin_post(f, gcol, ready, r0, hi=True):
                def post(G, i, q):
                    k = 4 * i + q
                    act.wait_ge(ready, r0 + k + 1)
                    if hi:
                        act.activation(ahk[:, k, :], xk[:, k, :], ACT.Copy,
                                       scale=gains[:, gcol + k:gcol + k + 1]).then_inc(ahi_ready, 1)
                    if 8 * f + k >= 2:
                        act.wait_ge(sqs_done, 8 * f + k - 1)
                    act.activation(zbuf[:, N * (k % 2):N * (k % 2) + N], xk[:, k, :], ACT.Square).then_inc(xsq_ready, 1)
                return post

            def mlp(L, t0):
                G0, fb = t0 // 4, (8, 48)[L]
                dense(lambda i: i + G0, 2, up_post(32 * L, fb), peel=True, hook=root(1 + 2 * L))
                dense(lambda i: i + (G0 + 2), 2)
                with act.Fori(1, 3) as c:
                    dense(lambda i: c * 4 + (i + G0), 2, up_post(c * 8 + 32 * L, fb))
                    dense(lambda i: c * 4 + (i + (G0 + 2)), 2)
                dense(lambda i: i + (G0 + 12), 2, up_post(24 + 32 * L, fb))
                dense(lambda i: i + (G0 + 14), 2,
                      fin_post(2 + 2 * L, G_MIX + 8, acc_free, 2 + t0 + 56, hi=(L == 0)), static=True, last=(L == 1))

            def token_major(T):
                for c in range(5):
                    n = 5 * T + c
                    act.wait_ge(tk_ps, n + 1)
                    if K_BEFORE[n]:
                        act.wait_ge(kout[n % 2], 16 * K_BEFORE[n])
                    rows = P if c < 4 else NS
                    act.activation(k_tok[n % 2][0:rows, :], bank[6][0:rows, :], ACT.Copy).then_inc(tk_done, 1)

            def sample_attention(L, pt, stat):
                B, S = BLK[L], SS[L]
                kt = (kt_l0, kt_l1)[L][:, :].rearrange("p (i g n) -> p i g n", i=4, g=4)
                with act.Fori(0, NB) as b:
                    for i in range(6):
                        if i < 4:
                            for p in range(0, B["pages"][i], 2):
                                act.wait_ge(S["kt_ps"], b * B["pn"] + (4 * i + p + 1))
                                act.wait_ge(S["s"], b * 5 + i)
                                act.activation(kt[:, :, p, :], bank[0].rearrange("p (i n) -> p i n", i=4),
                                               ACT.Copy).then_inc(S["kt_a"], 1)
                        if i >= 1:
                            j = i - 1
                            act.wait_ge(S["pt_ps"], b * 5 + (j + 1))
                            act.wait_ge(S["o_ps"], b * 5 + (j - 1 if j >= 2 else 0))
                            n, w = (B["pages"][j], P) if j < 4 else (B["new"], NS)
                            act.activation(pt[j % 2][0:w, 0:P * n], bank[4 + j % 2][0:w, 0:P * n],
                                           ACT.Copy).then_inc(S["pt"], 1)
                        if i < 5:
                            neg = stat[:, S_NEG + i:S_NEG + i + 1]
                            act.wait_ge(S["neg"], b * 5 + (i + 1))
                            act.wait_ge(S["pt_ps"], b * 5 + (i - 1 if i >= 2 else 0))
                            if i:
                                act.activation(stat[:, S_ALPHA + i:S_ALPHA + i + 1],
                                               stat[:, S_NEG + i - 1:S_NEG + i], ACT.Exp, bias=neg, scale=-1.0)
                            w = P * B["pages"][i] if i < 4 else NS * B["new"]
                            act.activation(e2[i % 2][:, 0:w], bank[2 + i % 2][:, 0:w], ACT.Exp, bias=neg,
                                           accum_out=stat[:, S_SUM + i:S_SUM + i + 1]).then_inc(S["e"], 1)

            split_hi(0, 0)
            split_hi(0, 1)
            act.wait_ge(gain_ready, 1)
            for k in range(KT_N):
                fin_post(0, G_MIX, x_ready, 0)(0, 0, k)
            act.wait_ge(lam_d, 1)
            act.activation(lam_t[:, 130:132], lam_t[:, 128:130], ACT.Exp).then_inc(lam_e, 1)

            dense(lambda i: i, 4, peel=True, hook=root(0))
            token_major(0)
            for s in range(16 + 1):
                if s < 16:
                    qt, u = s % 4, s % 2
                    nk = P * (qt + 1)
                    act.wait_ge(p0_m, s + 1)
                    if s >= 2:
                        act.wait_ge(p0_t, s - 1)
                    for m in range(2):
                        last = act.activation(e4[u][m][:, 0:nk], bank[2 * u + m][:, 0:nk], ACT.Exp,
                                              bias=neg0[:, u, m:m + 1], accum_out=sum0[:, u, m:m + 1])
                    last.then_inc(p0_e, 1)
                if s >= 1:
                    n = s - 1
                    nk = P * (n % 4 + 1)
                    act.wait_ge(p0_t, n + 1)
                    if n >= 2:
                        act.wait_ge(p0_pv, n - 1)
                    act.activation(pt_l0[n % 2][:, 0:nk], bank[4 + n % 2][:, 0:nk], ACT.Copy).then_inc(p0_at, 1)
            for g in range(4):
                act.wait_ge(mix_ps, g + 1)
                act.activation(bhk[:, g, :].rearrange("p (h c) -> p h c", h=2), acc_h[g % 2], ACT.Copy,
                               scale=gains[:, G_SCALE + g:G_SCALE + g + 1]).then_inc(bhi_ready, 1)
            sample_attention(0, pt_l0, samp[0])
            of0 = tiles(o_feat0, 4)
            act.wait_ge(SS[0]["fin_d"], 1)
            for h in range(4 + 1):
                if h < 4:
                    if h >= 2:
                        act.wait_ge(sub_ms, h - 1)
                    act.activation(zbuf[:, N * (h % 2):N * (h % 2) + N], of0[:, h, :], ACT.Square).then_inc(sub_sq, 1)
                if h >= 1:
                    t1 = sqbuf[:, N * ((h - 1) % 2):N * ((h - 1) % 2) + N]
                    act.wait_ge(sub_v, h)
                    act.activation(t1, t1, ACT.Sqrt).then_inc(sub_r, 1)
                    act.wait_ge(sub_t, h)
                    act.activation(bhk[:, 3 + h, :], t1, ACT.Copy).then_inc(bhi_ready, 1)
            dense(lambda i: i + T_OA // 4, 2, fin_post(1, G_MLP, acc_free, 2 + T_OA), static=True)
            mlp(0, T_M0)

            dense(lambda i: i + T_CD // 4, 3, peel=True, hook=root(2))
            for k in range(4):
                act.wait_ge(sub_t, 4 + k + 1)
                act.activation(bhk[:, k, :], cv[:, N * (k % 2):N * (k % 2) + N], ACT.Copy).then_inc(bhi_ready, 1)
            for g in range(3):
                dense(lambda i: i + (T_CD // 4 + 3 + 3 * g), 3)
                token_major(1 + g)
                for s in range(8 + 1):
                    if s < 8:
                        c, quad, its = units1[g][s]
                        act.wait_ge(p1_m, 8 * g + s + 1)
                        for n, it in enumerate(its):
                            if it >= 2:
                                act.wait_ge(p1_t, it - 1)
                            for hh in range(4):
                                head = 4 * quad + hh
                                dst = sum1[:, g, c, head:head + 1] if n == 0 else sump[:, c, head:head + 1]
                                last = act.activation(e2[it % 2][:, P * hh:P * hh + P],
                                                      bank[it % 4][:, P * hh:P * hh + P], ACT.Exp,
                                                      bias=neg1[:, g, c, head:head + 1], accum_out=dst)
                            last.then_inc(p1_e, 1)
                    if s >= 1:
                        for it in units1[g][s - 1][2]:
                            act.wait_ge(p1_t, it + 1)
                            if it >= 2:
                                act.wait_ge(p1_pv, UNIT_OF[it - 2] + 1)
                            act.activation(pt_l1[it % 2][:, :], bank[4 + it % 2][:, :], ACT.Copy).then_inc(p1_pt, 1)
            act.wait_ge(cb_x, 1)
            for g in range(3):
                act.activation(nm[g][0:8, :], nm[g][0:8, :], ACT.Exp).then_inc(cb_e, 1)
            act.wait_ge(qs_saved, 8)
            sample_attention(1, pt_l1, samp[1])
            for t in range(4):
                act.wait_ge(sub_t, 8 + t + 1)
                act.activation(bhk[:, 4 + t, :], sqbuf[:, N * (t % 2):N * (t % 2) + N], ACT.Copy).then_inc(bhi_ready, 1)
            dense(lambda i: i + T_OC // 4, 2, fin_post(3, G_MLP + 8, acc_free, 2 + T_OC), static=True)
            mlp(1, T_M1)

            root(4)()
            for t in range(0, 5, 2):
                rows = P if t < 4 else NS
                act.wait_ge(yt_ps, t + 1)
                act.wait_ge(yt_done, t)
                act.activation(y_tok[0:rows, t, :], acc[t % 2][0:rows, :], ACT.Copy).then_inc(yt_done, 1)

        @block.gpsimd
        def _(pool):
            steps = Tally()

            def link(ins):
                ins.then_inc(pool_step, 1)
                pool.wait_ge(pool_step, steps.add())

            def sum_squares(f):
                for k in range(KT_N):
                    pool.wait_ge(xsq_ready, 8 * f + k + 1)
                    src = zbuf[:, N * (k % 2):N * (k % 2) + N]
                    if k == 0:
                        if f:
                            pool.wait_ge(ms_ready, f)
                        pool.tensor_copy(sqsum[:, :], src).then_inc(sqs_done, 1)
                    else:
                        pool.wait_ge(sqs_done, 8 * f + k)
                        pool.tensor_tensor(sqsum[:, :], sqsum[:, :], src, ALU.add).then_inc(sqs_done, 1)

            def save_samples(n, g, qb):
                pool.wait_ge(q_scaled, n)
                pool.tensor_copy(q_s[:, g, :, :], pk[:, qb:qb + 4, SEQ:N]).then_inc(qs_saved, 1)
                pool.tensor_copy(k_s[:, g, :, :], pk[:, qb + 4:qb + 8, SEQ:N]).then_inc(qs_saved, 1)

            def stage_queries(L, groups):
                S = SS[L]
                pool.wait_ge(qs_saved, (2, 8)[L])
                with pool.Fori(0, NB) as b:
                    pool.wait_ge(S["s"], b * 5)
                    for hf in range(2):
                        pool.wait_ge(S["q"], b * 2 + hf)
                        src = q_s[64 * hf:64 * hf + 64, 0:groups, :, :]
                        pool.tensor_copy(q_st[64 * hf:64 * hf + 64, 0:groups, :, 8 * hf:8 * hf + 8],
                                         src[:, :, :, ds(b * 8, 8)]).then_inc(S["q"], 1)
                pool.wait_ge(S["q"], 2 * NB)

            def copy(dst, src):
                pool.dma_start(dst, src).then_inc(outs[3], 16)

            pool.memset(q_st, 0.0).then_inc(q_zero, 1)
            pool.wait_ge(q_zero, 1)
            copy(a["new_pool_sample"][0][:, 0:7, :], a["state_a_pool"][0][:, 8:15, :])
            sum_squares(0)
            link(pool.memset(pool_a[:, :, 0:16], 0.0))

            save_samples(1, 0, 4)
            pool.wait_ge(hist_done, 1)
            pool.wait_ge(rows_ps, 1)
            for g in range(4):
                w = 2 << g
                u = pk[:, g, 0:SEQ]
                us = pk[:, g, SEQ:N].rearrange("p (b c) -> p b c", b=NB)
                if g:
                    pool.wait_ge(pm_ready, g)
                pool.tensor_copy(pool_s[:, 0, :, 0:15], hist_f[:, g, :, :])
                pool.tensor_copy(pool_s[:, 0, :, 15:23], us)
                link(pool.tensor_copy(pool_a[:, 0, 16:528], u))
                for j in range(g + 1):
                    d, s, k = pool_a[:, (j + 1) % 2, :], pool_a[:, j % 2, :], 1 << j
                    ss_, sd = pool_s[:, j % 2, :, :], pool_s[:, (j + 1) % 2, :, :]
                    pool.tensor_tensor(sd[:, :, 2 * k - 1:23], ss_[:, :, 2 * k - 1:23], ss_[:, :, k - 1:23 - k], ALU.add)
                    link(pool.tensor_tensor(d[:, 16:528], s[:, 16:528], s[:, 16 - k:528 - k], ALU.add))
                m, ms = pool_a[:, (g + 1) % 2, :], pool_s[:, (g + 1) % 2, :, 15:23]
                pool.tensor_tensor(m[:, 16:16 + w - 1], m[:, 16:16 + w - 1], cc("rtab")[:, 0:w - 1], ALU.mult)
                pool.tensor_scalar(ms, ms, 1.0 / w, None, ALU.mult)
                link(pool.tensor_scalar(m[:, 16 + w - 1:528], m[:, 16 + w - 1:528], 1.0 / w, None, ALU.mult))
                pool.tensor_tensor(us, ms, us, ALU.subtract)
                pool.tensor_tensor(u, m[:, 16:528], u, ALU.subtract).then_inc(pm_ready, 1)
            pool.wait_ge(pm_ready, 4)
            stage_queries(0, 1)
            sum_squares(1)

            def kept(g):
                return (a[f"new_d{g}_sample"][0].rearrange("b t v h e -> b t (v h e)"),
                        a[f"cache_d{g}_kv"][0].rearrange("b t v h e -> b t (v h e)"))

            def piece(g, b, row, rows, cut):
                dst, src = kept(g)
                f = lambda v, r: (v[ds(b, 1), ds(r, rows), :].rearrange("o t f -> (o t f)")
                                  .rearrange("(p q) -> p q", q=cut))
                copy(f(dst, row), f(src, row + TS))

            QROWS = (WIN[2] - TS) // 4
            with pool.Fori(0, NB - 1) as b:
                for q in range(4):
                    pool.wait_ge(tile_done, b * 8 + (T_M0 + 2 * q + 1))
                    piece(2, b, QROWS * q, QROWS, QROWS * 1024 // 32)
            sum_squares(2)

            for g in range(3):
                save_samples(2 + g, g, 0)
            stage_queries(1, 3)
            sum_squares(3)
            for q in range(4):
                pool.wait_ge(tile_done, T_M1 + 2 * q + 1)
                piece(2, NB - 1, QROWS * q, QROWS, QROWS * 1024 // 32)
            with pool.Fori(0, NB) as b:
                pool.wait_ge(tile_done, b * 2 + (T_M1 + 9))
                piece(1, b, 0, WIN[1] - TS, (WIN[1] - TS) * 1024 // 32)
            for b in range(0, NB, 4):
                pool.wait_ge(tile_done, T_M1 + 25 + b // 2)
                dst, src = kept(0)
                copy(dst[b:b + 4, 0:WIN[0] - TS, :], src[b:b + 4, TS:WIN[0], :])
            sum_squares(4)
            pool.wait_ge(outs[3], 16 * (1 + 32 + 8 + 2))


_SHAPES = [("y_prompt", (1, SEQ, D)), ("y_sample", (NB, TS, D)), ("new_pool_prompt", (1, 1, 15, 512)),
           ("new_pool_sample", (1, NB, 15, 512)), ("new_bkv_prompt", (1, 1, SEQ, 2, 4, 128)),
           ("new_bkv_sample", (1, NB, TS, 2, 4, 128)), ("new_conv_prompt", (1, 1, 2, 512)),
           ("new_conv_sample", (1, NB, 2, 512))]
for _g in range(3):
    _SHAPES += [(f"new_d{_g}_prompt", (1, 1, min(WIN[_g], SEQ), 2, 8, 64)),
                (f"new_d{_g}_sample", (1, NB, WIN[_g], 2, 8, 64))]


def kernel(**inputs):
    import concourse.bacc as bacc
    from concourse.bass_utils import run_bass_kernel_spmd

    nc = bacc.Bacc("TRN2", target_bir_lowering=False, num_devices=1)
    arrays = {name: np.ascontiguousarray(v) for name, v in inputs.items()}
    arrays["consts"] = constants()
    arrays = {f"in_{name}": v for name, v in arrays.items()}
    aps = {name[3:]: nc.dram_tensor(name, v.shape, mybir.dt.from_np(v.dtype), kind="ExternalInput").ap()
           for name, v in arrays.items()}
    for name, shape in _SHAPES:
        aps[name] = nc.dram_tensor(f"out_{name}", shape, F32, kind="ExternalOutput").ap()
    build(nc, aps)
    r = run_bass_kernel_spmd(nc, [arrays], core_ids=[0])
    return tuple(r.results[0][f"out_{name}"] for name, _ in _SHAPES)
```

```python
from contextlib import ExitStack, contextmanager

import numpy as np
import concourse.bass as bass
from concourse import mybir

F32 = mybir.dt.float32
F32R = mybir.dt.float32r
I32 = mybir.dt.int32
ALU = mybir.AluOpType
ACT = mybir.ActivationFunctionType
AX = mybir.AxisListType
ds = bass.ds

P = 128
D = 1024
KT_N = D // P
SEQ, NB, TS = 512, 8, 8
NS = NB * TS
N = SEQ + NS
NH = N // 2
EPS = 1e-6
LAM_INIT = 0.8 - 0.6
NEG = -1e30
PAST, PAGE = 2048, 128
NPAGES = PAST // PAGE
WIN, DIL = (128, 512, 2048), (1, 4, 16)
FF = 4 * D

T_AB, T_OA, T_M0 = 0, 16, 24
T_CD = T_M0 + 64
T_OC = T_CD + 48
T_M1 = T_OC + 8
T_END = T_M1 + 64

C = {}
_at = 0
for _n, _w in (("ident", 128), ("ones", 128), ("causal", 128), ("prev", 128), ("g2m", 128), ("rm2", 8), ("rm1", 4),
               ("k01", 4), ("g0m", 8), ("selfm", 360), ("sel", 32), ("halfm", 2), ("m01", 2), ("rtab", 16),
               ("sel8", 512)):
    C[_n] = (_at, _w)
    _at += _w
NC_ = (_at + 7) // 8 * 8


def constants():
    c = np.zeros((P, NC_), np.float32)

    def put(name, a):
        c[:a.shape[0], C[name][0]:C[name][0] + C[name][1]] = a

    i = np.arange(P)
    put("ident", np.eye(P))
    put("ones", np.ones((P, P)))
    put("causal", np.where(i[None] <= i[:, None], 0, NEG))
    put("prev", np.where(i[None] >= i[:, None], 0, NEG))
    r, l = i // 32, i % 32
    put("g2m", np.where((r[:, None] == r[None]) & (l[None] <= l[:, None]), 0, NEG))
    real = (i % 32) < 16
    t, half = i % 8, (i % 32) // 8
    put("rm2", np.where(real[:, None] & (t[:, None] != np.arange(8)[None]), NEG, 0))
    put("rm1", np.where(real[:, None] & (t[:, None] % 4 != np.arange(4)[None]), NEG, 0))
    put("k01", np.where(real[:, None] & (t[:, None] == np.arange(4)[None] + 4), NEG, 0))
    put("g0m", np.where(real[:, None] & (np.arange(8)[None] < t[:, None]), NEG, 0))
    sm = np.zeros((P, 3, 15, 8), np.float32)
    sm[real] = NEG
    for g in range(3):
        for row in i[real]:
            for t2 in range(8):
                if t2 <= t[row] and (t[row] - t2) % DIL[g] == 0:
                    sm[row, g, 7, t2] = 0
    put("selfm", sm.reshape(P, 360))
    sel = np.zeros((P, 32), np.float32)
    for row in i[real]:
        sel[row, (row // 32) * 8 + t[row]] = 1
    put("sel", sel)
    put("halfm", (half[:, None] == np.arange(2)[None]) & real[:, None])
    put("m01", (half[:, None] == np.arange(2)[None]) & real[:, None])
    put("rtab", np.broadcast_to(1.0 / (1.0 + np.arange(16)), (P, 16)))
    s8 = np.zeros((8, 4, P), np.float32)
    for h in range(8):
        s8[h, h % 4, 64 * (h // 4):64 * (h // 4) + 64] = 1
    put("sel8", s8.reshape(8, 512))
    return c


class Tally:

    def __init__(self):
        self.n, self.terms = 0, []

    def add(self, k=1):
        self.n += k
        return self.now()

    def now(self):
        v = self.n
        for reg, k in self.terms:
            v = reg * k + v
        return v

    @contextmanager
    def loop(self, reg, per, first, end):
        start = self.n
        self.n = start - first * per
        self.terms.append((reg, per))
        inner = self.n
        yield
        self.terms.pop()
        assert self.n - inner == per, (self.n - inner, per)
        self.n = start + per * (end - first)


def build(nc, a):
    with ExitStack() as ctx:
        sem = lambda name: ctx.enter_context(nc.semaphore(name))

        pp = [ctx.enter_context(nc.psum_tensor(f"pp{i}", [P, 1024], F32)) for i in range(4)]
        bank = [pp[i // 2][:, 512 * (i % 2):512 * (i % 2) + 512] for i in range(8)]
        halves = [pp[i][:, :].rearrange("p (h c) -> p h c", h=2)[:, :, 0:NH] for i in range(4)]
        acc = pp[0:2]
        acc_h = halves[0:2]

        base = nc.sbuf_base
        total = (nc.sbuf_usable_end - base) // 32 * 8 - 16
        ctx.enter_context(nc.sbuf_tensor("whole_map", [P, total], F32))
        base = (base + 31) // 32 * 32

        def at(name, word, words, dt=F32):
            assert word + words <= total, (name, word + words, total)
            return nc.alloc_sbuf_tensor_at(name, [P, words], dt, offset=base + 4 * word)

        def tiles(t, n, first=0):
            return t[:, first * N:(first + n) * N].rearrange("p (k n) -> p k n", n=N)

        W_X, W_A, W_B = 0, KT_N * N, 3 * KT_N * N
        W_RAW = W_B + 2 * KT_N * N
        W_W = W_RAW + 4096
        W_PROJ = W_W + 4096
        W_TMP = W_PROJ + 16 * N
        W_CONST = W_TMP + 6 * N
        W_G = W_CONST + NC_
        W_S = W_G + 64
        x = at("x", W_X, KT_N * N)
        a_hi, a_lo = at("a_hi", W_A, KT_N * N, F32R), at("a_lo", W_A + KT_N * N, KT_N * N, F32R)
        b_hi, b_lo = at("b_hi", W_B, KT_N * N, F32R), at("b_lo", W_B + KT_N * N, KT_N * N, F32R)
        xk = tiles(x, 8)
        ahk, alk, bhk, blk = (tiles(t, 8) for t in (a_hi, a_lo, b_hi, b_lo))
        raw = [at(f"raw{i}", W_RAW + 2048 * i, 2048) for i in range(2)]
        whi = [at(f"whi{i}", W_W + 1024 * i, 1024, F32R) for i in range(2)]
        wlo = [at(f"wlo{i}", W_W + 2048 + 1024 * i, 1024, F32R) for i in range(2)]
        raw_v = [t[:, :].rearrange("p (k j n) -> p k j n", k=KT_N, j=2) for t in raw]
        whi_v = [t[:, :].rearrange("p (k n) -> p k n", k=KT_N) for t in whi]
        wlo_v = [t[:, :].rearrange("p (k n) -> p k n", k=KT_N) for t in wlo]
        proj = at("proj", W_PROJ, 16 * N)
        pk = tiles(proj, 16)
        rnorm = at("rnorm", W_TMP, N)
        r_h = rnorm[:, :].rearrange("p (h c) -> p h c", h=2)
        zbuf = at("zbuf", W_TMP + N, 2 * N)
        sqbuf = at("sqbuf", W_TMP + 3 * N, 2 * N)
        sqsum = at("sqsum", W_TMP + 5 * N, N)
        dummy = at("dummy", total - 8, 1)
        con = at("con", W_CONST, NC_)
        gains = at("gains", W_G, 64)
        cc = lambda n: con[:, C[n][0]:C[n][0] + C[n][1]]
        ident, ones = cc("ident"), cc("ones")
        G_MIX, G_MLP, G_OUT, G_SCALE, G_CONV, G_SUBLN = 0, 16, 32, 40, 44, 56

        W_AX = W_A + 4 * 2048
        W_BH, W_BL = W_B + 4 * N, W_B + KT_N * N + 4 * N
        W_V, W_K, W_Q, W_E = W_S, W_S + 2048, W_S + 3072, W_S + 6144
        W_QST = W_S + 7168
        W_STAT = W_TMP + 3 * N
        x_tok = at("x_tok", W_PROJ, 5 * D)[:, :].rearrange("p (t d) -> p t d", d=D)
        gain_rows = at("gain_rows", W_S, P)
        kring = [at(f"kring{i}", W_A + 2048 * i, 2048) for i in range(2)]
        vring = [at(f"vring{i}", W_A + 4096 + 2048 * i, 2048) for i in range(2)]
        kring0, vring0 = at("kring_l0", W_B, 2048), at("vring_l0", W_B + KT_N * N, 2048)
        kring_v, vring_v = ([[t[:, :].rearrange("p (g f) -> p g f", g=4) for t in r] for r in rings]
                            for rings in (((kring0, kring[1]), kring), ((vring0, vring[1]), vring)))
        v_all = at("v_all", W_V, 2048)[:, :].rearrange("p (c f) -> p c f", c=4)
        k_tok = [at(f"k_tok{i}", W_K + 512 * i, 512) for i in range(2)]
        qkv_s = at("qkv_s", W_Q, 3072)[:, :].rearrange("p (g w) -> p g w", g=3)
        q_s = qkv_s[:, :, 0:256].rearrange("p g (i n) -> p g i n", i=4)
        k_s = qkv_s[:, :, 256:512].rearrange("p g (i n) -> p g i n", i=4)
        v_s = qkv_s[:, :, 512:1024]
        e2 = [at(f"e{i}", W_E + 512 * i, 512) for i in range(2)]
        q_st = at("q_st", W_QST, 384)[:, :].rearrange("p (g i c) -> p g i c", g=3, i=4)
        neglam = at("neglam", W_QST + 384, 2)
        pages = nc.alloc_sbuf_tensor_at("pages", [1, P], I32, offset=base + 4 * (W_Q + 2928))
        lam_in = at("lam_in", W_E, 256)
        lam_t = at("lam_t", W_E + 256, 132)
        pt_l0 = [at(f"pt_l0{i}", W_AX + 512 * i, 512) for i in range(2)]
        pt_l1 = [at(f"pt_l1{i}", W_PROJ + 12 * N + 512 * i, 512) for i in range(2)]
        hist_tok = at("hist_tok", W_STAT, 512)
        a_mix = at("a_mix", W_STAT + 640, 512)
        stat0 = at("stat0", W_STAT + 512, 128)
        e4 = [[at(f"e4{u}{m}", W_BL + 1024 * u + 512 * m, 512) for m in range(2)] for u in range(2)]
        pt_p0 = [at(f"pt_p0{i}", W_PROJ + 12 * N + 512 * i, 512) for i in range(2)]
        kt_l0 = [at(f"kt_l0{i}", W_A + 4096 * i, 2048) for i in range(2)]
        o_feat0 = at("o_feat0", W_BH, 4 * N)
        orun0 = at("orun0", W_TMP + N, 1024)
        pool_a = at("pool_a", W_Q + 1024, 2 * 528)[:, :].rearrange("p (i c) -> p i c", i=2)
        pool_s = at("pool_s", W_Q + 1024 + 1056, 2 * 184)[:, :].rearrange("p (i b c) -> p i b c", i=2, b=NB)
        hist_f = at("hist_f", W_Q + 1024 + 1056 + 368, 480)[:, :].rearrange("p (g b c) -> p g b c", g=4, b=NB)
        conv_tok = at("conv_tok", W_STAT, 512)
        stat1 = at("stat1", W_STAT + 512, 640)
        cv = at("cv", W_V, 2 * N)
        zext = at("zext", W_V + 2 * N, 320)[:, :].rearrange("p (k b c) -> p k b c", k=4, b=NB)
        kt_l1 = [at(f"kt_l1{i}", W_RAW + 2048 * i, 2048) for i in range(2)]
        e_l1 = [at(f"e_l1{i}", W_W + 512 * i, 512) for i in range(2)]
        pt_s1 = [at(f"pt_s1{i}", W_W + 1024 + 512 * i, 512) for i in range(2)]
        e_sa = [e2, e_l1]
        q_st1 = at("q_st1", W_W + 3072, 384)[:, :].rearrange("p (g i c) -> p g i c", g=3, i=4)
        staged = [[q_st[:, 0:1, :, :], q_st[:, 1:2, :, :]], [q_st, q_st1]]
        kt_sa = [[t[:, :].rearrange("p (i g n) -> p i g n", i=4, g=4) for t in k] for k in (kt_l0, kt_l1)]
        orun1 = at("orun1", W_W + 2048, 1024)
        o_g = [at("o_g0", W_BH, 4 * N), at("o_g1", W_BL, 4 * N), at("o_g2", W_PROJ + 8 * N, 4 * N)]
        nm = [at(f"nm{g}", W_V + 512 * g, 512) for g in range(3)]
        sm = [at(f"sm{g}", W_V + 1536 + 512 * g, 512) for g in range(3)]
        y_feat = at("y_feat", W_A, KT_N * N)
        y_tok = at("y_tok", W_PROJ, 5 * D)[:, :].rearrange("p (t d) -> p t d", d=D)

        neg0 = stat0[:, 0:4].rearrange("p (u m) -> p u m", u=2)
        sum0 = stat0[:, 4:8].rearrange("p (u m) -> p u m", u=2)
        rs0 = stat0[:, 8:12].rearrange("p (u m) -> p u m", u=2)
        S_NEG, S_TMP, S_ALPHA, S_SUM, S_RUN, S_REC, S_COMB = 0, 5, 6, 12, 18, 26, 34
        neg1 = stat1[:, 320:416].rearrange("p (g c h) -> p g c h", g=3, c=4)
        sum1 = stat1[:, 416:512].rearrange("p (g c h) -> p g c h", g=3, c=4)
        negp = stat1[:, 512:544].rearrange("p (c h) -> p c h", c=4)
        sump = stat1[:, 544:576].rearrange("p (c h) -> p c h", c=4)
        samp = [at("samp0", W_STAT, 512), at("samp1", W_STAT, 512)]

        s_const, s_x, s_gain, s_lam, s_hist, s_page = (sem(n) for n in
            ("const_loaded", "x_loaded", "gains_loaded", "lam_loaded", "hist_loaded", "pages_loaded"))
        raw_loaded = [sem(f"raw_loaded{i}") for i in range(2)]
        whi_ready, wlo_ready = sem("whi_ready"), sem("wlo_ready")
        tile_done, acc_free = sem("tile_done"), sem("acc_free")
        ahi_ready, a_ready = sem("ahi_ready"), sem("a_ready")
        bhi_ready, b_ready = sem("bhi_ready"), sem("b_ready")
        xsq_ready, sqs_done = sem("xsq_ready"), sem("sqs_done")
        ms_ready, v_ready, sqrt_ready = sem("ms_ready"), sem("v_ready"), sem("sqrt_ready")
        gain_ps, gain_ready, xt_ps, x_ready = sem("gain_ps"), sem("gain_ready"), sem("xt_ps"), sem("x_ready")
        sq_up = sem("sq_up")
        dve_step, pool_step = sem("dve_step"), sem("pool_step")
        lam_e, lam_d = sem("lam_e"), sem("lam_d")
        outs = [sem(f"outs{i}") for i in range(4)]
        tk_ps, tv_ps, tk_done, tv_done = (sem(n) for n in ("tk_ps", "tv_ps", "tk_done", "tv_done"))
        kout = [sem(f"kout{i}") for i in range(2)]
        vout = sem("vout")
        q_scaled, qs_saved = sem("q_scaled"), sem("qs_saved")
        hist_ps, hist_done, rows_ps, rows_done, rows_out = (sem(n) for n in
            ("hist_ps", "hist_done", "rows_ps", "rows_done", "rows_out"))
        pm_ready, mix_ps = sem("pm_ready"), sem("mix_ps")
        p0_s, p0_m, p0_e, p0_a, p0_t, p0_at, p0_pv, p0_o = (sem(f"p0_{n}") for n in
            ("s", "m", "e", "a", "t", "at", "pv", "o"))
        p1_s, p1_m, p1_e, p1_t, p1_pt, p1_pv, p1_o = (sem(f"p1_{n}") for n in
            ("s", "m", "e", "t", "pt", "pv", "o"))
        sub_sq, sub_ms, sub_v, sub_r, sub_t = (sem(f"sub_{n}") for n in ("sq", "ms", "v", "r", "t"))
        SS = []
        for L in range(2):
            SS.append({n: sem(f"sa{L}_{n}") for n in
                       ("k00", "k01", "k10", "k11", "v00", "v01", "v10", "v11", "q", "kt_ps", "kt_a", "kt_d", "s", "neg", "e", "pt_ps", "pt",
                        "o_ps", "o", "fin", "fin_ps", "fin_d")})
        cb_t, cb_d, cb_v, cb_x, cb_e, cb_c, cb_ps, cb_u = (sem(f"cb_{n}") for n in
            ("t", "d", "v", "x", "e", "c", "ps", "u"))
        y_ready, yt_ps, yt_done = sem("y_ready"), sem("yt_ps"), sem("yt_done")
        q_zero = sem("q_zero")

        def tok_cols(v, g, c):
            if g == 0:
                return v[:, 128 * c:128 * c + 128]
            if g == 1:
                return v.rearrange("p (l r) -> p r l", r=4)[:, c, :]
            return v.rearrange("p (l c r) -> p c r l", c=4, r=4)[:, c, :, :]

        def proj_cols(v, g, c):
            return tok_cols(v, g if g < 2 else 0, c)

        units1, items1 = [[], [], []], []
        for g in range(3):
            for c in range(4):
                for quad in range(2):
                    parts = [(c, ("causal", "causal", "g2m")[g])] + ([(c - 1, "prev")] if g == 0 and c else [])
                    u = []
                    for kc, mask in parts:
                        u.append(len(items1))
                        items1.append((g, c, quad, kc, mask))
                    units1[g].append((c, quad, u))
        UNIT_OF = {it: 8 * g + s for g in range(3) for s, u in enumerate(units1[g]) for it in u[2]}
        BLK = [dict(pages=(4, 4, 4, 4), groups=(0, 0, 0, 0), new=1, mask=(None,) * 4),
               dict(pages=(4, 4, 4, 1), groups=(2, 2, 1, 0), new=3, mask=("rm2a", "rm2b", "rm1", "g0m"))]
        for b_ in BLK:
            b_["pn"] = sum(b_["pages"])
            b_["pa"] = sum((n + 1) // 2 for n in b_["pages"])
            b_["pd"] = b_["pn"] - b_["pa"]

        def each_sequence(engine, body):
            body(0)
            with engine.Fori(1, NB - 1) as b:
                body(b)
            body(NB - 1)

        SCORES, WEIGHTS, OUTPUT = bank[2], bank[3], bank[6][:, 0:P]
        P0_SCORES, P0_WEIGHTS, P0_OUTPUT = pp[2], bank[7], bank[7][:, 0:P]

        def beside(b, i, first, stage, last):
            s, rest = divmod(5 * b + i - first, 2)
            if rest == 0 and 0 <= s <= last:
                stage(s)

        P1_SCORES, P1_WEIGHTS, P1_OUTPUT, CB_BANKS = bank[4], bank[5], bank[7], (bank[4], bank[5], bank[7])

        def once(b, i, m, stage):
            if 5 * b + i == m:
                stage()

        def at_least(engine, semaphore, value):
            if not isinstance(value, int) or value > 0:
                engine.wait_ge(semaphore, value)

        def keys_beside(b, i, keys, pages):
            if i < 3:
                keys(b, i + 1, pages)
            elif i == 4 and b < NB - 1:
                keys(b + 1, 0, pages)

        def load_block(eng, L, kv, b, i, half):
            B, S = BLK[L], SS[L]
            slot, ring, done = i % 2, (kring_v, vring_v)[kv][L], S[f"{'kv'[kv]}{i % 2}{half}"]
            p0 = 2 * half
            p1 = min(p0 + 2, B["pages"][i])
            if p1 <= p0:
                return
            if L == 0:
                page = [eng.value_load(pages[0:1, ds(b * 16 + (4 * i + p), 1)], min_val=0,
                                       max_val=a["cache_b_kv"].shape[1] - 1) for p in range(p0, p1)]
            if kv == 0:
                if i >= 2:
                    at_least(eng, S["kt_ps"], b * B["pn"] + (4 * (i - 2) + min(B["pages"][i - 2], p0 + 2)))
                else:
                    at_least(eng, S["kt_ps"], b * B["pn"] + (4 * (i + 2) + min(B["pages"][i + 2], p0 + 2) - B["pn"]))
            else:
                at_least(eng, S["o_ps"], b * 5 + (i - 1 if i >= 2 else i - 2))
            if L == 0:
                for p in range(p0, p1):
                    eng.dma_start(ring[slot][:, p, :],
                                  a["cache_b_kv"][0][ds(page[p - p0], 1)].rearrange("o t v h e -> (o t) v (h e)")
                                  [:, kv, :]).then_inc(done, 16)
            else:
                g = B["groups"][i]
                src = a[f"cache_d{g}_kv"][0][ds(b, 1)].rearrange("o (i s) v h e -> (o i) s v (h e)", s=DIL[g])
                s0 = p0 + (4 * i if g == 2 else 0)
                eng.dma_start(ring[slot][:, p0:p1, :], src[:, s0:s0 + p1 - p0, kv, :]).then_inc(done, 16)

        def loaded(L, b, i, half):
            B = BLK[L]
            n = [B["pages"][j] > 2 * half for j in (i % 2, i % 2 + 2)]
            return (b * sum(n) + sum(n[:1 + i // 2])) * (32 if L == 0 else 16)

        stored = [not (T == 1 and c < 3) for T in range(4) for c in range(5)]
        V_STORES = [sum(stored[0:5 * T + 5]) for T in range(4)]
        K_BEFORE = [sum(stored[j] for j in range(n % 2, n, 2)) for n in range(22)]
        K_STORES = (K_BEFORE[20], K_BEFORE[21])

        block = ctx.enter_context(nc.Block())

        @block.sync
        def _(sp):
            sp.dma_start(con[:, :], a["consts"]).then_inc(s_const, 16)
            sp.dma_start(x_tok[:, 0:4, :], a["x_prompt"][0].rearrange("(t p) d -> p t d", p=P)).then_inc(s_x, 16)
            sp.dma_start(x_tok[0:NS, 4, :], a["x_sample"].rearrange("b t d -> (b t) d")).then_inc(s_x, 16)

            def unit(w, col, n, slot, wait=True):
                if wait:
                    sp.wait_ge(wlo_ready, 2 * n - 2)
                sp.dma_start(raw_v[slot].rearrange("p k j n -> p k (j n)"),
                             w.rearrange("(k p) n -> p k n", p=P)[:, :, ds(col, 256)]).then_inc(raw_loaded[slot], 16)

            def matrix(w, t0, n_tiles, first=0):
                if n_tiles // 4 - first == 1:
                    for s in range(2):
                        unit(w, 512 * first + 256 * s, t0 // 2 + 2 * first + s, s)
                    return
                with sp.Fori(first, n_tiles // 4) as i:
                    for s in range(2):
                        unit(w, i * 512 + 256 * s, i * 2 + t0 // 2 + s, s)

            def mlp_weights(L, t0):
                up, down = a["w_up"][L], a["w_down"][L].rearrange("(c k) n -> c k n", c=4)
                with sp.Fori(0, 4) as c:
                    with sp.Fori(0, 2) as i:
                        for s in range(2):
                            unit(up, c * 1024 + i * 512 + 256 * s, c * 8 + i * 2 + t0 // 2 + s, s)
                    with sp.Fori(0, 2) as i:
                        for s in range(2):
                            sp.wait_ge(wlo_ready, (c * 8 + i * 2 + (t0 // 2 + 4 + s)) * 2 - 2)
                            sp.dma_start(raw_v[s].rearrange("p k j n -> p k (j n)"),
                                         down[ds(c, 1), :, ds(i * 512 + 256 * s, 256)]
                                         .rearrange("o (k p) n -> p (o k) n", p=P)).then_inc(raw_loaded[s], 16)

            def cache_blocks(L):
                def sequence(b):
                    for i in range(4):
                        after = (b, i + 2) if i < 2 else None if isinstance(b, int) and b == NB - 1 else (b + 1, i - 2)
                        if after:
                            load_block(sp, L, 0, *after, 0)
                        if L:
                            load_block(sp, L, 1, b, i, 0)
                            load_block(sp, L, 1, b, i, 1)
                        if after:
                            load_block(sp, L, 0, *after, 1)

                for i in range(L == 0, 2):
                    for half in range(2):
                        load_block(sp, L, 0, 0, i, half)
                each_sequence(sp, sequence)

            def store_tokens(T, out_p, out_s, g):
                for c in range(5):
                    n = 5 * T + c
                    for kv, done in ((0, tk_done), (1, tv_done)):
                        if not stored[n]:
                            continue
                        sp.wait_ge(done, n + 1)
                        if c < 4:
                            src = k_tok[n % 2][:, :] if kv == 0 else v_all[:, c, :]
                            v = out_p[0, 0].rearrange("t v h e -> t v (h e)")[:, kv, :]
                            if T == 0:
                                dst = v[P * c:P * c + P, :]
                            elif g == 0:
                                dst = v
                            elif g == 1:
                                dst = v.rearrange("(l r) f -> r l f", r=4)[c]
                            else:
                                dst = v.rearrange("(l c r) f -> c r l f", c=4, r=4)[c]
                        else:
                            src = k_tok[n % 2][0:NS, :] if kv == 0 else v_s[0:NS, g, :]
                            v = out_s[0].rearrange("b t v h e -> b t v (h e)")
                            dst = v[:, v.shape[1] - TS:, kv, :]
                        sp.dma_start(dst, src).then_inc(kout[n % 2] if kv == 0 else vout, 16)

            w_ab, w_oa = a["w_in_ab"][0], a["w_out_ab"][0]
            unit(w_ab, 0, 0, 0, wait=False)
            unit(w_ab, 256, 1, 1, wait=False)
            for m, n in enumerate(("norm_mix_g", "norm_mlp_g")):
                sp.dma_start(gain_rows[16 * m:16 * m + 16, :],
                             a[n].rearrange("l (k p) -> (l k) p", p=P)).then_inc(s_gain, 16)
            sp.dma_start(gain_rows[32:40, :], a["norm_out_g"].rearrange("(k p) -> k p", p=P)).then_inc(s_gain, 16)
            sp.dma_start(gain_rows[40:44, :], a["a_scale"][0].rearrange("(k p) -> k p", p=P)).then_inc(s_gain, 16)
            sp.dma_start(gain_rows[44:56, :], a["c_conv_w"][0].rearrange("j (k p) -> (j k) p", p=P)).then_inc(s_gain, 16)
            sp.dma_start(gain_rows[56:57, :], a["b_subln_g"]).then_inc(s_gain, 16)
            sp.dma_start(lam_in[:, :], a["b_lam"][0].rearrange("a d -> (a d)").partition_broadcast(P)).then_inc(s_lam, 16)
            sp.dma_start(hist_tok[0:120, :], a["state_a_pool"][0].rearrange("b t c -> (b t) c")).then_inc(s_hist, 16)
            sp.dma_start(a_mix[:, :].rearrange("p (g d) -> p g d", g=4),
                         a["a_mix"][0].rearrange("g c d -> c g d")).then_inc(s_hist, 16)
            sp.dma_start(pages[0:1, :], a["page_table"].rearrange("(o b) n -> o (b n)", o=1)).then_inc(s_page, 16)
            sp.wait_ge(s_page, 16)
            load_block(sp, 0, 0, 0, 0, 0)
            load_block(sp, 0, 0, 0, 0, 1)
            matrix(w_ab, T_AB, 16, first=1)
            unit(w_oa, 0, T_OA // 2, 0)
            unit(w_oa, 256, T_OA // 2 + 1, 1)
            sp.wait_ge(rows_done, 1)
            sp.dma_start(a["new_pool_prompt"][0, 0], e2[0][49:64, :]).then_inc(rows_out, 16)
            sp.dma_start(a["new_pool_sample"][0][:, 7:15, :], e2[0][NS:P, :]).then_inc(rows_out, 16)
            store_tokens(0, a["new_bkv_prompt"], a["new_bkv_sample"], 0)
            sp.wait_ge(tile_done, T_AB + 16)
            cache_blocks(0)
            unit(w_oa, 512, T_OA // 2 + 2, 0)
            unit(w_oa, 768, T_OA // 2 + 3, 1)
            mlp_weights(0, T_M0)
            w_cd, w_oc = a["w_in_cd"][0], a["w_out_cd"][0]
            unit(w_cd, 0, T_CD // 2, 0)
            unit(w_cd, 256, T_CD // 2 + 1, 1)
            sp.wait_ge(b_ready, 8 + 32)
            sp.dma_start(conv_tok[0:16, :], a["state_c_conv"][0].rearrange("b t c -> (b t) c")).then_inc(s_hist, 16)
            for g, (first, end) in enumerate(((1, 7), (7, 10), (10, 12))):
                with sp.Fori(first, end) as i:
                    for s in range(2):
                        unit(w_cd, i * 512 + 256 * s, i * 2 + T_CD // 2 + s, s)
                if g == 0:
                    sp.wait_ge(rows_done, 2)
                    sp.dma_start(a["new_conv_prompt"][0, 0], e2[0][NS - 2:NS, :]).then_inc(rows_out, 16)
                    for j in range(2):
                        sp.dma_start(a["new_conv_sample"][0][:, j, :], e2[0][NS + 6 + j:P:8, :]).then_inc(rows_out, 16)
                store_tokens(1 + g, a[f"new_d{g}_prompt"], a[f"new_d{g}_sample"], g)
            sp.wait_ge(tile_done, T_CD + 48)
            cache_blocks(1)
            sp.wait_ge(SS[1]["fin"], 1)
            unit(w_oc, 0, T_OC // 2, 0)
            unit(w_oc, 256, T_OC // 2 + 1, 1)
            unit(w_oc, 512, T_OC // 2 + 2, 0)
            unit(w_oc, 768, T_OC // 2 + 3, 1)
            mlp_weights(1, T_M1)

            for t in range(5):
                sp.wait_ge(yt_done, t + 1)
                if t < 4:
                    sp.dma_start(a["y_prompt"][0, P * t:P * t + P, :], y_tok[:, t, :]).then_inc(outs[2], 16)
                else:
                    sp.dma_start(a["y_sample"].rearrange("b t d -> (b t) d"), y_tok[0:NS, t, :]).then_inc(outs[2], 16)
            sp.wait_ge(outs[2], 80)
            sp.wait_ge(rows_out, 80)
            sp.wait_ge(vout, 16 * V_STORES[3])
            for i in range(2):
                sp.wait_ge(kout[i], 16 * K_STORES[i])

        @block.tensor
        def _(pe):
            def dense(group, n_groups, m_hi, m_lo, ready, ready_base, hook=None, peel=False):

                def four(G, first):
                    for q in range(4):
                        s = q % 2
                        pe.wait_ge(wlo_ready, G * 4 + (q + 1))
                        pe.wait_ge(acc_free, G * 4 + (q + 1))
                        for k in range(KT_N):
                            if first and q == 0:
                                pe.wait_ge(ready, ready_base + (k + 1))
                            for n, (w, m) in enumerate(((whi_v, m_hi), (whi_v, m_lo), (wlo_v, m_hi))):
                                for h in range(2):
                                    last = pe.matmul(acc_h[s][:, h, :], w[s][:, k, :], m[:, k, NH * h:NH * h + NH],
                                                     start=(k == 0 and n == 0), stop=(k == KT_N - 1 and n == 2))
                        last.then_inc(tile_done, 1)
                        if hook and first and q == 0:
                            hook()

                done = 0
                if peel or n_groups == 1:
                    four(group(0), True)
                    done = 1
                if n_groups - done == 1:
                    four(group(done), done == 0)
                elif n_groups > done:
                    with pe.Fori(done, n_groups) as i:
                        four(group(i), done == 0)

            def mean_square(f):
                def go():
                    pe.wait_ge(sqs_done, 8 * (f + 1))
                    for h in range(2):
                        last = pe.matmul(halves[2][:, h, :], ones, sqsum[:, NH * h:NH * h + NH], start=True, stop=True)
                    last.then_inc(ms_ready, 1)
                return go

            def mlp(L, t0):
                G0, fa, fb = t0 // 4, 8 * (1 + 2 * L), (8, 48)[L]
                dense(lambda i: i + G0, 2, ahk, alk, a_ready, fa, hook=mean_square(1 + 2 * L), peel=True)
                dense(lambda i: i + (G0 + 2), 2, bhk, blk, b_ready, fb)
                with pe.Fori(1, 4) as c:
                    dense(lambda i: c * 4 + (i + G0), 2, ahk, alk, a_ready, fa)
                    dense(lambda i: c * 4 + (i + (G0 + 2)), 2, bhk, blk, b_ready, c * 8 + fb)

            def token_major(T, kb, g):
                for c in range(5):
                    for kv, (ps, done, bk) in enumerate(((tk_ps, tk_done, bank[6]), (tv_ps, tv_done, bank[7]))):
                        if T or c:
                            pe.wait_ge(done, 5 * T + c)
                        rows = P if c < 4 else NS
                        for i in range(4):
                            tile = kb + 4 * kv + i
                            src = proj_cols(pk[:, tile, 0:SEQ], g, c) if c < 4 else pk[:, tile, SEQ:N]
                            last = pe.transpose(bk[0:rows, P * i:P * i + P], src, ident)
                        last.then_inc(ps, 1)

            def rows_of(tile0):
                for i in range(4):
                    last = pe.transpose(bank[7][:, P * i:P * i + P], pk[:, tile0 + i, N - P:N], ident)
                last.then_inc(rows_ps, 1)

            def sample_attention(L, pt, other_work):
                B, S = BLK[L], SS[L]

                def keys(b, i, pages):
                    for p in pages[:max(0, B["pages"][i] - pages[0])]:
                        if p % 2 == 0:
                            pe.wait_ge(S[f"k{i % 2}{p // 2}"], loaded(L, b, i, p // 2))
                        if p % 2 == 0:
                            at_least(pe, S["kt_a"], b * B["pa"] + (2 * i + p // 2))
                        else:
                            at_least(pe, S["kt_d"], b * B["pd"] + (2 * i + p // 2))
                        for t in range(4):
                            last = pe.transpose(bank[p % 2][:, P * t:P * t + P],
                                                kring_v[L][i % 2][:, p, P * t:P * t + P], ident)
                        last.then_inc(S["kt_ps"], 1)

                def scores(b, i):
                    if i == 0:
                        pe.wait_ge(S["q"], b * 2 + 2)
                    sb = SCORES
                    if i < 4:
                        np_, g = B["pages"][i], B["groups"][i]
                        kt = kt_sa[L][i % 2]
                        pe.wait_ge(S["kt_a"], b * B["pa"] + (2 * i + (np_ + 1) // 2))
                        if np_ > 1:
                            pe.wait_ge(S["kt_d"], b * B["pd"] + (2 * i + np_ // 2))
                        for t in range(4):
                            last = pe.matmul(sb[32 * t:32 * t + 32, 0:P * np_], staged[L][b % 2][:, g, t, :],
                                             kt[:, t, 0:np_, :], start=True, stop=True)
                    else:
                        for g in range(B["new"]):
                            for t in range(4):
                                last = pe.matmul(sb[32 * t:32 * t + 32, NS * g:NS * g + NS],
                                                 staged[L][b % 2][:, g, t, :], k_s[:, g, t, :], start=True, stop=True)
                    last.then_inc(S["s"], 1)

                def weights(b, i):
                    pe.wait_ge(S["e"], b * 5 + (i + 1))
                    n, w = (B["pages"][i], P) if i < 4 else (B["new"], NS)
                    for p in range(n):
                        last = pe.transpose(WEIGHTS[:, P * p:P * p + P],
                                            e_sa[L][i % 2][:, w * p:w * p + P], ident)
                    last.then_inc(S["pt_ps"], 1)

                def values(b, i):
                    if i == 4:
                        pe.wait_ge(tv_done, (5, 20)[L])
                    pe.wait_ge(S["pt"], b * 5 + (i + 1))
                    at_least(pe, S["o"], b * 5 + i)
                    ob = OUTPUT
                    n, w = (B["pages"][i], P) if i < 4 else (B["new"], NS)
                    for p in range(n):
                        if i < 4 and p % 2 == 0:
                            pe.wait_ge(S[f"v{i % 2}{p // 2}"], loaded(L, b, i, p // 2))
                        v = vring_v[L][i % 2][:, p, :] if i < 4 else v_s[0:NS, p, :]
                        for t in range(4):
                            last = pe.matmul(ob[32 * t:32 * t + 32, 0:P],
                                             pt[i % 2][0:w, P * p + 32 * t:P * p + 32 * t + 32],
                                             v[:, P * t:P * t + P], start=(p == 0), stop=(p == n - 1))
                    last.then_inc(S["o_ps"], 1)

                def sequence(b):
                    for i in range(5):
                        scores(b, i)
                        keys_beside(b, i, keys, (0, 1))
                        if i:
                            values(b, i - 1)
                        elif not isinstance(b, int) or b:
                            values(b - 1, 4)
                        keys_beside(b, i, keys, (2, 3))
                        other_work(b, i)
                        weights(b, i)

                keys(0, 0, (0, 1, 2, 3))
                for b in range(NB):
                    sequence(b)
                values(NB - 1, 4)

            def sample_finish(L, orun, stat):
                S = SS[L]
                comb = stat[:, S_COMB:S_COMB + 256].rearrange("p (b c) -> p b c", b=NB)
                pe.wait_ge(S["fin"], 1)
                for b in range(NB):
                    last = pe.matmul(bank[0][:, 32 * b:32 * b + 32], orun[:, P * b:P * b + P], comb[:, b, :],
                                     start=True, stop=True)
                last.then_inc(S["fin_ps"], 1)

            pe.wait_ge(s_const, 16)
            pe.wait_ge(s_gain, 96)
            pe.transpose(bank[7][:, 0:57], gain_rows[0:57, :], ident[0:57, 0:57]).then_inc(gain_ps, 1)
            pe.wait_ge(s_x, 32)
            for k in range(KT_N):
                if k >= 2:
                    pe.wait_ge(x_ready, k - 1)
                for t in range(5):
                    rows = P if t < 4 else NS
                    last = pe.transpose(acc[k % 2][:, P * t:P * t + rows], x_tok[0:rows, t, P * k:P * k + P],
                                        ident[0:rows, 0:rows])
                last.then_inc(xt_ps, 1)

            pe.wait_ge(x_ready, 8)
            dense(lambda i: i, 1, ahk, alk, a_ready, 0, hook=mean_square(0), peel=True)
            pe.wait_ge(s_hist, 32)
            for i in range(4):
                last = pe.transpose(bank[6][:, P * i:P * i + 120], hist_tok[0:120, P * i:P * i + P],
                                    ident[0:120, 0:120])
            last.then_inc(hist_ps, 1)
            pe.wait_ge(acc_free, 2 + T_AB + 4)
            rows_of(0)
            dense(lambda i: i + 1, 3, ahk, alk, a_ready, 0)
            pe.wait_ge(acc_free, 2 + T_AB + 16)
            pe.wait_ge(hist_done, 1)
            pe.wait_ge(rows_done, 1)
            token_major(0, 8, 0)

            def prompt_stage(s):
                if s < 16:
                    h, qt = s // 4, s % 4
                    if s >= 1:
                        pe.wait_ge(p0_e, s)
                    for m in range(2):
                        last = pe.matmul(P0_SCORES[:, 512 * m:512 * m + P * (qt + 1)],
                                         pk[64 * m:64 * m + 64, 4 + h, P * qt:P * qt + P],
                                         pk[64 * m:64 * m + 64, 8 + h, 0:P * (qt + 1)], start=True, stop=True)
                    last.then_inc(p0_s, 1)
                if s >= 1:
                    n = s - 1
                    qt = n % 4
                    pe.wait_ge(p0_a, n + 1)
                    if n >= 1:
                        pe.wait_ge(p0_o, n)
                    for kb in range(qt + 1):
                        last = pe.transpose(P0_WEIGHTS[:, P * kb:P * kb + P], e4[n % 2][0][:, P * kb:P * kb + P], ident)
                    last.then_inc(p0_t, 1)

            def prompt_product(n):
                h, qt = n // 4, n % 4
                pe.wait_ge(p0_at, n + 1)
                for kb in range(qt + 1):
                    last = pe.matmul(P0_OUTPUT, v_all[:, kb, P * h:P * h + P], pt_p0[n % 2][:, P * kb:P * kb + P],
                                     start=(kb == 0), stop=(kb == qt))
                last.then_inc(p0_pv, 1)

            def prompt_work(b, i):
                beside(b, i, 1, prompt_stage, 16)
                beside(b, i, 4, prompt_product, 15)

            pe.wait_ge(q_scaled, 1)
            pe.wait_ge(tk_done, 5)
            pe.wait_ge(tv_done, 5)
            sample_attention(0, pt_l0, prompt_work)
            sample_finish(0, orun0, samp[0])

            for g in range(4):
                pe.wait_ge(pm_ready, g + 1)
                pe.wait_ge(SS[0]["fin_d"], 1)
                if g >= 2:
                    pe.wait_ge(b_ready, g - 1)
                for h in range(2):
                    last = pe.matmul(acc_h[g % 2][:, h, :], a_mix[:, P * g:P * g + P],
                                     pk[:, g, NH * h:NH * h + NH], start=True, stop=True)
                last.then_inc(mix_ps, 1)

            for h in range(4):
                pe.wait_ge(sub_sq, h + 1)
                if h == 0:
                    pe.wait_ge(b_ready, 4)
                elif h >= 2:
                    pe.wait_ge(sub_v, h - 1)
                for f in range(2):
                    last = pe.matmul(halves[1 + h % 2][:, f, :], ones, zbuf[:, N * (h % 2) + NH * f:N * (h % 2) + NH * f + NH],
                                     start=True, stop=True)
                last.then_inc(sub_ms, 1)
            pe.wait_ge(sub_v, 4)
            pe.wait_ge(SS[0]["fin_d"], 1)
            dense(lambda i: i + T_OA // 4, 2, bhk, blk, b_ready, 0)
            mlp(0, T_M0)

            dense(lambda i: i + T_CD // 4, 3, ahk, alk, a_ready, 16, hook=mean_square(2), peel=True)
            pe.wait_ge(acc_free, 2 + T_CD + 12)
            pe.wait_ge(s_hist, 48)
            for i in range(4):
                last = pe.transpose(bank[6][:, 16 * i:16 * i + 16], conv_tok[0:16, P * i:P * i + P], ident[0:16, 0:16])
            last.then_inc(hist_ps, 1)
            pe.wait_ge(pm_ready, 5)
            rows_of(4)

            def group_scores(g, it, bk):
                _, c, par, kc, _ = items1[it]
                for t in range(4):
                    r = 64 * par
                    last = pe.matmul(bk[:, P * t:P * t + P], proj_cols(pk[r:r + 64, t, 0:SEQ], g, c),
                                     proj_cols(pk[r:r + 64, 4 + t, 0:SEQ], g, kc), start=True, stop=True)
                last.then_inc(p1_s, 1)

            def group_weights(it, bk):
                pe.wait_ge(p1_e, it + 1)
                for t in range(4):
                    last = pe.transpose(bk[:, P * t:P * t + P], e2[it % 2][:, P * t:P * t + P], ident)
                last.then_inc(p1_t, 1)

            def group_product(g, n, bk):
                c, par, its = units1[g][n]
                pe.wait_ge(p1_pt, its[-1] + 1)
                for t in range(4):
                    head, r = 2 * t + par, 64 * par
                    for k, it in enumerate(its):
                        last = pe.matmul(bk[r:r + 64, P * t:P * t + P], v_all[:, items1[it][3], 64 * head:64 * head + 64],
                                         pt_l1[it % 2][:, P * t:P * t + P], start=(k == 0), stop=(k == len(its) - 1))
                last.then_inc(p1_pv, 1)

            for g in range(3):
                dense(lambda i: i + (T_CD // 4 + 3 + 3 * g), 3, ahk, alk, a_ready, 16)
                pe.wait_ge(acc_free, 2 + T_CD + 12 * (g + 2))
                if g == 0:
                    pe.wait_ge(hist_done, 2)
                    pe.wait_ge(rows_done, 2)
                else:
                    pe.wait_ge(p1_o, 4 * g)
                token_major(1 + g, 4, g)
                pe.wait_ge(q_scaled, 2 + g)
                for s in range(8 + 2 if g < 2 else 0):
                    if s < 8:
                        for it in units1[g][s][2]:
                            if it >= 4:
                                pe.wait_ge(p1_e, it - 3)
                            group_scores(g, it, bank[it % 4])
                    if s >= 2:
                        u = 8 * g + s - 2
                        if s == 2:
                            pe.wait_ge(tk_done, 5 * (2 + g))
                            pe.wait_ge(tv_done, 5 * (2 + g))
                        if u >= 4 and u % 2 == 0:
                            pe.wait_ge(p1_o, u // 2 - 1)
                        group_product(g, s - 2, bank[6 + u // 2 % 2])
                    if 1 <= s <= 8:
                        for it in units1[g][s - 1][2]:
                            if it >= 2:
                                pe.wait_ge(p1_pt, it - 1)
                            group_weights(it, bank[4 + it % 2])

            def prompt_stage(s):
                if s < 8:
                    it = units1[2][s][2][0]
                    pe.wait_ge(p1_e, it)
                    group_scores(2, it, P1_SCORES)
                if s >= 1:
                    it = units1[2][s - 1][2][0]
                    pe.wait_ge(p1_pt, it)
                    group_weights(it, P1_WEIGHTS)

            def prompt_product(n):
                if n % 2 == 0:
                    pe.wait_ge(p1_o, 8 + n // 2)
                group_product(2, n, P1_OUTPUT)

            def statistics(n):
                if n == 0:
                    pe.wait_ge(p1_o, 12)
                    pe.wait_ge(cb_t, 1)
                else:
                    pe.wait_ge(cb_v, 1)
                for g in range(3):
                    for c in range(4):
                        last = pe.transpose(CB_BANKS[g][0:8, P * c:P * c + P], (neg1, sum1)[n][:, g, c, :], ident)
                last.then_inc(cb_d, 1)

            def factors(t):
                pe.wait_ge(cb_c, 1)
                if t:
                    pe.wait_ge(cb_u, t)
                for g in range(3):
                    last = pe.matmul(CB_BANKS[g][:, :], cc("sel8")[0:8, P * t:P * t + P], nm[g][0:8, :],
                                     start=True, stop=True)
                last.then_inc(cb_ps, 1)

            def prompt_work(b, i):
                beside(b, i, 1, prompt_stage, 8)
                beside(b, i, 4, prompt_product, 7)
                beside(b, i, 20, statistics, 1)
                beside(b, i, 27, factors, 3)

            pe.wait_ge(tk_done, 20)
            pe.wait_ge(tv_done, 20)
            pe.wait_ge(p1_e, units1[2][0][2][0])
            pe.wait_ge(p1_pt, units1[2][0][2][0])
            sample_attention(1, pt_s1, prompt_work)
            pe.wait_ge(cb_u, 4)
            sample_finish(1, orun1, samp[1])
            pe.wait_ge(SS[1]["fin_d"], 1)
            dense(lambda i: i + T_OC // 4, 2, bhk, blk, b_ready, 40)
            mlp(1, T_M1)

            mean_square(4)()
            for t in range(5):
                rows = P if t < 4 else NS
                pe.wait_ge(y_ready, 8)
                if t >= 2:
                    pe.wait_ge(yt_done, t - 1)
                for k in range(KT_N):
                    last = pe.transpose(acc[t % 2][0:rows, P * k:P * k + P], y_feat[:, N * k + P * t:N * k + P * t + rows],
                                        ident)
                last.then_inc(yt_ps, 1)

        @block.vector
        def _(dve):
            steps = Tally()

            def link(ins):
                ins.then_inc(dve_step, 1)
                dve.wait_ge(dve_step, steps.add())

            def split_lo(G, q):
                j = q % 2
                dve.wait_ge(whi_ready, G * 4 + (q + 1))
                dve.tensor_tensor(wlo_v[j], raw_v[q // 2][:, :, j, :], whi_v[j].bitcast(F32),
                                  ALU.subtract).then_inc(wlo_ready, 1)

            def dense(group, n_groups, evac, post=None, peel=False, hook=None, static=False, last=False):
                def four(G, i):
                    for q in range(4):
                        dve.wait_ge(tile_done, G * 4 + (q + 1))
                        if hook and q == 0 and isinstance(i, int) and i == 0:
                            hook()
                        evac(G, i, q)
                        if not (last and q >= 2 and i == n_groups - 1):
                            split_lo(*((G, q + 2) if q < 2 else (G + 1, q - 2)))
                        if post:
                            post(G, i, q)
                done = 0
                while done < n_groups and (static or n_groups - done == 1 or (peel and done == 0)):
                    four(group(done), done)
                    done += 1
                if done < n_groups:
                    with dve.Fori(done, n_groups) as i:
                        four(group(i), i)

            def rms(f):
                def go():
                    dve.wait_ge(ms_ready, f + 1)
                    dve.tensor_scalar(r_h, halves[2], 1.0 / D, EPS, ALU.mult, ALU.add).then_inc(v_ready, 1)
                    dve.wait_ge(sqrt_ready, f + 1)
                    link(dve.reciprocal(rnorm[:, :], rnorm[:, :]))
                return go

            def to_proj(group0=0):
                def evac(G, i, q):
                    dst = proj[:, ds(i * (4 * N) + (4 * group0 + q) * N, N)].rearrange("p (h c) -> p h c", h=2)
                    dve.tensor_tensor(dst, acc_h[q % 2], r_h, ALU.mult).then_inc(acc_free, 1)
                return evac

            def to_proj_streams(group0=0):
                L0 = NH // 16

                def evac(G, i, q):
                    dst = proj[:, ds(i * (4 * N) + (4 * group0 + q) * N, N)]
                    dp = dst[:, 0:SEQ].rearrange("p (r l) -> p r l", r=16)
                    rl = lambda v: v.rearrange("p (l r) -> p r l", r=16)
                    a0, a1 = acc_h[q % 2][:, 0, :], acc_h[q % 2][:, 1, :]
                    dve.tensor_tensor(dp[:, :, 0:L0], rl(a0), rl(rnorm[:, 0:NH]), ALU.mult)
                    dve.tensor_tensor(dp[:, :, L0:32], rl(a1[:, 0:SEQ - NH]), rl(rnorm[:, NH:SEQ]), ALU.mult)
                    dve.tensor_tensor(dst[:, SEQ:N], a1[:, SEQ - NH:NH], rnorm[:, SEQ:N], ALU.mult).then_inc(acc_free, 1)
                return evac

            def up(G, i, q):
                j = q % 2
                z = zbuf[:, N * j:N * j + N]
                dve.tensor_tensor(z.rearrange("p (h c) -> p h c", h=2), acc_h[j], r_h, ALU.mult).then_inc(acc_free, 1)
                dve.wait_ge(acc_free, G * 4 + (q + 3))
                dve.scalar_tensor_tensor(out=sqbuf[:, N * j:N * j + N], in0=z, scalar=0.0, in1=z, op0=ALU.max,
                                         op1=ALU.mult).then_inc(sq_up, 1)

            def up_post(b0):
                def post(G, i, q):
                    dve.wait_ge(bhi_ready, b0 + i * 4 + (q + 1))
                    at_ = ds(i * (4 * N) + q * N, N)
                    dve.tensor_tensor(b_lo[:, at_], sqbuf[:, N * (q % 2):N * (q % 2) + N], b_hi[:, at_].bitcast(F32),
                                      ALU.subtract).then_inc(b_ready, 1)
                return post

            def down(G, i, q):
                xt = x[:, ds(i * (4 * N) + q * N, N)].rearrange("p (h c) -> p h c", h=2)
                dve.tensor_tensor(xt, xt, acc_h[q % 2], ALU.add).then_inc(acc_free, 1)

            def fin_post(f, gcol):
                def post(G, i, q):
                    k = 4 * i + q
                    dve.wait_ge(ahi_ready, 8 * f + k + 1)
                    dve.scalar_tensor_tensor(out=alk[:, k, :], in0=xk[:, k, :], scalar=gains[:, gcol + k:gcol + k + 1],
                                             in1=ahk[:, k, :].bitcast(F32), op0=ALU.mult,
                                             op1=ALU.subtract).then_inc(a_ready, 1)
                return post

            def mlp(L, t0):
                G0, fb = t0 // 4, (8, 48)[L]
                dense(lambda i: i + G0, 2, up, up_post(fb), peel=True, hook=rms(1 + 2 * L))
                dense(lambda i: i + (G0 + 2), 2, down)
                with dve.Fori(1, 3) as c:
                    dense(lambda i: c * 4 + (i + G0), 2, up, up_post(c * 8 + fb))
                    dense(lambda i: c * 4 + (i + (G0 + 2)), 2, down)
                dense(lambda i: i + (G0 + 12), 2, up, up_post(24 + fb))
                if L == 0:
                    dense(lambda i: i + (G0 + 14), 2, down, fin_post(2, G_MIX + 8), static=True)
                else:
                    dense(lambda i: i + (G0 + 14), 2, down, static=True, last=True)

            def token_major(T, g):
                for c in range(5):
                    dve.wait_ge(tv_ps, 5 * T + c + 1)
                    if c == 0 and T:
                        dve.wait_ge(vout, 16 * V_STORES[T - 1])
                    dst, rows = (v_all[:, c, :], P) if c < 4 else (v_s[0:NS, g, :], NS)
                    dve.tensor_copy(dst, bank[7][0:rows, :]).then_inc(tv_done, 1)

            def sample_attention(L, orun, stat, other_work):
                B, S = BLK[L], SS[L]
                neg = lambda i: stat[:, S_NEG + i:S_NEG + i + 1]
                tmp = stat[:, S_TMP:S_TMP + 1]
                ob, run = stat[:, 300:428], stat[:, 510:511]

                def keys(b, i, pages):
                    for p in pages:
                        if p >= B["pages"][i]:
                            continue
                        dve.wait_ge(S["kt_ps"], b * B["pn"] + (4 * i + p + 1))
                        dve.tensor_copy(kt_sa[L][i % 2][:, :, p, :], bank[1].rearrange("p (i n) -> p i n", i=4)
                                        ).then_inc(S["kt_d"], 1)

                def maximum(b, i):
                    dve.wait_ge(S["s"], b * 5 + (i + 1))
                    sb = SCORES
                    w = P * B["pages"][i] if i < 4 else NS * B["new"]
                    if i < 4 and B["mask"][i]:
                        m = B["mask"][i]
                        sv = sb[:, 0:w].rearrange("p (g n) -> p g n", n=P)
                        if m == "g0m":
                            link(dve.tensor_tensor(sb[:, 0:8], sb[:, 0:8], cc("g0m"), ALU.add))
                        else:
                            rm = {"rm2a": cc("rm2")[:, 0:4], "rm2b": cc("rm2")[:, 4:8], "rm1": cc("rm1")}[m]
                            link(dve.tensor_tensor(sv, sv, rm.unsqueeze(2).broadcast_to([P, 4, P]), ALU.add))
                            if m == "rm1":
                                link(dve.tensor_tensor(sv[:, :, 0], sv[:, :, 0], cc("k01"), ALU.add))
                    if i == 4:
                        sv = sb[:, 0:w].rearrange("p (g n) -> p g n", n=NS)
                        mv = cc("selfm").rearrange("p (g n) -> p g n", g=3)
                        link(dve.tensor_tensor(sv, sv, mv[:, 0:B["new"], ds(b * (-8) + 56, NS)], ALU.add))
                    if i == 0:
                        dve.tensor_reduce(neg(0), sb[:, 0:w], AX.X, ALU.max, negate=True).then_inc(S["neg"], 1)
                    else:
                        link(dve.tensor_reduce(tmp, sb[:, 0:w], AX.X, ALU.max, negate=True))
                        dve.wait_ge(S["neg"], b * 5 + i)
                        dve.tensor_tensor(neg(i), tmp, neg(i - 1), ALU.min).then_inc(S["neg"], 1)

                def output(b, i):
                    al = stat[:, S_ALPHA + i:S_ALPHA + i + 1]
                    su = stat[:, S_SUM + i:S_SUM + i + 1]
                    dve.wait_ge(S["o_ps"], b * 5 + (i + 1))
                    pv = OUTPUT
                    rdst = run if i < 4 else stat[:, ds(b + S_RUN, 1)]
                    odst = ob if i < 4 else orun[:, ds(b * P, P)]
                    at_least(dve, S["o"], b * 5 + i)
                    if i == 0:
                        link(dve.tensor_copy(run, su))
                        dve.tensor_copy(ob, pv).then_inc(S["o"], 1)
                    else:
                        link(dve.scalar_tensor_tensor(out=rdst, in0=run, scalar=al, in1=su, op0=ALU.mult, op1=ALU.add))
                        dve.scalar_tensor_tensor(out=odst, in0=ob, scalar=al, in1=pv, op0=ALU.mult,
                                                 op1=ALU.add).then_inc(S["o"], 1)

                def sequence(b):
                    for i in range(5):
                        maximum(b, i)
                        keys_beside(b, i, keys, (1,))
                        if i:
                            output(b, i - 1)
                        elif not isinstance(b, int) or b:
                            output(b - 1, 4)
                        keys_beside(b, i, keys, (3,))
                        other_work(b, i)

                keys(0, 0, (1, 3))
                for b in range(NB):
                    sequence(b)
                output(NB - 1, 4)

            def sample_finish(L, orun, stat, o_feat):
                S = SS[L]
                rec = stat[:, S_REC:S_REC + 8]
                comb = stat[:, S_COMB:S_COMB + 256].rearrange("p (b c) -> p b c", b=NB)
                dve.wait_ge(S["o"], 5 * NB)
                link(dve.reciprocal(rec, stat[:, S_RUN:S_RUN + 8]))
                if L == 0:
                    link(dve.tensor_scalar(rec, rec, neglam[:, 1:2], None, ALU.mult))
                else:
                    ov = orun[:, :].rearrange("p (b e) -> p b e", b=NB)
                    for hf in range(2):
                        o2 = ov[:, :, 64 * hf:64 * hf + 64]
                        link(dve.tensor_scalar(o2, o2, cc("halfm")[:, hf:hf + 1], None, ALU.mult))
                dve.tensor_tensor(comb, cc("sel").unsqueeze(1).broadcast_to([P, NB, 32]),
                                  rec.unsqueeze(2).broadcast_to([P, NB, 32]), ALU.mult).then_inc(S["fin"], 1)
                dve.wait_ge(S["fin_ps"], 1)
                for t in range(4):
                    last = dve.tensor_copy(o_feat[:, t, SEQ:N].rearrange("p (b t) -> p b t", b=NB),
                                           bank[0][:, 0:256].rearrange("p (b i t) -> p b i t", b=NB, i=4)[:, :, t, :])
                last.then_inc(S["fin_d"], 1)

            dve.wait_ge(gain_ps, 1)
            dve.tensor_copy(gains[:, 0:57], bank[7][:, 0:57]).then_inc(gain_ready, 1)
            dve.wait_ge(s_const, 16)
            dve.tensor_scalar(dummy[:, :], cc("ones")[:, 0:1], 1.0, None, ALU.mult).then_inc(acc_free, 2)
            split_lo(0, 0)
            split_lo(0, 1)
            for k in range(KT_N + 1):
                if k < KT_N:
                    dve.wait_ge(xt_ps, k + 1)
                    dve.tensor_copy(xk[:, k, :], acc[k % 2][:, 0:N]).then_inc(x_ready, 1)
                if k >= 1:
                    fin_post(0, G_MIX)(0, 0, k - 1)

            dve.wait_ge(s_lam, 16)
            lv = lam_in[:, :].rearrange("p (m s d) -> p m s d", m=2, s=2)
            lt = lam_t[:, 0:128].rearrange("p (m d) -> p m d", m=2)
            link(dve.tensor_tensor(lt, lv[:, :, 0, :], lv[:, :, 1, :], ALU.mult))
            dve.tensor_reduce(lam_t[:, 128:130], lt, AX.X, ALU.add).then_inc(lam_d, 1)
            dve.wait_ge(lam_e, 1)
            link(dve.tensor_tensor(neglam[:, 0:1], lam_t[:, 131:132], lam_t[:, 130:131], ALU.subtract))
            link(dve.tensor_scalar(neglam[:, 0:1], neglam[:, 0:1], -LAM_INIT, None, ALU.add))
            link(dve.scalar_tensor_tensor(out=neglam[:, 1:2], in0=cc("m01")[:, 1:2], scalar=neglam[:, 0:1],
                                          in1=cc("m01")[:, 0:1], op0=ALU.mult, op1=ALU.add))

            dense(lambda i: i, 1, to_proj(), peel=True, hook=rms(0))
            dve.wait_ge(hist_ps, 1)
            dve.tensor_copy(hist_f.rearrange("p g b c -> p g (b c)"),
                            bank[6].rearrange("p (g w) -> p g w", g=4)[:, :, 0:120]).then_inc(hist_done, 1)
            dve.wait_ge(rows_ps, 1)
            dve.tensor_copy(e2[0][:, :], bank[7]).then_inc(rows_done, 1)
            dense(lambda i: i + 1, 3, to_proj(1))
            dve.wait_ge(acc_free, 2 + T_AB + 16)
            dve.tensor_scalar(proj[:, 4 * N:8 * N], proj[:, 4 * N:8 * N], 0.125, None, ALU.mult).then_inc(q_scaled, 1)
            token_major(0, 0)

            def prompt_stage(s):
                qt, u = s % 4, s % 2
                nk = P * (qt + 1)
                dve.wait_ge(p0_s, s + 1)
                sv = P0_SCORES[:, :].rearrange("p (m n) -> p m n", m=2)
                diag = sv[:, :, P * qt:P * qt + P]
                link(dve.tensor_tensor(diag, diag, cc("causal").unsqueeze(1).broadcast_to([P, 2, P]), ALU.add))
                dve.tensor_reduce(neg0[:, u, :], sv[:, :, 0:nk], AX.X, ALU.max, negate=True).then_inc(p0_m, 1)

            def prompt_output(n):
                h, qt = n // 4, n % 4
                dve.wait_ge(p0_pv, n + 1)
                dve.tensor_copy(o_feat0[:, N * h + P * qt:N * h + P * qt + P], P0_OUTPUT).then_inc(p0_o, 1)

            def prompt_combine(n):
                u, nk = n % 2, P * (n % 4 + 1)
                dve.wait_ge(p0_e, n + 1)
                link(dve.reciprocal(rs0[:, u, :], sum0[:, u, :]))
                link(dve.tensor_scalar(rs0[:, u, 1:2], rs0[:, u, 1:2], neglam[:, 0:1], None, ALU.mult))
                e0, e1 = e4[u][0][:, 0:nk], e4[u][1][:, 0:nk]
                link(dve.tensor_scalar(e0, e0, rs0[:, u, 0:1], None, ALU.mult))
                dve.scalar_tensor_tensor(out=e0, in0=e1, scalar=rs0[:, u, 1:2], in1=e0, op0=ALU.mult,
                                         op1=ALU.add).then_inc(p0_a, 1)

            dve.wait_ge(q_scaled, 1)
            def prompt_work(b, i):
                beside(b, i, 1, prompt_stage, 15)
                beside(b, i, 2, prompt_combine, 15)
                beside(b, i, 4, prompt_output, 15)

            sample_attention(0, orun0, samp[0], prompt_work)
            of0 = tiles(o_feat0, 4)
            sample_finish(0, orun0, samp[0], of0)

            for g in range(4):
                dve.wait_ge(bhi_ready, g + 1)
                dve.scalar_tensor_tensor(out=blk[:, g, :].rearrange("p (h c) -> p h c", h=2), in0=acc_h[g % 2],
                                         scalar=gains[:, G_SCALE + g:G_SCALE + g + 1],
                                         in1=bhk[:, g, :].bitcast(F32).rearrange("p (h c) -> p h c", h=2),
                                         op0=ALU.mult, op1=ALU.subtract).then_inc(b_ready, 1)

            dve.wait_ge(p0_o, 16)
            for h in range(4):
                dve.wait_ge(sub_ms, h + 1)
                t1 = sqbuf[:, N * (h % 2):N * (h % 2) + N]
                t1h = t1.rearrange("p (h c) -> p h c", h=2)
                dve.tensor_scalar(t1h, halves[1 + h % 2], 1.0 / P, EPS, ALU.mult, ALU.add).then_inc(sub_v, 1)
                dve.wait_ge(sub_r, h + 1)
                link(dve.reciprocal(t1, t1))
                link(dve.scalar_tensor_tensor(out=t1, in0=of0[:, h, :], scalar=gains[:, G_SUBLN:G_SUBLN + 1], in1=t1,
                                              op0=ALU.mult, op1=ALU.mult))
                dve.tensor_scalar(t1, t1, 1.0 - LAM_INIT, None, ALU.mult).then_inc(sub_t, 1)
                dve.wait_ge(bhi_ready, 5 + h)
                dve.tensor_tensor(blk[:, 4 + h, :], t1, bhk[:, 4 + h, :].bitcast(F32), ALU.subtract).then_inc(b_ready, 1)

            dense(lambda i: i + T_OA // 4, 2, down, fin_post(1, G_MLP), static=True)
            mlp(0, T_M0)

            dense(lambda i: i + T_CD // 4, 3, to_proj(), peel=True, hook=rms(2))
            dve.wait_ge(acc_free, 2 + T_CD + 12)
            link(dve.tensor_tensor(proj[:, 4 * N:8 * N], proj[:, 4 * N:8 * N], proj[:, 8 * N:12 * N], ALU.mult))
            dve.wait_ge(hist_ps, 2)
            dve.tensor_copy(zext[:, :, :, 0:2], bank[6][:, 0:64].rearrange("p (k b c) -> p k b c", k=4, b=NB)
                            ).then_inc(hist_done, 1)
            dve.wait_ge(hist_done, 2)
            for k in range(4):
                link(dve.tensor_copy(zext[:, k, :, 2:10], pk[:, 4 + k, SEQ:N].rearrange("p (b c) -> p b c", b=NB)))
            dve.tensor_copy(dummy[:, :], cc("ones")[:, 0:1]).then_inc(pm_ready, 1)
            for k in range(4):
                w = [gains[:, G_CONV + 4 * j + k:G_CONV + 4 * j + k + 1] for j in range(3)]
                z, y = pk[:, 4 + k, :], cv[:, N * (k % 2):N * (k % 2) + N]
                ys = y[:, SEQ:N].rearrange("p (b c) -> p b c", b=NB)
                if k >= 2:
                    dve.wait_ge(b_ready, 40 + k - 1)
                link(dve.tensor_scalar(y, z, w[2], None, ALU.mult))
                for j in (1, 0):
                    d = 2 - j
                    dve.scalar_tensor_tensor(out=ys, in0=zext[:, k, :, j:j + 8], scalar=w[j], in1=ys, op0=ALU.mult,
                                             op1=ALU.add)
                    link(dve.scalar_tensor_tensor(out=y[:, d:SEQ], in0=z[:, 0:SEQ - d], scalar=w[j], in1=y[:, d:SEQ],
                                                  op0=ALU.mult, op1=ALU.add))
                dve.tensor_tensor(y, y, pk[:, k, :], ALU.mult).then_inc(sub_t, 1)
                dve.wait_ge(bhi_ready, 40 + k + 1)
                dve.tensor_tensor(blk[:, k, :], y, bhk[:, k, :].bitcast(F32), ALU.subtract).then_inc(b_ready, 1)
            dve.wait_ge(rows_ps, 2)
            dve.tensor_copy(e2[0][:, :], bank[7]).then_inc(rows_done, 1)

            def group_maximum(g, n, scores):
                c, par, its = units1[g][n]
                d = neg1[:, g, c, 4 * par:4 * par + 4]
                for k, it in enumerate(its):
                    dve.wait_ge(p1_s, it + 1)
                    sv = scores(it).rearrange("p (h n) -> p h n", h=4)
                    link(dve.tensor_tensor(sv, sv, cc(items1[it][4]).unsqueeze(1).broadcast_to([P, 4, P]), ALU.add))
                    ins = dve.tensor_reduce(d if k == 0 else negp[:, c, 4 * par:4 * par + 4], sv, AX.X, ALU.max,
                                            negate=True)
                    if len(its) == 1:
                        ins.then_inc(p1_m, 1)
                    else:
                        link(ins)
                if len(its) == 2:
                    dve.tensor_tensor(d, d, negp[:, c, 4 * par:4 * par + 4], ALU.min).then_inc(p1_m, 1)

            def group_output(g, n, bk):
                dve.wait_ge(p1_pv, 8 * g + n + 1)
                src = bk.rearrange("p (i n) -> p i n", i=4)
                og = tiles(o_g[g], 4)
                for i in range(4):
                    dst, sr = tok_cols(og[:, i, 0:SEQ], g, units1[g][n][0]), src[:, i, :]
                    if g == 2:
                        sr = sr.rearrange("p (r l) -> p r l", r=4)
                    last = dve.tensor_copy(dst, sr)
                last.then_inc(p1_o, 1)

            for g in range(3):
                if g:
                    dve.wait_ge(qs_saved, 2 * (g + 1))
                if g < 2:
                    dense(lambda i: i + (T_CD // 4 + 3 + 3 * g), 3, to_proj())
                else:
                    dense(lambda i: i + (T_CD // 4 + 9), 2, to_proj_streams())
                    dense(lambda i: i + (T_CD // 4 + 11), 1, to_proj_streams(2), last=True)
                dve.wait_ge(acc_free, 2 + T_CD + 12 * (g + 2))
                dve.tensor_scalar(proj[:, 0:4 * N], proj[:, 0:4 * N], 0.125, None, ALU.mult).then_inc(q_scaled, 1)
                token_major(1 + g, g)
                if g == 0:
                    dve.wait_ge(rows_out, 80)
                for s in range(8 + 2 if g < 2 else 0):
                    if s < 8:
                        group_maximum(g, s, lambda it: bank[it % 4])
                    if s >= 2 and s % 2:
                        group_output(g, s - 2, bank[6 + (8 * g + s - 2) // 2 % 2])

            low = e2[0][0:8, :]

            def total_sums():
                dve.wait_ge(p1_e, len(items1))
                s0 = sum1[:, 0, 1:4, :]
                dve.tensor_tensor(s0, s0, sump[:, 1:4, :], ALU.add).then_inc(cb_t, 1)

            def statistics(n):
                dve.wait_ge(cb_d, n + 1)
                if n == 0:
                    dve.wait_ge(p1_pv, 24)
                    dve.wait_ge(vout, 16 * V_STORES[3])
                    for i in range(2):
                        dve.wait_ge(kout[i], 16 * K_STORES[i])
                dst = (nm, sm)[n]
                for g in range(3):
                    src = CB_BANKS[g][0:8, :].rearrange("p (c n) -> p c n", c=4)
                    for c in range(4):
                        d, s_ = tok_cols(dst[g][0:8, :], g, c), src[:, c, :]
                        if g == 2:
                            s_ = s_.rearrange("p (r l) -> p r l", r=4)
                        last = dve.tensor_copy(d, s_)
                last.then_inc(cb_v, 1)

            def relative():
                dve.wait_ge(cb_v, 2)
                link(dve.tensor_tensor(low, nm[0][0:8, :], nm[1][0:8, :], ALU.min))
                link(dve.tensor_tensor(low, low, nm[2][0:8, :], ALU.min))
                for g in range(3):
                    last = dve.tensor_tensor(nm[g][0:8, :], low, nm[g][0:8, :], ALU.subtract)
                last.then_inc(cb_x, 1)

            def group_factors():
                dve.wait_ge(cb_e, 3)
                for g in range(3):
                    last = dve.tensor_tensor(sm[g][0:8, :], sm[g][0:8, :], nm[g][0:8, :], ALU.mult)
                link(last)
                link(dve.tensor_tensor(low, sm[0][0:8, :], sm[1][0:8, :], ALU.add))
                link(dve.tensor_tensor(low, low, sm[2][0:8, :], ALU.add))
                link(dve.reciprocal(low, low))
                for g in range(3):
                    last = dve.tensor_tensor(nm[g][0:8, :], nm[g][0:8, :], low, ALU.mult)
                last.then_inc(cb_c, 1)

            of1 = tiles(o_g[0], 4)

            def combine(t):
                dve.wait_ge(cb_ps, t + 1)
                for g in range(3):
                    o = tiles(o_g[g], 4)[:, t, 0:SEQ]
                    last = dve.tensor_tensor(o, o, CB_BANKS[g][:, :], ALU.mult)
                last.then_inc(cb_u, 1)
                dve.wait_ge(cb_u, t + 1)
                o = of1[:, t, 0:SEQ]
                link(dve.tensor_tensor(o, o, tiles(o_g[1], 4)[:, t, 0:SEQ], ALU.add))
                link(dve.tensor_tensor(o, o, tiles(o_g[2], 4)[:, t, 0:SEQ], ALU.add))

            def prompt_work(b, i):
                beside(b, i, 1, lambda s: group_maximum(2, s, lambda it: P1_SCORES), 7)
                beside(b, i, 6, lambda s: s % 2 or group_output(2, s + 1, P1_OUTPUT), 6)
                once(b, i, 19, total_sums)
                beside(b, i, 20, statistics, 1)
                once(b, i, 23, relative)
                once(b, i, 25, group_factors)
                beside(b, i, 27, combine, 3)

            dve.wait_ge(qs_saved, 8)
            sample_attention(1, orun1, samp[1], prompt_work)
            sample_finish(1, orun1, samp[1], of1)
            dve.wait_ge(SS[1]["fin_d"], 1)
            split_lo(T_OC // 4, 0)
            split_lo(T_OC // 4, 1)
            for t in range(4):
                t1 = sqbuf[:, N * (t % 2):N * (t % 2) + N]
                if t == 0:
                    dve.wait_ge(SS[1]["fin_ps"], 1)
                dve.tensor_copy(t1, of1[:, t, :]).then_inc(sub_t, 1)
                dve.wait_ge(bhi_ready, 45 + t)
                dve.tensor_tensor(blk[:, 4 + t, :], t1, bhk[:, 4 + t, :].bitcast(F32), ALU.subtract).then_inc(b_ready, 1)

            dense(lambda i: i + T_OC // 4, 2, down, fin_post(3, G_MLP + 8), static=True)
            mlp(1, T_M1)

            rms(4)()
            for k in range(KT_N):
                dve.scalar_tensor_tensor(out=y_feat[:, N * k:N * k + N], in0=xk[:, k, :],
                                         scalar=gains[:, G_OUT + k:G_OUT + k + 1], in1=rnorm[:, :], op0=ALU.mult,
                                         op1=ALU.mult).then_inc(y_ready, 1)
            for t in range(1, 5, 2):
                dve.wait_ge(yt_ps, t + 1)
                dve.wait_ge(yt_done, t)
                dve.tensor_copy(y_tok[:, t, :], acc[t % 2][:, :]).then_inc(yt_done, 1)

        @block.scalar
        def _(act):
            def split_hi(G, q, free=True):
                j = q % 2
                if j == 0:
                    act.wait_ge(raw_loaded[q // 2], G * 16 + 16)
                act.activation(whi_v[j], raw_v[q // 2][:, :, j, :], ACT.Copy).then_inc(whi_ready, 1)

            def dense(group, n_groups, post=None, peel=False, hook=None, static=False, last=False):
                def four(G, i):
                    for q in range(4):
                        act.wait_ge(tile_done, G * 4 + (q + 1))
                        if not (last and q >= 2 and i == n_groups - 1):
                            split_hi(*((G, q + 2) if q < 2 else (G + 1, q - 2)))
                        if hook and q == 0 and isinstance(i, int) and i == 0:
                            hook()
                        if post:
                            post(G, i, q)
                done = 0
                while done < n_groups and (static or n_groups - done == 1 or (peel and done == 0)):
                    four(group(done), done)
                    done += 1
                if done < n_groups:
                    with act.Fori(done, n_groups) as i:
                        four(group(i), i)

            def root(f):
                def go():
                    act.wait_ge(v_ready, f + 1)
                    act.activation(rnorm[:, :], rnorm[:, :], ACT.Sqrt).then_inc(sqrt_ready, 1)
                return go

            def up_post(s0, b0):
                def post(G, i, q):
                    act.wait_ge(sq_up, s0 + i * 4 + (q + 1))
                    act.activation(b_hi[:, ds(i * (4 * N) + q * N, N)], sqbuf[:, N * (q % 2):N * (q % 2) + N],
                                   ACT.Copy).then_inc(bhi_ready, 1)
                return post

            def fin_post(f, gcol, ready, r0, hi=True):
                def post(G, i, q):
                    k = 4 * i + q
                    act.wait_ge(ready, r0 + k + 1)
                    if hi:
                        act.activation(ahk[:, k, :], xk[:, k, :], ACT.Copy,
                                       scale=gains[:, gcol + k:gcol + k + 1]).then_inc(ahi_ready, 1)
                    if 8 * f + k >= 2:
                        act.wait_ge(sqs_done, 8 * f + k - 1)
                    act.activation(zbuf[:, N * (k % 2):N * (k % 2) + N], xk[:, k, :], ACT.Square).then_inc(xsq_ready, 1)
                return post

            def mlp(L, t0):
                G0, fb = t0 // 4, (8, 48)[L]
                dense(lambda i: i + G0, 2, up_post(32 * L, fb), peel=True, hook=root(1 + 2 * L))
                dense(lambda i: i + (G0 + 2), 2)
                with act.Fori(1, 3) as c:
                    dense(lambda i: c * 4 + (i + G0), 2, up_post(c * 8 + 32 * L, fb))
                    dense(lambda i: c * 4 + (i + (G0 + 2)), 2)
                dense(lambda i: i + (G0 + 12), 2, up_post(24 + 32 * L, fb))
                dense(lambda i: i + (G0 + 14), 2,
                      fin_post(2 + 2 * L, G_MIX + 8, acc_free, 2 + t0 + 56, hi=(L == 0)), static=True, last=(L == 1))

            def token_major(T):
                for c in range(5):
                    n = 5 * T + c
                    act.wait_ge(tk_ps, n + 1)
                    if K_BEFORE[n]:
                        act.wait_ge(kout[n % 2], 16 * K_BEFORE[n])
                    rows = P if c < 4 else NS
                    act.activation(k_tok[n % 2][0:rows, :], bank[6][0:rows, :], ACT.Copy).then_inc(tk_done, 1)

            def sample_attention(L, pt, stat, other_work):
                B, S = BLK[L], SS[L]

                def keys(b, i, pages):
                    for p in pages:
                        if p >= B["pages"][i]:
                            continue
                        act.wait_ge(S["kt_ps"], b * B["pn"] + (4 * i + p + 1))
                        act.activation(kt_sa[L][i % 2][:, :, p, :], bank[0].rearrange("p (i n) -> p i n", i=4),
                                       ACT.Copy).then_inc(S["kt_a"], 1)

                def sequence(b):
                    for i in range(5):
                        keys_beside(b, i, keys, (0,))
                        neg = stat[:, S_NEG + i:S_NEG + i + 1]
                        act.wait_ge(S["neg"], b * 5 + (i + 1))
                        if i:
                            act.activation(stat[:, S_ALPHA + i:S_ALPHA + i + 1],
                                           stat[:, S_NEG + i - 1:S_NEG + i], ACT.Exp, bias=neg, scale=-1.0)
                        at_least(act, S["pt_ps"], b * 5 + i)
                        w = P * B["pages"][i] if i < 4 else NS * B["new"]
                        act.activation(e_sa[L][i % 2][:, 0:w], SCORES[:, 0:w], ACT.Exp, bias=neg,
                                       accum_out=stat[:, S_SUM + i:S_SUM + i + 1]).then_inc(S["e"], 1)
                        keys_beside(b, i, keys, (2,))
                        act.wait_ge(S["pt_ps"], b * 5 + (i + 1))
                        n, w = (B["pages"][i], P) if i < 4 else (B["new"], NS)
                        act.activation(pt[i % 2][0:w, 0:P * n], WEIGHTS[0:w, 0:P * n],
                                       ACT.Copy).then_inc(S["pt"], 1)
                        other_work(b, i)

                keys(0, 0, (0, 2))
                for b in range(NB):
                    sequence(b)

            split_hi(0, 0)
            split_hi(0, 1)
            act.wait_ge(gain_ready, 1)
            for k in range(KT_N):
                fin_post(0, G_MIX, x_ready, 0)(0, 0, k)
            act.wait_ge(lam_d, 1)
            act.activation(lam_t[:, 130:132], lam_t[:, 128:130], ACT.Exp).then_inc(lam_e, 1)

            dense(lambda i: i, 4, peel=True, hook=root(0))
            token_major(0)

            def prompt_stage(s):
                if s < 16:
                    qt, u = s % 4, s % 2
                    nk = P * (qt + 1)
                    act.wait_ge(p0_m, s + 1)
                    if s >= 2:
                        act.wait_ge(p0_t, s - 1)
                    for m in range(2):
                        last = act.activation(e4[u][m][:, 0:nk], P0_SCORES[:, 512 * m:512 * m + nk], ACT.Exp,
                                              bias=neg0[:, u, m:m + 1], accum_out=sum0[:, u, m:m + 1])
                    last.then_inc(p0_e, 1)
                if s >= 1:
                    n = s - 1
                    nk = P * (n % 4 + 1)
                    act.wait_ge(p0_t, n + 1)
                    if n >= 2:
                        act.wait_ge(p0_pv, n - 1)
                    act.activation(pt_p0[n % 2][:, 0:nk], P0_WEIGHTS[:, 0:nk], ACT.Copy).then_inc(p0_at, 1)

            sample_attention(0, pt_l0, samp[0], lambda b, i: beside(b, i, 1, prompt_stage, 16))
            for g in range(4):
                act.wait_ge(mix_ps, g + 1)
                act.activation(bhk[:, g, :].rearrange("p (h c) -> p h c", h=2), acc_h[g % 2], ACT.Copy,
                               scale=gains[:, G_SCALE + g:G_SCALE + g + 1]).then_inc(bhi_ready, 1)
            of0 = tiles(o_feat0, 4)
            act.wait_ge(SS[0]["fin_d"], 1)
            for h in range(4 + 1):
                if h < 4:
                    if h >= 2:
                        act.wait_ge(sub_ms, h - 1)
                    act.activation(zbuf[:, N * (h % 2):N * (h % 2) + N], of0[:, h, :], ACT.Square).then_inc(sub_sq, 1)
                if h >= 1:
                    t1 = sqbuf[:, N * ((h - 1) % 2):N * ((h - 1) % 2) + N]
                    act.wait_ge(sub_v, h)
                    act.activation(t1, t1, ACT.Sqrt).then_inc(sub_r, 1)
                    act.wait_ge(sub_t, h)
                    act.activation(bhk[:, 3 + h, :], t1, ACT.Copy).then_inc(bhi_ready, 1)
            dense(lambda i: i + T_OA // 4, 2, fin_post(1, G_MLP, acc_free, 2 + T_OA), static=True)
            mlp(0, T_M0)

            dense(lambda i: i + T_CD // 4, 3, peel=True, hook=root(2))
            for k in range(4):
                act.wait_ge(sub_t, 4 + k + 1)
                act.activation(bhk[:, k, :], cv[:, N * (k % 2):N * (k % 2) + N], ACT.Copy).then_inc(bhi_ready, 1)

            def group_exp(g, n, scores):
                c, par, its = units1[g][n]
                act.wait_ge(p1_m, 8 * g + n + 1)
                for k, it in enumerate(its):
                    if it >= 2:
                        act.wait_ge(p1_t, it - 1)
                    for t in range(4):
                        h = 4 * par + t
                        dst = sum1[:, g, c, h:h + 1] if k == 0 else sump[:, c, h:h + 1]
                        last = act.activation(e2[it % 2][:, P * t:P * t + P], scores(it)[:, P * t:P * t + P], ACT.Exp,
                                              bias=neg1[:, g, c, h:h + 1], accum_out=dst)
                    last.then_inc(p1_e, 1)

            def group_weights(g, n, weights):
                for it in units1[g][n][2]:
                    act.wait_ge(p1_t, it + 1)
                    if it >= 2:
                        act.wait_ge(p1_pv, UNIT_OF[it - 2] + 1)
                    act.activation(pt_l1[it % 2][:, :], weights(it)[:, :], ACT.Copy).then_inc(p1_pt, 1)

            for g in range(3):
                if g < 2:
                    dense(lambda i: i + (T_CD // 4 + 3 + 3 * g), 3)
                else:
                    dense(lambda i: i + (T_CD // 4 + 9), 2)
                    dense(lambda i: i + (T_CD // 4 + 11), 1, last=True)
                token_major(1 + g)
                for s in range(8 + 1 if g < 2 else 0):
                    if s < 8:
                        group_exp(g, s, lambda it: bank[it % 4])
                    if s >= 1:
                        group_weights(g, s - 1, lambda it: bank[4 + it % 2])

            def prompt_stage(s):
                if s < 8:
                    group_exp(2, s, lambda it: P1_SCORES)
                if s >= 1:
                    group_weights(2, s - 1, lambda it: P1_WEIGHTS)

            def relative():
                act.wait_ge(cb_x, 1)
                for g in range(3):
                    act.activation(nm[g][0:8, :], nm[g][0:8, :], ACT.Exp).then_inc(cb_e, 1)

            def prompt_work(b, i):
                beside(b, i, 1, prompt_stage, 8)
                once(b, i, 25, relative)

            act.wait_ge(qs_saved, 8)
            sample_attention(1, pt_s1, samp[1], prompt_work)
            act.wait_ge(SS[1]["fin_ps"], 1)
            split_hi(T_OC // 4, 0)
            split_hi(T_OC // 4, 1)
            for t in range(4):
                act.wait_ge(sub_t, 8 + t + 1)
                act.activation(bhk[:, 4 + t, :], sqbuf[:, N * (t % 2):N * (t % 2) + N], ACT.Copy).then_inc(bhi_ready, 1)
            dense(lambda i: i + T_OC // 4, 2, fin_post(3, G_MLP + 8, acc_free, 2 + T_OC), static=True)
            mlp(1, T_M1)

            root(4)()
            for t in range(0, 5, 2):
                rows = P if t < 4 else NS
                act.wait_ge(yt_ps, t + 1)
                act.wait_ge(yt_done, t)
                act.activation(y_tok[0:rows, t, :], acc[t % 2][0:rows, :], ACT.Copy).then_inc(yt_done, 1)

        @block.gpsimd
        def _(pool):
            steps = Tally()

            def link(ins):
                ins.then_inc(pool_step, 1)
                pool.wait_ge(pool_step, steps.add())

            def sum_squares(f):
                for k in range(KT_N):
                    pool.wait_ge(xsq_ready, 8 * f + k + 1)
                    src = zbuf[:, N * (k % 2):N * (k % 2) + N]
                    if k == 0:
                        if f:
                            pool.wait_ge(ms_ready, f)
                        pool.tensor_copy(sqsum[:, :], src).then_inc(sqs_done, 1)
                    else:
                        pool.wait_ge(sqs_done, 8 * f + k)
                        pool.tensor_tensor(sqsum[:, :], sqsum[:, :], src, ALU.add).then_inc(sqs_done, 1)

            def save_samples(n, g, qb):
                pool.wait_ge(q_scaled, n)
                pool.tensor_copy(q_s[:, g, :, :], pk[:, qb:qb + 4, SEQ:N]).then_inc(qs_saved, 1)
                pool.tensor_copy(k_s[:, g, :, :], pk[:, qb + 4:qb + 8, SEQ:N]).then_inc(qs_saved, 1)

            def stage_queries(L, groups):
                S = SS[L]
                pool.wait_ge(qs_saved, (2, 8)[L])

                def stage(b):
                    if b >= 2:
                        pool.wait_ge(S["s"], 5 * (b - 1))
                    for hf in range(2):
                        if b or hf:
                            pool.wait_ge(S["q"], b * 2 + hf)
                        pool.tensor_copy(staged[L][b % 2][64 * hf:64 * hf + 64, 0:groups, :, 8 * hf:8 * hf + 8],
                                         q_s[64 * hf:64 * hf + 64, 0:groups, :, 8 * b:8 * b + 8]).then_inc(S["q"], 1)

                def values(b, i):
                    load_block(pool, 0, 1, b, i, 0)
                    load_block(pool, 0, 1, b, i, 1)

                stage(0)
                if L == 0:
                    pool.wait_ge(tile_done, T_AB + 16)
                for b in range(NB):
                    if L == 0 and b:
                        values(b, 0)
                    if L == 0:
                        values(b, 1)
                    if b < NB - 1:
                        stage(b + 1)
                    if L == 0:
                        values(b, 2)
                        values(b, 3)
                pool.wait_ge(S["q"], 2 * NB)

            def copy(dst, src):
                pool.dma_start(dst, src).then_inc(outs[3], 16)

            pool.memset(q_st, 0.0).then_inc(q_zero, 1)
            pool.wait_ge(q_zero, 1)
            copy(a["new_pool_sample"][0][:, 0:7, :], a["state_a_pool"][0][:, 8:15, :])
            pool.wait_ge(s_page, 16)
            load_block(pool, 0, 1, 0, 0, 0)
            load_block(pool, 0, 1, 0, 0, 1)
            sum_squares(0)
            link(pool.memset(pool_a[:, :, 0:16], 0.0))

            pool.wait_ge(hist_done, 1)
            pool.wait_ge(rows_ps, 1)
            for g in range(4):
                w = 2 << g
                u = pk[:, g, 0:SEQ]
                us = pk[:, g, SEQ:N].rearrange("p (b c) -> p b c", b=NB)
                if g:
                    pool.wait_ge(pm_ready, g)
                pool.tensor_copy(pool_s[:, 0, :, 0:15], hist_f[:, g, :, :])
                pool.tensor_copy(pool_s[:, 0, :, 15:23], us)
                link(pool.tensor_copy(pool_a[:, 0, 16:528], u))
                for j in range(g + 1):
                    d, s, k = pool_a[:, (j + 1) % 2, :], pool_a[:, j % 2, :], 1 << j
                    ss_, sd = pool_s[:, j % 2, :, :], pool_s[:, (j + 1) % 2, :, :]
                    pool.tensor_tensor(sd[:, :, 2 * k - 1:23], ss_[:, :, 2 * k - 1:23], ss_[:, :, k - 1:23 - k], ALU.add)
                    link(pool.tensor_tensor(d[:, 16:528], s[:, 16:528], s[:, 16 - k:528 - k], ALU.add))
                m, ms = pool_a[:, (g + 1) % 2, :], pool_s[:, (g + 1) % 2, :, 15:23]
                pool.tensor_tensor(m[:, 16:16 + w - 1], m[:, 16:16 + w - 1], cc("rtab")[:, 0:w - 1], ALU.mult)
                pool.tensor_scalar(ms, ms, 1.0 / w, None, ALU.mult)
                link(pool.tensor_scalar(m[:, 16 + w - 1:528], m[:, 16 + w - 1:528], 1.0 / w, None, ALU.mult))
                pool.tensor_tensor(us, ms, us, ALU.subtract)
                pool.tensor_tensor(u, m[:, 16:528], u, ALU.subtract).then_inc(pm_ready, 1)
            save_samples(1, 0, 4)
            pool.wait_ge(pm_ready, 4)
            stage_queries(0, 1)
            sum_squares(1)

            def kept(g):
                return (a[f"new_d{g}_sample"][0].rearrange("b t v h e -> b t (v h e)"),
                        a[f"cache_d{g}_kv"][0].rearrange("b t v h e -> b t (v h e)"))

            def piece(g, b, row, rows, cut):
                dst, src = kept(g)
                f = lambda v, r: (v[ds(b, 1), ds(r, rows), :].rearrange("o t f -> (o t f)")
                                  .rearrange("(p q) -> p q", q=cut))
                copy(f(dst, row), f(src, row + TS))

            QROWS = (WIN[2] - TS) // 4
            with pool.Fori(0, NB - 1) as b:
                for q in range(4):
                    pool.wait_ge(tile_done, b * 8 + (T_M0 + 2 * q + 1))
                    piece(2, b, QROWS * q, QROWS, QROWS * 1024 // 32)
            sum_squares(2)

            for g in range(3):
                save_samples(2 + g, g, 0)
            pool.wait_ge(tile_done, T_CD + 48)
            pool.memset(q_st1, 0.0).then_inc(q_zero, 1)
            pool.wait_ge(q_zero, 2)
            stage_queries(1, 3)
            sum_squares(3)
            for q in range(4):
                pool.wait_ge(tile_done, T_M1 + 2 * q + 1)
                piece(2, NB - 1, QROWS * q, QROWS, QROWS * 1024 // 32)
            with pool.Fori(0, NB) as b:
                pool.wait_ge(tile_done, b * 2 + (T_M1 + 9))
                piece(1, b, 0, WIN[1] - TS, (WIN[1] - TS) * 1024 // 32)
            for b in range(0, NB, 4):
                pool.wait_ge(tile_done, T_M1 + 25 + b // 2)
                dst, src = kept(0)
                copy(dst[b:b + 4, 0:WIN[0] - TS, :], src[b:b + 4, TS:WIN[0], :])
            sum_squares(4)
            pool.wait_ge(outs[3], 16 * (1 + 32 + 8 + 2))


_SHAPES = [("y_prompt", (1, SEQ, D)), ("y_sample", (NB, TS, D)), ("new_pool_prompt", (1, 1, 15, 512)),
           ("new_pool_sample", (1, NB, 15, 512)), ("new_bkv_prompt", (1, 1, SEQ, 2, 4, 128)),
           ("new_bkv_sample", (1, NB, TS, 2, 4, 128)), ("new_conv_prompt", (1, 1, 2, 512)),
           ("new_conv_sample", (1, NB, 2, 512))]
for _g in range(3):
    _SHAPES += [(f"new_d{_g}_prompt", (1, 1, min(WIN[_g], SEQ), 2, 8, 64)),
                (f"new_d{_g}_sample", (1, NB, WIN[_g], 2, 8, 64))]


def kernel(**inputs):
    import concourse.bacc as bacc
    from concourse.bass_utils import run_bass_kernel_spmd

    nc = bacc.Bacc("TRN2", target_bir_lowering=False, num_devices=1)
    arrays = {name: np.ascontiguousarray(v) for name, v in inputs.items()}
    arrays["consts"] = constants()
    arrays = {f"in_{name}": v for name, v in arrays.items()}
    aps = {name[3:]: nc.dram_tensor(name, v.shape, mybir.dt.from_np(v.dtype), kind="ExternalInput").ap()
           for name, v in arrays.items()}
    for name, shape in _SHAPES:
        aps[name] = nc.dram_tensor(f"out_{name}", shape, F32, kind="ExternalOutput").ap()
    build(nc, aps)
    r = run_bass_kernel_spmd(nc, [arrays], core_ids=[0])
    return tuple(r.results[0][f"out_{name}"] for name, _ in _SHAPES)
```

```python
from contextlib import ExitStack, contextmanager

import numpy as np
import concourse.bass as bass
from concourse import mybir

F32 = mybir.dt.float32
F32R = mybir.dt.float32r
I32 = mybir.dt.int32
ALU = mybir.AluOpType
ACT = mybir.ActivationFunctionType
AX = mybir.AxisListType
ds = bass.ds

P = 128
D = 1024
KT_N = D // P
SEQ, NB, TS = 512, 8, 8
NS = NB * TS
N = SEQ + NS
NH = N // 2
EPS = 1e-6
LAM_INIT = 0.8 - 0.6
NEG = -1e30
PAST, PAGE = 2048, 128
NPAGES = PAST // PAGE
WIN, DIL = (128, 512, 2048), (1, 4, 16)
FF = 4 * D

T_AB, T_OA, T_M0 = 0, 16, 24
T_CD = T_M0 + 64
T_OC = T_CD + 48
T_M1 = T_OC + 8
T_END = T_M1 + 64

C = {}
_at = 0
for _n, _w in (("ident", 128), ("ones", 128), ("causal", 128), ("prev", 128), ("g2m", 128), ("rm2", 8), ("rm1", 4),
               ("k01", 4), ("g0m", 8), ("selfm", 360), ("sel", 32), ("halfm", 2), ("rtab", 16),
               ("sel8", 512)):
    C[_n] = (_at, _w)
    _at += _w
NC_ = (_at + 7) // 8 * 8


def constants():
    c = np.zeros((P, NC_), np.float32)

    def put(name, a):
        c[:a.shape[0], C[name][0]:C[name][0] + C[name][1]] = a

    i = np.arange(P)
    put("ident", np.eye(P))
    put("ones", np.ones((P, P)))
    put("causal", np.where(i[None] <= i[:, None], 0, NEG))
    put("prev", np.where(i[None] >= i[:, None], 0, NEG))
    r, l = i // 32, i % 32
    put("g2m", np.where((r[:, None] == r[None]) & (l[None] <= l[:, None]), 0, NEG))
    real = (i % 32) < 16
    t, half = i % 8, (i % 32) // 8
    put("rm2", np.where(real[:, None] & (t[:, None] != np.arange(8)[None]), NEG, 0))
    put("rm1", np.where(real[:, None] & (t[:, None] % 4 != np.arange(4)[None]), NEG, 0))
    put("k01", np.where(real[:, None] & (t[:, None] == np.arange(4)[None] + 4), NEG, 0))
    put("g0m", np.where(real[:, None] & (np.arange(8)[None] < t[:, None]), NEG, 0))
    sm = np.zeros((P, 3, 15, 8), np.float32)
    sm[real] = NEG
    for g in range(3):
        for row in i[real]:
            for t2 in range(8):
                if t2 <= t[row] and (t[row] - t2) % DIL[g] == 0:
                    sm[row, g, 7, t2] = 0
    put("selfm", sm.reshape(P, 360))
    sel = np.zeros((P, 32), np.float32)
    for row in i[real]:
        sel[row, (row // 32) * 8 + t[row]] = 1
    put("sel", sel)
    put("halfm", (half[:, None] == np.arange(2)[None]) & real[:, None])
    put("rtab", np.broadcast_to(1.0 / (1.0 + np.arange(16)), (P, 16)))
    s8 = np.zeros((8, 4, P), np.float32)
    for h in range(8):
        s8[h, h % 4, 64 * (h // 4):64 * (h // 4) + 64] = 1
    put("sel8", s8.reshape(8, 512))
    return c


class Tally:

    def __init__(self):
        self.n, self.terms = 0, []

    def add(self, k=1):
        self.n += k
        return self.now()

    def now(self):
        v = self.n
        for reg, k in self.terms:
            v = reg * k + v
        return v

    @contextmanager
    def loop(self, reg, per, first, end):
        start = self.n
        self.n = start - first * per
        self.terms.append((reg, per))
        inner = self.n
        yield
        self.terms.pop()
        assert self.n - inner == per, (self.n - inner, per)
        self.n = start + per * (end - first)


def build(nc, a):
    with ExitStack() as ctx:
        sem = lambda name: ctx.enter_context(nc.semaphore(name))

        pp = [ctx.enter_context(nc.psum_tensor(f"pp{i}", [P, 1024], F32)) for i in range(4)]
        bank = [pp[i // 2][:, 512 * (i % 2):512 * (i % 2) + 512] for i in range(8)]
        halves = [pp[i][:, :].rearrange("p (h c) -> p h c", h=2)[:, :, 0:NH] for i in range(4)]
        acc = pp[0:2]
        acc_h = halves[0:2]

        base = nc.sbuf_base
        total = (nc.sbuf_usable_end - base) // 32 * 8 - 16
        ctx.enter_context(nc.sbuf_tensor("whole_map", [P, total], F32))
        base = (base + 31) // 32 * 32

        def at(name, word, words, dt=F32):
            assert word + words <= total, (name, word + words, total)
            return nc.alloc_sbuf_tensor_at(name, [P, words], dt, offset=base + 4 * word)

        def tiles(t, n, first=0):
            return t[:, first * N:(first + n) * N].rearrange("p (k n) -> p k n", n=N)

        W_X, W_A, W_B = 0, KT_N * N, 3 * KT_N * N
        W_RAW = W_B + 2 * KT_N * N
        W_W = W_RAW + 4096
        W_PROJ = W_W + 4096
        W_TMP = W_PROJ + 16 * N
        W_CONST = W_TMP + 6 * N
        W_G = W_CONST + NC_
        W_S = W_G + 64
        x = at("x", W_X, KT_N * N)
        a_hi, a_lo = at("a_hi", W_A, KT_N * N, F32R), at("a_lo", W_A + KT_N * N, KT_N * N, F32R)
        b_hi, b_lo = at("b_hi", W_B, KT_N * N, F32R), at("b_lo", W_B + KT_N * N, KT_N * N, F32R)
        xk = tiles(x, 8)
        ahk, alk, bhk, blk = (tiles(t, 8) for t in (a_hi, a_lo, b_hi, b_lo))
        raw = [at(f"raw{i}", W_RAW + 2048 * i, 2048) for i in range(2)]
        whi = [at(f"whi{i}", W_W + 1024 * i, 1024, F32R) for i in range(2)]
        wlo = [at(f"wlo{i}", W_W + 2048 + 1024 * i, 1024, F32R) for i in range(2)]
        raw_v = [t[:, :].rearrange("p (k j n) -> p k j n", k=KT_N, j=2) for t in raw]
        whi_v = [t[:, :].rearrange("p (k n) -> p k n", k=KT_N) for t in whi]
        wlo_v = [t[:, :].rearrange("p (k n) -> p k n", k=KT_N) for t in wlo]
        proj = at("proj", W_PROJ, 16 * N)
        pk = tiles(proj, 16)
        rnorm = at("rnorm", W_TMP, N)
        r_h = rnorm[:, :].rearrange("p (h c) -> p h c", h=2)
        zbuf = at("zbuf", W_TMP + N, 2 * N)
        sqbuf = at("sqbuf", W_TMP + 3 * N, 2 * N)
        sqsum = at("sqsum", W_TMP + 5 * N, N)
        dummy = at("dummy", total - 8, 1)
        con = at("con", W_CONST, NC_)
        gains = at("gains", W_G, 64)
        cc = lambda n: con[:, C[n][0]:C[n][0] + C[n][1]]
        ident, ones = cc("ident"), cc("ones")
        G_MIX, G_MLP, G_OUT, G_SCALE, G_CONV, G_SUBLN = 0, 16, 32, 40, 44, 56

        W_AX = W_A + 4 * 2048
        W_BH, W_BL = W_B + 4 * N, W_B + KT_N * N + 4 * N
        W_V, W_K, W_Q, W_E = W_S, W_S + 2048, W_S + 3072, W_S + 6144
        W_QST = W_S + 7168
        W_STAT = W_TMP + 3 * N
        x_tok = at("x_tok", W_PROJ, 5 * D)[:, :].rearrange("p (t d) -> p t d", d=D)
        gain_rows = at("gain_rows", W_S, P)
        kring = [at(f"kring{i}", W_A + 2048 * i, 2048) for i in range(2)]
        vring = [at(f"vring{i}", W_A + 4096 + 2048 * i, 2048) for i in range(2)]
        kring0, vring0 = at("kring_l0", W_B, 2048), at("vring_l0", W_B + KT_N * N, 2048)
        kring_v, vring_v = ([[t[:, :].rearrange("p (g f) -> p g f", g=4) for t in r] for r in rings]
                            for rings in (((kring0, kring[1]), kring), ((vring0, vring[1]), vring)))
        v_all = at("v_all", W_V, 2048)[:, :].rearrange("p (c f) -> p c f", c=4)
        k_tok = [at(f"k_tok{i}", W_K + 512 * i, 512) for i in range(2)]
        qkv_s = at("qkv_s", W_Q, 3072)[:, :].rearrange("p (g w) -> p g w", g=3)
        q_s = qkv_s[:, :, 0:256].rearrange("p g (i n) -> p g i n", i=4)
        k_s = qkv_s[:, :, 256:512].rearrange("p g (i n) -> p g i n", i=4)
        v_s = qkv_s[:, :, 512:1024]
        e2 = [at(f"e{i}", W_E + 512 * i, 512) for i in range(2)]
        q_st = at("q_st", W_QST, 384)[:, :].rearrange("p (g i c) -> p g i c", g=3, i=4)
        neglam = at("neglam", W_QST + 384, 2)
        pages = nc.alloc_sbuf_tensor_at("pages", [1, P], I32, offset=base + 4 * (W_Q + 2928))
        lam_in = at("lam_in", W_E, 256)
        lam_t = at("lam_t", W_E + 256, 132)
        pt_l0 = [at(f"pt_l0{i}", W_AX + 512 * i, 512) for i in range(2)]
        pt_l1 = [at(f"pt_l1{i}", W_PROJ + 12 * N + 512 * i, 512) for i in range(2)]
        hist_tok = at("hist_tok", W_STAT, 512)
        a_mix = at("a_mix", W_STAT + 640, 512)
        stat0 = at("stat0", W_STAT + 512, 128)
        e4 = [[at(f"e4{u}{m}", W_BL + 1024 * u + 512 * m, 512) for m in range(2)] for u in range(2)]
        pt_p0 = [at(f"pt_p0{i}", W_PROJ + 12 * N + 512 * i, 512) for i in range(2)]
        kt_l0 = [at(f"kt_l0{i}", W_A + 4096 * i, 2048) for i in range(2)]
        o_feat0 = at("o_feat0", W_BH, 4 * N)
        orun0 = at("orun0", W_TMP + N, 1024)
        pool_a = at("pool_a", W_Q + 1024, 2 * 528)[:, :].rearrange("p (i c) -> p i c", i=2)
        pool_s = at("pool_s", W_Q + 1024 + 1056, 2 * 184)[:, :].rearrange("p (i b c) -> p i b c", i=2, b=NB)
        hist_f = at("hist_f", W_Q + 1024 + 1056 + 368, 480)[:, :].rearrange("p (g b c) -> p g b c", g=4, b=NB)
        conv_tok = at("conv_tok", W_STAT, 512)
        stat1 = at("stat1", W_STAT + 512, 640)
        cv = at("cv", W_V, 4 * N)
        zext = at("zext", W_V + 4 * N, 320)[:, :].rearrange("p (k b c) -> p k b c", k=4, b=NB)
        e_p1 = [e2[0], e2[1], zbuf[:, 0:512]]
        kt_l1 = [at(f"kt_l1{i}", W_RAW + 2048 * i, 2048) for i in range(2)]
        e_l1 = [at(f"e_l1{i}", W_W + 512 * i, 512) for i in range(2)]
        pt_s1 = [at(f"pt_s1{i}", W_W + 1024 + 512 * i, 512) for i in range(2)]
        e_sa = [e2, e_l1]
        q_st1 = at("q_st1", W_W + 3072, 384)[:, :].rearrange("p (g i c) -> p g i c", g=3, i=4)
        staged = [[q_st[:, 0:1, :, :], q_st[:, 1:2, :, :]], [q_st, q_st1]]
        kt_sa = [[t[:, :].rearrange("p (i g n) -> p i g n", i=4, g=4) for t in k] for k in (kt_l0, kt_l1)]
        orun1 = at("orun1", W_W + 2048, 1024)
        o_g = [at("o_g0", W_BH, 4 * N), at("o_g1", W_BL, 4 * N), at("o_g2", W_PROJ + 8 * N, 4 * N)]
        nm = [at(f"nm{g}", W_V + 512 * g, 512) for g in range(3)]
        sm = [at(f"sm{g}", W_V + 1536 + 512 * g, 512) for g in range(3)]
        y_feat = at("y_feat", W_A, KT_N * N)
        y_tok = at("y_tok", W_PROJ, 5 * D)[:, :].rearrange("p (t d) -> p t d", d=D)

        y_ps = [pp[3], pp[0], pp[1], pp[3], pp[0]]
        r_tok = rnorm[:, 0:5]

        r_head = rnorm[:, 0:20]

        neg0 = stat0[:, 0:4].rearrange("p (u m) -> p u m", u=2)
        sum0 = stat0[:, 4:8].rearrange("p (u m) -> p u m", u=2)
        rs0 = stat0[:, 8:12].rearrange("p (u m) -> p u m", u=2)
        S_NEG, S_TMP, S_ALPHA, S_SUM, S_RUN, S_REC, S_COMB = 0, 5, 6, 12, 18, 26, 34
        neg1 = stat1[:, 320:416].rearrange("p (g c h) -> p g c h", g=3, c=4)
        sum1 = stat1[:, 416:512].rearrange("p (g c h) -> p g c h", g=3, c=4)
        negp = stat1[:, 512:544].rearrange("p (c h) -> p c h", c=4)
        sump = stat1[:, 544:576].rearrange("p (c h) -> p c h", c=4)
        samp = [at("samp0", W_STAT, 512), at("samp1", W_STAT, 512)]

        s_const, s_x, s_gain, s_lam, s_hist, s_page = (sem(n) for n in
            ("const_loaded", "x_loaded", "gains_loaded", "lam_loaded", "hist_loaded", "pages_loaded"))
        raw_loaded = [sem(f"raw_loaded{i}") for i in range(2)]
        whi_ready, wlo_ready = sem("whi_ready"), sem("wlo_ready")
        tile_done, acc_free = sem("tile_done"), sem("acc_free")
        ahi_ready, a_ready = sem("ahi_ready"), sem("a_ready")
        bhi_ready, b_ready = sem("bhi_ready"), sem("b_ready")
        xsq_ready, sqs_done = sem("xsq_ready"), sem("sqs_done")
        ms_ready, v_ready, sqrt_ready = sem("ms_ready"), sem("v_ready"), sem("sqrt_ready")
        gain_ps, gain_ready, xt_ps, x_ready = sem("gain_ps"), sem("gain_ready"), sem("xt_ps"), sem("x_ready")
        sq_up = sem("sq_up")
        dve_step, pool_step = sem("dve_step"), sem("pool_step")
        lam_e, lam_d = sem("lam_e"), sem("lam_d")
        outs = [sem(f"outs{i}") for i in range(4)]
        tk_ps, tv_ps, tk_done, tv_done = (sem(n) for n in ("tk_ps", "tv_ps", "tk_done", "tv_done"))
        kout = [sem(f"kout{i}") for i in range(2)]
        vout = sem("vout")
        q_scaled, qs_saved = sem("q_scaled"), sem("qs_saved")
        hist_ps, hist_done, rows_ps, rows_done, rows_out = (sem(n) for n in
            ("hist_ps", "hist_done", "rows_ps", "rows_done", "rows_out"))
        pm_ready, mix_ps, mix_done = sem("pm_ready"), sem("mix_ps"), sem("mix_done")
        p0_s, p0_m, p0_e, p0_a, p0_t, p0_at, p0_pv, p0_o = (sem(f"p0_{n}") for n in
            ("s", "m", "e", "a", "t", "at", "pv", "o"))
        p1_s, p1_m, p1_e, p1_t, p1_pt, p1_pv, p1_o = (sem(f"p1_{n}") for n in
            ("s", "m", "e", "t", "pt", "pv", "o"))
        sub_sq, sub_ms, sub_v, sub_r, sub_d, sub_b, sub_t = (sem(f"sub_{n}") for n in
            ("sq", "ms", "v", "r", "d", "b", "t"))
        SS = []
        for L in range(2):
            SS.append({n: sem(f"sa{L}_{n}") for n in
                       ("k00", "k01", "k10", "k11", "v00", "v01", "v10", "v11", "q", "kt_ps", "kt_a", "kt_d", "s", "neg", "e", "pt_ps", "pt",
                        "o_ps", "o", "fin", "fin_ps", "fin_d")})
        cb_t, cb_d, cb_v, cb_x, cb_e, cb_c, cb_ps, cb_u = (sem(f"cb_{n}") for n in
            ("t", "d", "v", "x", "e", "c", "ps", "u"))
        y_ready, yt_ps, yt_done = sem("y_ready"), sem("yt_ps"), sem("yt_done")
        q_zero, rtok_ready = sem("q_zero"), sem("rtok_ready")

        def tok_cols(v, g, c):
            if g == 0:
                return v[:, 128 * c:128 * c + 128]
            if g == 1:
                return v.rearrange("p (l r) -> p r l", r=4)[:, c, :]
            return v.rearrange("p (l c r) -> p c r l", c=4, r=4)[:, c, :, :]

        def proj_cols(v, g, c):
            return tok_cols(v, g if g < 2 else 0, c)

        units1, items1 = [[], [], []], []
        for g in range(3):
            for c in range(4):
                for quad in range(2):
                    parts = [(c, ("causal", "causal", "g2m")[g])] + ([(c - 1, "prev")] if g == 0 and c else [])
                    u = []
                    for kc, mask in parts:
                        u.append(len(items1))
                        items1.append((g, c, quad, kc, mask))
                    units1[g].append((c, quad, u))
        UNIT_OF = {it: 8 * g + s for g in range(3) for s, u in enumerate(units1[g]) for it in u[2]}
        BLK = [dict(pages=(4, 4, 4, 4), groups=(0, 0, 0, 0), new=1, mask=(None,) * 4),
               dict(pages=(4, 4, 4, 1), groups=(2, 2, 1, 0), new=3, mask=("rm2a", "rm2b", "rm1", "g0m"))]
        for b_ in BLK:
            b_["nb"] = 5 if b_["pages"][3] == 4 else 4
            b_["cols"] = [P * n for n in b_["pages"]] + [0] * (b_["nb"] - 4)
            b_["new_at"] = b_["cols"][-1]
            b_["cols"][-1] += NS * b_["new"]
            b_["pn"] = sum(b_["pages"])
            b_["pa"] = sum((n + 1) // 2 for n in b_["pages"])
            b_["pd"] = b_["pn"] - b_["pa"]

        def each_sequence(engine, body):
            body(0)
            with engine.Fori(1, NB - 1) as b:
                body(b)
            body(NB - 1)

        SCORES, WEIGHTS, OUTPUT = bank[2], bank[3], bank[6][:, 0:P]
        P0_SCORES, P0_WEIGHTS, P0_OUTPUT = pp[2], bank[7], bank[7][:, 0:P]

        def chunks(B, i):
            c = [(P * p, P, p, None) for p in range(B["pages"][i] if i < 4 else 0)]
            return c + [(B["new_at"] + NS * g, NS, None, g) for g in range(B["new"]) if i == B["nb"] - 1]

        def beside(m, first, stage, last):
            s, rest = divmod(m - first, 2)
            if rest == 0 and 0 <= s <= last:
                stage(s)

        P1_SCORES, P1_WEIGHTS, P1_OUTPUT, CB_BANKS = bank[4], bank[5], bank[7], (bank[4], bank[5], bank[7])

        def at_least(engine, semaphore, value):
            if not isinstance(value, int) or value > 0:
                engine.wait_ge(semaphore, value)

        def keys_beside(L, b, i, keys, pages):
            if i < 3:
                keys(b, i + 1, pages)
            elif i == BLK[L]["nb"] - 1 and b < NB - 1:
                keys(b + 1, 0, pages)

        def load_block(eng, L, kv, b, i, half):
            B, S = BLK[L], SS[L]
            slot, ring, done = i % 2, (kring_v, vring_v)[kv][L], S[f"{'kv'[kv]}{i % 2}{half}"]
            p0 = 2 * half
            p1 = min(p0 + 2, B["pages"][i])
            if p1 <= p0:
                return
            if L == 0:
                page = [eng.value_load(pages[0:1, ds(b * 16 + (4 * i + p), 1)], min_val=0,
                                       max_val=a["cache_b_kv"].shape[1] - 1) for p in range(p0, p1)]
            if kv == 0:
                if i >= 2:
                    at_least(eng, S["kt_ps"], b * B["pn"] + (4 * (i - 2) + min(B["pages"][i - 2], p0 + 2)))
                else:
                    at_least(eng, S["kt_ps"], b * B["pn"] + (4 * (i + 2) + min(B["pages"][i + 2], p0 + 2) - B["pn"]))
            else:
                at_least(eng, S["o_ps"], b * B["nb"] + (i - 1 if i >= 2 else i + 3 - B["nb"]))
            if L == 0:
                for p in range(p0, p1):
                    eng.dma_start(ring[slot][:, p, :],
                                  a["cache_b_kv"][0][ds(page[p - p0], 1)].rearrange("o t v h e -> (o t) v (h e)")
                                  [:, kv, :]).then_inc(done, 16)
            else:
                g = B["groups"][i]
                src = a[f"cache_d{g}_kv"][0][ds(b, 1)].rearrange("o (i s) v h e -> (o i) s v (h e)", s=DIL[g])
                s0 = p0 + (4 * i if g == 2 else 0)
                eng.dma_start(ring[slot][:, p0:p1, :], src[:, s0:s0 + p1 - p0, kv, :]).then_inc(done, 16)

        def loaded(L, b, i, half):
            B = BLK[L]
            n = [B["pages"][j] > 2 * half for j in (i % 2, i % 2 + 2)]
            return (b * sum(n) + sum(n[:1 + i // 2])) * (32 if L == 0 else 16)

        stored = [not (T == 1 and c < 3) for T in range(4) for c in range(5)]
        V_STORES = [sum(stored[0:5 * T + 5]) for T in range(4)]
        K_BEFORE = [sum(stored[j] for j in range(n % 2, n, 2)) for n in range(22)]
        K_STORES = (K_BEFORE[20], K_BEFORE[21])

        block = ctx.enter_context(nc.Block())

        @block.sync
        def _(sp):
            def unit(w, col, n, slot, wait=True):
                if wait:
                    sp.wait_ge(wlo_ready, 2 * n - 2)
                sp.dma_start(raw_v[slot].rearrange("p k j n -> p k (j n)"),
                             w.rearrange("(k p) n -> p k n", p=P)[:, :, ds(col, 256)]).then_inc(raw_loaded[slot], 16)

            def matrix(w, t0, n_tiles, first=0):
                if n_tiles // 4 - first == 1:
                    for s in range(2):
                        unit(w, 512 * first + 256 * s, t0 // 2 + 2 * first + s, s)
                    return
                with sp.Fori(first, n_tiles // 4) as i:
                    for s in range(2):
                        unit(w, i * 512 + 256 * s, i * 2 + t0 // 2 + s, s)

            def mlp_weights(L, t0):
                up, down = a["w_up"][L], a["w_down"][L].rearrange("(c k) n -> c k n", c=4)
                with sp.Fori(0, 4) as c:
                    with sp.Fori(0, 2) as i:
                        for s in range(2):
                            unit(up, c * 1024 + i * 512 + 256 * s, c * 8 + i * 2 + t0 // 2 + s, s)
                    with sp.Fori(0, 2) as i:
                        for s in range(2):
                            sp.wait_ge(wlo_ready, (c * 8 + i * 2 + (t0 // 2 + 4 + s)) * 2 - 2)
                            sp.dma_start(raw_v[s].rearrange("p k j n -> p k (j n)"),
                                         down[ds(c, 1), :, ds(i * 512 + 256 * s, 256)]
                                         .rearrange("o (k p) n -> p (o k) n", p=P)).then_inc(raw_loaded[s], 16)

            def cache_blocks(L):
                def sequence(b):
                    for i in range(4):
                        after = (b, i + 2) if i < 2 else None if isinstance(b, int) and b == NB - 1 else (b + 1, i - 2)
                        if after:
                            load_block(sp, L, 0, *after, 0)
                        if L:
                            load_block(sp, L, 1, b, i, 0)
                            load_block(sp, L, 1, b, i, 1)
                        if after:
                            load_block(sp, L, 0, *after, 1)

                for i in range(L == 0, 2):
                    for half in range(2):
                        load_block(sp, L, 0, 0, i, half)
                each_sequence(sp, sequence)

            def store_tokens(T, out_p, out_s, g):
                for c in range(5):
                    n = 5 * T + c
                    for kv, done in ((0, tk_done), (1, tv_done)):
                        if not stored[n]:
                            continue
                        sp.wait_ge(done, n + 1)
                        if c < 4:
                            src = k_tok[n % 2][:, :] if kv == 0 else v_all[:, c, :]
                            v = out_p[0, 0].rearrange("t v h e -> t v (h e)")[:, kv, :]
                            if T == 0:
                                dst = v[P * c:P * c + P, :]
                            elif g == 0:
                                dst = v
                            elif g == 1:
                                dst = v.rearrange("(l r) f -> r l f", r=4)[c]
                            else:
                                dst = v.rearrange("(l c r) f -> c r l f", c=4, r=4)[c]
                        else:
                            src = k_tok[n % 2][0:NS, :] if kv == 0 else v_s[0:NS, g, :]
                            v = out_s[0].rearrange("b t v h e -> b t v (h e)")
                            dst = v[:, v.shape[1] - TS:, kv, :]
                        sp.dma_start(dst, src).then_inc(kout[n % 2] if kv == 0 else vout, 16)

            w_ab, w_oa = a["w_in_ab"][0], a["w_out_ab"][0]
            for m, n in enumerate(("norm_mix_g", "norm_mlp_g")):
                sp.dma_start(gain_rows[16 * m:16 * m + 16, :],
                             a[n].rearrange("l (k p) -> (l k) p", p=P)).then_inc(s_gain, 16)
            sp.dma_start(gain_rows[32:40, :], a["norm_out_g"].rearrange("(k p) -> k p", p=P)).then_inc(s_gain, 16)
            sp.dma_start(gain_rows[40:44, :], a["a_scale"][0].rearrange("(k p) -> k p", p=P)).then_inc(s_gain, 16)
            sp.dma_start(gain_rows[44:56, :], a["c_conv_w"][0].rearrange("j (k p) -> (j k) p", p=P)).then_inc(s_gain, 16)
            sp.dma_start(gain_rows[56:57, :], a["b_subln_g"]).then_inc(s_gain, 16)
            sp.dma_start(con[:, :], a["consts"]).then_inc(s_const, 16)
            sp.dma_start(x_tok[:, 0:4, :], a["x_prompt"][0].rearrange("(t p) d -> p t d", p=P)).then_inc(s_x, 16)
            sp.dma_start(x_tok[0:NS, 4, :], a["x_sample"].rearrange("b t d -> (b t) d")).then_inc(s_x, 16)
            unit(w_ab, 0, 0, 0, wait=False)
            unit(w_ab, 256, 1, 1, wait=False)
            sp.dma_start(lam_in[:, :], a["b_lam"][0].rearrange("a d -> (a d)").partition_broadcast(P)).then_inc(s_lam, 16)
            sp.dma_start(hist_tok[0:120, :], a["state_a_pool"][0].rearrange("b t c -> (b t) c")).then_inc(s_hist, 16)
            sp.dma_start(a_mix[:, :].rearrange("p (g d) -> p g d", g=4),
                         a["a_mix"][0].rearrange("g c d -> c g d")).then_inc(s_hist, 16)
            sp.dma_start(pages[0:1, :], a["page_table"].rearrange("(o b) n -> o (b n)", o=1)).then_inc(s_page, 16)
            sp.wait_ge(s_page, 16)
            load_block(sp, 0, 0, 0, 0, 0)
            load_block(sp, 0, 0, 0, 0, 1)
            matrix(w_ab, T_AB, 16, first=1)
            unit(w_oa, 0, T_OA // 2, 0)
            unit(w_oa, 256, T_OA // 2 + 1, 1)
            sp.wait_ge(rows_done, 1)
            sp.dma_start(a["new_pool_prompt"][0, 0], e2[0][49:64, :]).then_inc(rows_out, 16)
            sp.dma_start(a["new_pool_sample"][0][:, 7:15, :], e2[0][NS:P, :]).then_inc(rows_out, 16)
            store_tokens(0, a["new_bkv_prompt"], a["new_bkv_sample"], 0)
            sp.wait_ge(tile_done, T_AB + 16)
            cache_blocks(0)
            unit(w_oa, 512, T_OA // 2 + 2, 0)
            unit(w_oa, 768, T_OA // 2 + 3, 1)
            mlp_weights(0, T_M0)
            w_cd, w_oc = a["w_in_cd"][0], a["w_out_cd"][0]
            unit(w_cd, 0, T_CD // 2, 0)
            unit(w_cd, 256, T_CD // 2 + 1, 1)
            sp.wait_ge(b_ready, 8 + 32)
            sp.dma_start(conv_tok[0:16, :], a["state_c_conv"][0].rearrange("b t c -> (b t) c")).then_inc(s_hist, 16)
            for g, (first, end) in enumerate(((1, 7), (7, 10), (10, 12))):
                with sp.Fori(first, end) as i:
                    for s in range(2):
                        unit(w_cd, i * 512 + 256 * s, i * 2 + T_CD // 2 + s, s)
                if g == 0:
                    sp.wait_ge(rows_done, 2)
                    sp.dma_start(a["new_conv_prompt"][0, 0], e2[0][NS - 2:NS, :]).then_inc(rows_out, 16)
                    for j in range(2):
                        sp.dma_start(a["new_conv_sample"][0][:, j, :], e2[0][NS + 6 + j:P:8, :]).then_inc(rows_out, 16)
                store_tokens(1 + g, a[f"new_d{g}_prompt"], a[f"new_d{g}_sample"], g)
            sp.wait_ge(tile_done, T_CD + 48)
            cache_blocks(1)
            sp.wait_ge(SS[1]["fin"], 1)
            unit(w_oc, 0, T_OC // 2, 0)
            unit(w_oc, 256, T_OC // 2 + 1, 1)
            unit(w_oc, 512, T_OC // 2 + 2, 0)
            unit(w_oc, 768, T_OC // 2 + 3, 1)
            mlp_weights(1, T_M1)

            for t in range(5):
                sp.wait_ge(yt_done, t + 1)
                if t < 4:
                    sp.dma_start(a["y_prompt"][0, P * t:P * t + P, :], y_tok[:, t, :]).then_inc(outs[2], 16)
                else:
                    sp.dma_start(a["y_sample"].rearrange("b t d -> (b t) d"), y_tok[0:NS, t, :]).then_inc(outs[2], 16)
            sp.wait_ge(outs[2], 80)
            sp.wait_ge(rows_out, 80)
            sp.wait_ge(vout, 16 * V_STORES[3])
            for i in range(2):
                sp.wait_ge(kout[i], 16 * K_STORES[i])

        @block.tensor
        def _(pe):
            def dense(group, n_groups, m_hi, m_lo, ready, ready_base, hook=None, peel=False):

                def four(G, first):
                    for q in range(4):
                        s = q % 2
                        pe.wait_ge(wlo_ready, G * 4 + (q + 1))
                        pe.wait_ge(acc_free, G * 4 + (q + 1))
                        for k in range(KT_N):
                            if first and q == 0:
                                pe.wait_ge(ready, ready_base + (k + 1))
                            for n, (w, m) in enumerate(((whi_v, m_hi), (whi_v, m_lo), (wlo_v, m_hi))):
                                for h in range(2):
                                    last = pe.matmul(acc_h[s][:, h, :], w[s][:, k, :], m[:, k, NH * h:NH * h + NH],
                                                     start=(k == 0 and n == 0), stop=(k == KT_N - 1 and n == 2))
                        last.then_inc(tile_done, 1)
                        if hook and first and q == 0:
                            hook()

                done = 0
                if peel or n_groups == 1:
                    four(group(0), True)
                    done = 1
                if n_groups - done == 1:
                    four(group(done), done == 0)
                elif n_groups > done:
                    with pe.Fori(done, n_groups) as i:
                        four(group(i), done == 0)

            def mean_square(f):
                def go():
                    pe.wait_ge(sqs_done, 8 * (f + 1))
                    for h in range(2):
                        last = pe.matmul(halves[2][:, h, :], ones, sqsum[:, NH * h:NH * h + NH], start=True, stop=True)
                    last.then_inc(ms_ready, 1)
                return go

            def mlp(L, t0):
                G0, fa, fb = t0 // 4, 8 * (1 + 2 * L), (8, 48)[L]
                dense(lambda i: i + G0, 2, ahk, alk, a_ready, fa, hook=mean_square(1 + 2 * L), peel=True)
                dense(lambda i: i + (G0 + 2), 2, bhk, blk, b_ready, fb)
                with pe.Fori(1, 4) as c:
                    dense(lambda i: c * 4 + (i + G0), 2, ahk, alk, a_ready, fa)
                    dense(lambda i: c * 4 + (i + (G0 + 2)), 2, bhk, blk, b_ready, c * 8 + fb)

            def token_major(T, kb, g):
                for c in range(5):
                    for kv, (ps, done) in enumerate(((tk_ps, tk_done), (tv_ps, tv_done))):
                        bk = bank[4 + c % 2 + 2 * kv]
                        if c >= 2:
                            pe.wait_ge(done, 5 * T + c - 1)
                        rows = P if c < 4 else NS
                        for i in range(4):
                            tile = kb + 4 * kv + i
                            src = proj_cols(pk[:, tile, 0:SEQ], g, c) if c < 4 else pk[:, tile, SEQ:N]
                            last = pe.transpose(bk[0:rows, P * i:P * i + P], src, ident)
                        last.then_inc(ps, 1)

            def rows_of(tile0):
                for i in range(4):
                    last = pe.transpose(bank[7][:, P * i:P * i + P], pk[:, tile0 + i, N - P:N], ident)
                last.then_inc(rows_ps, 1)

            def sample_attention(L, pt, other_work):
                B, S, nb = BLK[L], SS[L], BLK[L]["nb"]

                def keys(b, i, pages):
                    for p in pages[:max(0, B["pages"][i] - pages[0])]:
                        if p % 2 == 0:
                            pe.wait_ge(S[f"k{i % 2}{p // 2}"], loaded(L, b, i, p // 2))
                        if p % 2 == 0:
                            at_least(pe, S["kt_a"], b * B["pa"] + (2 * i + p // 2))
                        else:
                            at_least(pe, S["kt_d"], b * B["pd"] + (2 * i + p // 2))
                        for t in range(4):
                            last = pe.transpose(bank[p % 2][:, P * t:P * t + P],
                                                kring_v[L][i % 2][:, p, P * t:P * t + P], ident)
                        last.then_inc(S["kt_ps"], 1)

                def scores(b, i):
                    if i == 0:
                        pe.wait_ge(S["q"], b * 2 + 2)
                    q = staged[L][b % 2]
                    if i < 4:
                        np_, g = B["pages"][i], B["groups"][i]
                        pe.wait_ge(S["kt_a"], b * B["pa"] + (2 * i + (np_ + 1) // 2))
                        if np_ > 1:
                            pe.wait_ge(S["kt_d"], b * B["pd"] + (2 * i + np_ // 2))
                        for t in range(4):
                            last = pe.matmul(SCORES[32 * t:32 * t + 32, 0:P * np_], q[:, g, t, :],
                                             kt_sa[L][i % 2][:, t, 0:np_, :], start=True, stop=True)
                    for at_, _, _, g in chunks(B, i):
                        for t in range(4 if g is not None else 0):
                            last = pe.matmul(SCORES[32 * t:32 * t + 32, at_:at_ + NS], q[:, g, t, :], k_s[:, g, t, :],
                                             start=True, stop=True)
                    last.then_inc(S["s"], 1)

                def weights(b, i):
                    pe.wait_ge(S["e"], b * nb + (i + 1))
                    for n, (at_, _, _, _) in enumerate(chunks(B, i)):
                        last = pe.transpose(WEIGHTS[:, P * n:P * n + P],
                                            e_sa[L][i % 2][:, at_:at_ + P], ident)
                    last.then_inc(S["pt_ps"], 1)

                def values(b, i):
                    pe.wait_ge(S["pt"], b * nb + (i + 1))
                    at_least(pe, S["o"], b * nb + i)
                    parts = chunks(B, i)
                    for n, (_, w, p, g) in enumerate(parts):
                        if p is None:
                            v = v_s[0:NS, g, :]
                        else:
                            v = vring_v[L][i % 2][:, p, :]
                            if p % 2 == 0:
                                pe.wait_ge(S[f"v{i % 2}{p // 2}"], loaded(L, b, i, p // 2))
                        for t in range(4):
                            last = pe.matmul(OUTPUT[32 * t:32 * t + 32, :],
                                             pt[i % 2][0:w, P * n + 32 * t:P * n + 32 * t + 32],
                                             v[:, P * t:P * t + P], start=(n == 0), stop=(n == len(parts) - 1))
                    last.then_inc(S["o_ps"], 1)

                keys(0, 0, (0, 1, 2, 3))
                for b in range(NB):
                    for i in range(nb):
                        scores(b, i)
                        keys_beside(L, b, i, keys, (0, 1))
                        if i:
                            values(b, i - 1)
                        elif b:
                            values(b - 1, nb - 1)
                        keys_beside(L, b, i, keys, (2, 3))
                        other_work(nb * b + i)
                        weights(b, i)
                values(NB - 1, nb - 1)

            def sample_finish(L, orun, stat):
                S = SS[L]
                comb = stat[:, S_COMB:S_COMB + 256].rearrange("p (b c) -> p b c", b=NB)
                pe.wait_ge(S["fin"], 1)
                for b in range(NB):
                    last = pe.matmul(bank[0][:, 32 * b:32 * b + 32], orun[:, P * b:P * b + P], comb[:, b, :],
                                     start=True, stop=True)
                last.then_inc(S["fin_ps"], 1)

            pe.wait_ge(s_const, 16)
            pe.wait_ge(s_gain, 96)
            pe.transpose(bank[7][:, 0:57], gain_rows[0:57, :], ident[0:57, 0:57]).then_inc(gain_ps, 1)
            pe.wait_ge(s_x, 32)
            for k in range(KT_N):
                if k >= 2:
                    pe.wait_ge(x_ready, k - 1)
                for t in range(5):
                    rows = P if t < 4 else NS
                    last = pe.transpose(acc[k % 2][:, P * t:P * t + rows], x_tok[0:rows, t, P * k:P * k + P],
                                        ident[0:rows, 0:rows])
                last.then_inc(xt_ps, 1)

            pe.wait_ge(x_ready, 8)
            dense(lambda i: i, 1, ahk, alk, a_ready, 0, hook=mean_square(0), peel=True)
            pe.wait_ge(s_hist, 32)
            for i in range(4):
                last = pe.transpose(bank[6][:, P * i:P * i + 120], hist_tok[0:120, P * i:P * i + P],
                                    ident[0:120, 0:120])
            last.then_inc(hist_ps, 1)
            pe.wait_ge(acc_free, 2 + T_AB + 4)
            rows_of(0)
            dense(lambda i: i + 1, 3, ahk, alk, a_ready, 0)
            pe.wait_ge(acc_free, 2 + T_AB + 16)
            pe.wait_ge(hist_done, 1)
            pe.wait_ge(rows_done, 1)
            token_major(0, 8, 0)

            def prompt_stage(s):
                if s < 16:
                    h, qt = s // 4, s % 4
                    if s >= 1:
                        pe.wait_ge(p0_e, s)
                    for m in range(2):
                        last = pe.matmul(P0_SCORES[:, 512 * m:512 * m + P * (qt + 1)],
                                         pk[64 * m:64 * m + 64, 4 + h, P * qt:P * qt + P],
                                         pk[64 * m:64 * m + 64, 8 + h, 0:P * (qt + 1)], start=True, stop=True)
                    last.then_inc(p0_s, 1)
                if s >= 1:
                    n = s - 1
                    qt = n % 4
                    pe.wait_ge(p0_a, n + 1)
                    if n >= 1:
                        pe.wait_ge(p0_o, n)
                    for kb in range(qt + 1):
                        last = pe.transpose(P0_WEIGHTS[:, P * kb:P * kb + P], e4[n % 2][0][:, P * kb:P * kb + P], ident)
                    last.then_inc(p0_t, 1)

            def prompt_product(n):
                h, qt = n // 4, n % 4
                pe.wait_ge(p0_at, n + 1)
                for kb in range(qt + 1):
                    last = pe.matmul(P0_OUTPUT, v_all[:, kb, P * h:P * h + P], pt_p0[n % 2][:, P * kb:P * kb + P],
                                     start=(kb == 0), stop=(kb == qt))
                last.then_inc(p0_pv, 1)

            def mixer_product(g):
                pe.wait_ge(pm_ready, g + 1)
                if g == 0:
                    pe.wait_ge(p0_e, 16)
                else:
                    pe.wait_ge(mix_done, g)
                for h in range(2):
                    last = pe.matmul(halves[2][:, h, :], a_mix[:, P * g:P * g + P], pk[:, g, NH * h:NH * h + NH],
                                     start=True, stop=True)
                last.then_inc(mix_ps, 1)

            def prompt_work(m):
                beside(m, 1, prompt_stage, 16)
                beside(m, 4, prompt_product, 15)
                if 35 <= m < 39:
                    mixer_product(m - 35)

            pe.wait_ge(q_scaled, 1)
            pe.wait_ge(tk_done, 5)
            pe.wait_ge(tv_done, 5)
            sample_attention(0, pt_l0, prompt_work)
            sample_finish(0, orun0, samp[0])

            for h in range(4):
                pe.wait_ge(sub_sq, h + 1)
                sq = zbuf[:, N * (h % 2):N * (h % 2) + N]
                for t in range(4):
                    pe.matmul(bank[7][:, 4 * t + h:4 * t + h + 1], sq[:, P * t:P * t + P], ones[:, 0:1],
                              start=True, stop=True)
                for r in (0, NS):
                    last = pe.matmul(bank[7][r:r + NS, 16 + h:17 + h], sq[:, SEQ:N], ones[:, 0:1],
                                     start=True, stop=True)
                last.then_inc(sub_ms, 1)
            pe.wait_ge(mix_done, 4)
            for h in range(4):
                pe.wait_ge(sub_d, h + 1)
                if h >= 2:
                    pe.wait_ge(sub_t, h - 1)
                d = sqbuf[:, N * (h % 2):N * (h % 2) + N]
                pe.matmul(pp[1 + h % 2][:, 0:SEQ], ones, d[:, 0:SEQ], start=True, stop=True)
                pe.matmul(pp[1 + h % 2][:, SEQ:N], ones[0:NS, :], d[0:NS, SEQ:N], start=True,
                          stop=True).then_inc(sub_b, 1)
            pe.wait_ge(sub_t, 3)
            pe.wait_ge(SS[0]["fin_d"], 1)
            dense(lambda i: i + T_OA // 4, 2, bhk, blk, b_ready, 0)
            mlp(0, T_M0)

            dense(lambda i: i + T_CD // 4, 3, ahk, alk, a_ready, 16, hook=mean_square(2), peel=True)
            pe.wait_ge(acc_free, 2 + T_CD + 12)
            pe.wait_ge(s_hist, 48)
            for i in range(4):
                last = pe.transpose(bank[6][:, 16 * i:16 * i + 16], conv_tok[0:16, P * i:P * i + P], ident[0:16, 0:16])
            last.then_inc(hist_ps, 1)

            def conv_rows():
                pe.wait_ge(pm_ready, 5)
                rows_of(4)


            def group_scores(g, it, bk):
                _, c, par, kc, _ = items1[it]
                for t in range(4):
                    r = 64 * par
                    last = pe.matmul(bk[:, P * t:P * t + P], proj_cols(pk[r:r + 64, t, 0:SEQ], g, c),
                                     proj_cols(pk[r:r + 64, 4 + t, 0:SEQ], g, kc), start=True, stop=True)
                last.then_inc(p1_s, 1)

            def group_weights(it, bk):
                pe.wait_ge(p1_e, it + 1)
                for t in range(4):
                    last = pe.transpose(bk[:, P * t:P * t + P], e_p1[it % 3][:, P * t:P * t + P], ident)
                last.then_inc(p1_t, 1)

            def group_product(g, n, bk):
                c, par, its = units1[g][n]
                pe.wait_ge(p1_pt, its[-1] + 1)
                for t in range(4):
                    head, r = 2 * t + par, 64 * par
                    for k, it in enumerate(its):
                        last = pe.matmul(bk[r:r + 64, P * t:P * t + P], v_all[:, items1[it][3], 64 * head:64 * head + 64],
                                         pt_l1[it % 2][:, P * t:P * t + P], start=(k == 0), stop=(k == len(its) - 1))
                last.then_inc(p1_pv, 1)

            for g in range(3):
                dense(lambda i: i + (T_CD // 4 + 3 + 3 * g), 3, ahk, alk, a_ready, 16,
                      hook=conv_rows if g == 0 else None, peel=(g == 0))
                pe.wait_ge(acc_free, 2 + T_CD + 12 * (g + 2))
                if g == 0:
                    pe.wait_ge(hist_done, 2)
                    pe.wait_ge(rows_done, 2)
                else:
                    pe.wait_ge(p1_o, 4 * g)
                token_major(1 + g, 4, g)
                pe.wait_ge(q_scaled, 2 + g)
                for s in range(8 + 3 if g < 2 else 0):
                    if s < 8:
                        for it in units1[g][s][2]:
                            if it >= 4:
                                pe.wait_ge(p1_e, it - 3)
                            group_scores(g, it, bank[it % 4])
                    if 2 <= s < 10:
                        for it in units1[g][s - 2][2]:
                            if it >= 2:
                                pe.wait_ge(p1_pt, it - 1)
                            group_weights(it, bank[4 + it % 2])
                    if s >= 3:
                        u = 8 * g + s - 3
                        if s == 3:
                            pe.wait_ge(tk_done, 5 * (2 + g))
                            pe.wait_ge(tv_done, 5 * (2 + g))
                        if u >= 4 and u % 2 == 0:
                            pe.wait_ge(p1_o, u // 2 - 1)
                        group_product(g, s - 3, bank[6 + u // 2 % 2])

            def prompt_stage(s):
                if s < 8:
                    it = units1[2][s][2][0]
                    pe.wait_ge(p1_e, it)
                    group_scores(2, it, P1_SCORES)
                if s >= 1:
                    it = units1[2][s - 1][2][0]
                    pe.wait_ge(p1_pt, it)
                    group_weights(it, P1_WEIGHTS)

            def prompt_product(n):
                if n % 2 == 0:
                    pe.wait_ge(p1_o, 8 + n // 2)
                group_product(2, n, P1_OUTPUT)

            def statistics(n):
                if n == 0:
                    pe.wait_ge(p1_o, 12)
                    pe.wait_ge(cb_t, 1)
                else:
                    pe.wait_ge(cb_v, 1)
                for g in range(3):
                    for c in range(4):
                        last = pe.transpose(CB_BANKS[g][0:8, P * c:P * c + P], (neg1, sum1)[n][:, g, c, :], ident)
                last.then_inc(cb_d, 1)

            def factors(t):
                pe.wait_ge(cb_c, 1)
                if t:
                    pe.wait_ge(cb_u, t)
                for g in range(3):
                    last = pe.matmul(CB_BANKS[g][:, :], cc("sel8")[0:8, P * t:P * t + P], nm[g][0:8, :],
                                     start=True, stop=True)
                last.then_inc(cb_ps, 1)

            def prompt_work(m):
                beside(m, 1, prompt_stage, 8)
                beside(m, 4, prompt_product, 7)
                if m in (20, 21):
                    statistics(m - 20)
                beside(m, 25, factors, 3)

            pe.wait_ge(tk_done, 20)
            pe.wait_ge(tv_done, 20)
            pe.wait_ge(p1_e, units1[2][0][2][0])
            pe.wait_ge(p1_pt, units1[2][0][2][0])
            sample_attention(1, pt_s1, prompt_work)
            pe.wait_ge(cb_u, 4)
            sample_finish(1, orun1, samp[1])
            pe.wait_ge(SS[1]["fin_d"], 1)
            dense(lambda i: i + T_OC // 4, 2, bhk, blk, b_ready, 40)
            mlp(1, T_M1)

            def transpose_result(t):
                rows = P if t < 4 else NS
                if t >= 3:
                    pe.wait_ge(yt_done, t - 2)
                for k in range(KT_N):
                    pe.wait_ge(y_ready, k + 1)
                    last = pe.transpose(y_ps[t][0:rows, P * k:P * k + P],
                                        y_feat[:, N * k + P * t:N * k + P * t + rows], ident)
                last.then_inc(yt_ps, 1)

            transpose_result(0)
            pe.wait_ge(sqs_done, 8 * 5)
            for t in range(5):
                rows = P if t < 4 else NS
                last = pe.matmul(bank[4][0:rows, t:t + 1], sqsum[:, P * t:P * t + rows], ones[:, 0:1],
                                 start=True, stop=True)
            last = pe.matmul(bank[4][NS:P, 4:5], sqsum[:, SEQ:N], ones[:, 0:1], start=True, stop=True)
            last.then_inc(ms_ready, 1)
            pe.wait_ge(acc_free, 2 + T_END)
            for t in range(1, 5):
                transpose_result(t)

        @block.vector
        def _(dve):
            steps = Tally()

            def link(ins):
                ins.then_inc(dve_step, 1)
                dve.wait_ge(dve_step, steps.add())

            def split_lo(G, q):
                j = q % 2
                dve.wait_ge(whi_ready, G * 4 + (q + 1))
                dve.tensor_tensor(wlo_v[j], raw_v[q // 2][:, :, j, :], whi_v[j].bitcast(F32),
                                  ALU.subtract).then_inc(wlo_ready, 1)

            def dense(group, n_groups, evac, post=None, peel=False, hook=None, static=False, last=False):
                def four(G, i):
                    for q in range(4):
                        dve.wait_ge(tile_done, G * 4 + (q + 1))
                        if hook and q == 0 and isinstance(i, int) and i == 0:
                            hook()
                        evac(G, i, q)
                        if not (last and q >= 2 and i == n_groups - 1):
                            split_lo(*((G, q + 2) if q < 2 else (G + 1, q - 2)))
                        if post:
                            post(G, i, q)
                done = 0
                while done < n_groups and (static or n_groups - done == 1 or (peel and done == 0)):
                    four(group(done), done)
                    done += 1
                if done < n_groups:
                    with dve.Fori(done, n_groups) as i:
                        four(group(i), i)

            def rms(f):
                def go():
                    dve.wait_ge(ms_ready, f + 1)
                    dve.tensor_scalar(r_h, halves[2], 1.0 / D, EPS, ALU.mult, ALU.add).then_inc(v_ready, 1)
                    dve.wait_ge(sqrt_ready, f + 1)
                    link(dve.reciprocal(rnorm[:, :], rnorm[:, :]))
                return go

            def to_proj(group0=0):
                def evac(G, i, q):
                    dst = proj[:, ds(i * (4 * N) + (4 * group0 + q) * N, N)].rearrange("p (h c) -> p h c", h=2)
                    dve.tensor_tensor(dst, acc_h[q % 2], r_h, ALU.mult).then_inc(acc_free, 1)
                return evac

            def to_proj_streams(group0=0):
                L0 = NH // 16

                def evac(G, i, q):
                    dst = proj[:, ds(i * (4 * N) + (4 * group0 + q) * N, N)]
                    dp = dst[:, 0:SEQ].rearrange("p (r l) -> p r l", r=16)
                    rl = lambda v: v.rearrange("p (l r) -> p r l", r=16)
                    a0, a1 = acc_h[q % 2][:, 0, :], acc_h[q % 2][:, 1, :]
                    dve.tensor_tensor(dp[:, :, 0:L0], rl(a0), rl(rnorm[:, 0:NH]), ALU.mult)
                    dve.tensor_tensor(dp[:, :, L0:32], rl(a1[:, 0:SEQ - NH]), rl(rnorm[:, NH:SEQ]), ALU.mult)
                    dve.tensor_tensor(dst[:, SEQ:N], a1[:, SEQ - NH:NH], rnorm[:, SEQ:N], ALU.mult).then_inc(acc_free, 1)
                return evac

            def up(G, i, q):
                j = q % 2
                z = zbuf[:, N * j:N * j + N]
                dve.tensor_tensor(z.rearrange("p (h c) -> p h c", h=2), acc_h[j], r_h, ALU.mult).then_inc(acc_free, 1)
                dve.wait_ge(acc_free, G * 4 + (q + 3))
                dve.scalar_tensor_tensor(out=sqbuf[:, N * j:N * j + N], in0=z, scalar=0.0, in1=z, op0=ALU.max,
                                         op1=ALU.mult).then_inc(sq_up, 1)

            def up_post(b0):
                def post(G, i, q):
                    dve.wait_ge(bhi_ready, b0 + i * 4 + (q + 1))
                    at_ = ds(i * (4 * N) + q * N, N)
                    dve.tensor_tensor(b_lo[:, at_], sqbuf[:, N * (q % 2):N * (q % 2) + N], b_hi[:, at_].bitcast(F32),
                                      ALU.subtract).then_inc(b_ready, 1)
                return post

            def down(G, i, q):
                xt = x[:, ds(i * (4 * N) + q * N, N)].rearrange("p (h c) -> p h c", h=2)
                dve.tensor_tensor(xt, xt, acc_h[q % 2], ALU.add).then_inc(acc_free, 1)

            def fin_post(f, gcol):
                def post(G, i, q):
                    k = 4 * i + q
                    dve.wait_ge(ahi_ready, 8 * f + k + 1)
                    dve.scalar_tensor_tensor(out=alk[:, k, :], in0=xk[:, k, :], scalar=gains[:, gcol + k:gcol + k + 1],
                                             in1=ahk[:, k, :].bitcast(F32), op0=ALU.mult,
                                             op1=ALU.subtract).then_inc(a_ready, 1)
                return post

            def result_post(G, i, q):
                k = 4 * i + q
                dve.wait_ge(acc_free, 2 + T_M1 + 56 + k + 1)
                dve.tensor_scalar(y_feat[:, N * k:N * k + N], xk[:, k, :], gains[:, G_OUT + k:G_OUT + k + 1], None,
                                  ALU.mult).then_inc(y_ready, 1)

            def mlp(L, t0):
                G0, fb = t0 // 4, (8, 48)[L]
                dense(lambda i: i + G0, 2, up, up_post(fb), peel=True, hook=rms(1 + 2 * L))
                dense(lambda i: i + (G0 + 2), 2, down)
                with dve.Fori(1, 3) as c:
                    dense(lambda i: c * 4 + (i + G0), 2, up, up_post(c * 8 + fb))
                    dense(lambda i: c * 4 + (i + (G0 + 2)), 2, down)
                dense(lambda i: i + (G0 + 12), 2, up, up_post(24 + fb))
                if L == 0:
                    dense(lambda i: i + (G0 + 14), 2, down, fin_post(2, G_MIX + 8), static=True)
                else:
                    dense(lambda i: i + (G0 + 14), 2, down, result_post, static=True, last=True)

            def token_major(T, g):
                for c in range(5):
                    dve.wait_ge(tv_ps, 5 * T + c + 1)
                    if c == 0 and T:
                        dve.wait_ge(vout, 16 * V_STORES[T - 1])
                    dst, rows = (v_all[:, c, :], P) if c < 4 else (v_s[0:NS, g, :], NS)
                    dve.tensor_copy(dst, bank[6 + c % 2][0:rows, :]).then_inc(tv_done, 1)

            def sample_attention(L, orun, stat, other_work):
                B, S, nb = BLK[L], SS[L], BLK[L]["nb"]
                neg = lambda i: stat[:, S_NEG + i:S_NEG + i + 1]
                tmp = stat[:, S_TMP:S_TMP + 1]
                ob, run = stat[:, 300:428], stat[:, 510:511]

                def keys(b, i, pages):
                    for p in pages:
                        if p >= B["pages"][i]:
                            continue
                        dve.wait_ge(S["kt_ps"], b * B["pn"] + (4 * i + p + 1))
                        dve.tensor_copy(kt_sa[L][i % 2][:, :, p, :], bank[1].rearrange("p (i n) -> p i n", i=4)
                                        ).then_inc(S["kt_d"], 1)

                def maximum(b, i):
                    dve.wait_ge(S["s"], b * nb + (i + 1))
                    sb, w = SCORES, B["cols"][i]
                    if i < 4 and B["mask"][i]:
                        m = B["mask"][i]
                        sv = sb[:, 0:P * B["pages"][i]].rearrange("p (g n) -> p g n", n=P)
                        if m == "g0m":
                            link(dve.tensor_tensor(sb[:, 0:8], sb[:, 0:8], cc("g0m"), ALU.add))
                        else:
                            rm = {"rm2a": cc("rm2")[:, 0:4], "rm2b": cc("rm2")[:, 4:8], "rm1": cc("rm1")}[m]
                            link(dve.tensor_tensor(sv, sv, rm.unsqueeze(2).broadcast_to([P, 4, P]), ALU.add))
                            if m == "rm1":
                                link(dve.tensor_tensor(sv[:, :, 0], sv[:, :, 0], cc("k01"), ALU.add))
                    if i == nb - 1:
                        sv = sb[:, B["new_at"]:w].rearrange("p (g n) -> p g n", n=NS)
                        mv = cc("selfm").rearrange("p (g n) -> p g n", g=3)
                        link(dve.tensor_tensor(sv, sv, mv[:, 0:B["new"], ds(b * (-8) + 56, NS)], ALU.add))
                    if i == 0:
                        dve.tensor_reduce(neg(0), sb[:, 0:w], AX.X, ALU.max, negate=True).then_inc(S["neg"], 1)
                    else:
                        link(dve.tensor_reduce(tmp, sb[:, 0:w], AX.X, ALU.max, negate=True))
                        dve.wait_ge(S["neg"], b * nb + i)
                        dve.tensor_tensor(neg(i), tmp, neg(i - 1), ALU.min).then_inc(S["neg"], 1)

                def output(b, i):
                    al = stat[:, S_ALPHA + i:S_ALPHA + i + 1]
                    su = stat[:, S_SUM + i:S_SUM + i + 1]
                    dve.wait_ge(S["o_ps"], b * nb + (i + 1))
                    pv = OUTPUT
                    rdst = run if i < nb - 1 else stat[:, ds(b + S_RUN, 1)]
                    odst = ob if i < nb - 1 else orun[:, ds(b * P, P)]
                    at_least(dve, S["o"], b * nb + i)
                    if i == 0:
                        link(dve.tensor_copy(run, su))
                        dve.tensor_copy(ob, pv).then_inc(S["o"], 1)
                    else:
                        link(dve.scalar_tensor_tensor(out=rdst, in0=run, scalar=al, in1=su, op0=ALU.mult, op1=ALU.add))
                        dve.scalar_tensor_tensor(out=odst, in0=ob, scalar=al, in1=pv, op0=ALU.mult,
                                                 op1=ALU.add).then_inc(S["o"], 1)

                keys(0, 0, (1, 3))
                for b in range(NB):
                    for i in range(nb):
                        maximum(b, i)
                        keys_beside(L, b, i, keys, (1,))
                        if i:
                            output(b, i - 1)
                        elif b:
                            output(b - 1, nb - 1)
                        keys_beside(L, b, i, keys, (3,))
                        other_work(nb * b + i)
                output(NB - 1, nb - 1)

            def sample_finish(L, orun, stat, o_feat):
                S = SS[L]
                rec = stat[:, S_REC:S_REC + 8]
                comb = stat[:, S_COMB:S_COMB + 256].rearrange("p (b c) -> p b c", b=NB)
                dve.wait_ge(S["o"], BLK[L]["nb"] * NB)
                link(dve.reciprocal(rec, stat[:, S_RUN:S_RUN + 8]))
                if L == 0:
                    link(dve.tensor_scalar(rec, rec, neglam[:, 1:2], None, ALU.mult))
                else:
                    ov = orun[:, :].rearrange("p (b e) -> p b e", b=NB)
                    for hf in range(2):
                        o2 = ov[:, :, 64 * hf:64 * hf + 64]
                        link(dve.tensor_scalar(o2, o2, cc("halfm")[:, hf:hf + 1], None, ALU.mult))
                dve.tensor_tensor(comb, cc("sel").unsqueeze(1).broadcast_to([P, NB, 32]),
                                  rec.unsqueeze(2).broadcast_to([P, NB, 32]), ALU.mult).then_inc(S["fin"], 1)
                dve.wait_ge(S["fin_ps"], 1)
                for t in range(4):
                    last = dve.tensor_copy(o_feat[:, t, SEQ:N].rearrange("p (b t) -> p b t", b=NB),
                                           bank[0][:, 0:256].rearrange("p (b i t) -> p b i t", b=NB, i=4)[:, :, t, :])
                last.then_inc(S["fin_d"], 1)

            dve.wait_ge(gain_ps, 1)
            dve.tensor_copy(gains[:, 0:57], bank[7][:, 0:57]).then_inc(gain_ready, 1)
            dve.wait_ge(s_const, 16)
            dve.tensor_scalar(dummy[:, :], cc("ones")[:, 0:1], 1.0, None, ALU.mult).then_inc(acc_free, 2)
            for k in range(KT_N + 1):
                if k < KT_N:
                    dve.wait_ge(xt_ps, k + 1)
                    dve.tensor_copy(xk[:, k, :], acc[k % 2][:, 0:N]).then_inc(x_ready, 1)
                if k >= 1:
                    fin_post(0, G_MIX)(0, 0, k - 1)
                if k in (5, 7):
                    split_lo(0, k // 2 - 2)

            dve.wait_ge(s_lam, 16)
            lv = lam_in[:, :].rearrange("p (m s d) -> p m s d", m=2, s=2)
            lt = lam_t[:, 0:128].rearrange("p (m d) -> p m d", m=2)
            link(dve.tensor_tensor(lt, lv[:, :, 0, :], lv[:, :, 1, :], ALU.mult))
            dve.tensor_reduce(lam_t[:, 128:130], lt, AX.X, ALU.add).then_inc(lam_d, 1)
            dve.wait_ge(lam_e, 1)
            link(dve.tensor_tensor(neglam[:, 0:1], lam_t[:, 131:132], lam_t[:, 130:131], ALU.subtract))
            link(dve.tensor_scalar(neglam[:, 0:1], neglam[:, 0:1], -LAM_INIT, None, ALU.add))
            link(dve.scalar_tensor_tensor(out=neglam[:, 1:2], in0=cc("halfm")[:, 1:2], scalar=neglam[:, 0:1],
                                          in1=cc("halfm")[:, 0:1], op0=ALU.mult, op1=ALU.add))

            dense(lambda i: i, 1, to_proj(), peel=True, hook=rms(0))
            dve.wait_ge(hist_ps, 1)
            dve.tensor_copy(hist_f.rearrange("p g b c -> p g (b c)"),
                            bank[6].rearrange("p (g w) -> p g w", g=4)[:, :, 0:120]).then_inc(hist_done, 1)
            dve.wait_ge(rows_ps, 1)
            dve.tensor_copy(e2[0][:, :], bank[7]).then_inc(rows_done, 1)
            dense(lambda i: i + 1, 3, to_proj(1))
            dve.wait_ge(acc_free, 2 + T_AB + 16)
            dve.tensor_scalar(proj[:, 4 * N:8 * N], proj[:, 4 * N:8 * N], 0.125, None, ALU.mult).then_inc(q_scaled, 1)
            token_major(0, 0)

            def prompt_stage(s):
                qt, u = s % 4, s % 2
                nk = P * (qt + 1)
                dve.wait_ge(p0_s, s + 1)
                sv = P0_SCORES[:, :].rearrange("p (m n) -> p m n", m=2)
                diag = sv[:, :, P * qt:P * qt + P]
                link(dve.tensor_tensor(diag, diag, cc("causal").unsqueeze(1).broadcast_to([P, 2, P]), ALU.add))
                dve.tensor_reduce(neg0[:, u, :], sv[:, :, 0:nk], AX.X, ALU.max, negate=True).then_inc(p0_m, 1)

            def prompt_output(n):
                h, qt = n // 4, n % 4
                dve.wait_ge(p0_pv, n + 1)
                dve.tensor_copy(o_feat0[:, N * h + P * qt:N * h + P * qt + P], P0_OUTPUT).then_inc(p0_o, 1)

            def prompt_combine(n):
                u, nk = n % 2, P * (n % 4 + 1)
                dve.wait_ge(p0_e, n + 1)
                link(dve.reciprocal(rs0[:, u, :], sum0[:, u, :]))
                link(dve.tensor_scalar(rs0[:, u, 1:2], rs0[:, u, 1:2], neglam[:, 0:1], None, ALU.mult))
                e0, e1 = e4[u][0][:, 0:nk], e4[u][1][:, 0:nk]
                link(dve.tensor_scalar(e0, e0, rs0[:, u, 0:1], None, ALU.mult))
                dve.scalar_tensor_tensor(out=e0, in0=e1, scalar=rs0[:, u, 1:2], in1=e0, op0=ALU.mult,
                                         op1=ALU.add).then_inc(p0_a, 1)

            dve.wait_ge(q_scaled, 1)
            def prompt_work(m):
                beside(m, 1, prompt_stage, 15)
                beside(m, 2, prompt_combine, 15)
                beside(m, 4, prompt_output, 15)

            sample_attention(0, orun0, samp[0], prompt_work)
            of0 = tiles(o_feat0, 4)
            sample_finish(0, orun0, samp[0], of0)

            for g in range(4):
                dve.wait_ge(bhi_ready, g + 1)
                dve.tensor_tensor(blk[:, g, :], pk[:, g, :], bhk[:, g, :].bitcast(F32), ALU.subtract).then_inc(b_ready, 1)

            dve.wait_ge(p0_o, 16)
            dve.wait_ge(sub_ms, 4)
            dve.tensor_scalar(r_head, bank[7][:, 0:20], 1.0 / P, EPS, ALU.mult, ALU.add).then_inc(sub_v, 1)
            dve.wait_ge(sub_r, 1)
            link(dve.reciprocal(r_head, r_head))
            link(dve.tensor_scalar(r_head, r_head, 1.0 - LAM_INIT, None, ALU.mult))

            def diagonal(h):
                d = sqbuf[:, N * (h % 2):N * (h % 2) + N]
                dve.tensor_tensor(d[:, 0:SEQ].rearrange("p (t n) -> p t n", t=4),
                                  ident.unsqueeze(1).broadcast_to([P, 4, P]),
                                  r_head[:, h:16:4].unsqueeze(2).broadcast_to([P, 4, P]), ALU.mult)
                dve.tensor_scalar(d[0:NS, SEQ:N], ident[0:NS, 0:NS], r_head[0:NS, 16 + h:17 + h], None,
                                  ALU.mult).then_inc(sub_d, 1)

            diagonal(0)
            diagonal(1)
            for h in range(4):
                t1 = zbuf[:, N * (h % 2):N * (h % 2) + N]
                dve.wait_ge(sub_b, h + 1)
                dve.scalar_tensor_tensor(out=t1, in0=of0[:, h, :], scalar=gains[:, G_SUBLN:G_SUBLN + 1],
                                         in1=pp[1 + h % 2][:, 0:N], op0=ALU.mult, op1=ALU.mult).then_inc(sub_t, 1)
                if h < 2:
                    diagonal(h + 2)
                dve.wait_ge(bhi_ready, 5 + h)
                dve.tensor_tensor(blk[:, 4 + h, :], t1, bhk[:, 4 + h, :].bitcast(F32), ALU.subtract).then_inc(b_ready, 1)

            dense(lambda i: i + T_OA // 4, 2, down, fin_post(1, G_MLP), static=True)
            mlp(0, T_M0)

            dense(lambda i: i + T_CD // 4, 3, to_proj(), peel=True, hook=rms(2))
            dve.wait_ge(acc_free, 2 + T_CD + 12)
            link(dve.tensor_tensor(proj[:, 4 * N:8 * N], proj[:, 4 * N:8 * N], proj[:, 8 * N:12 * N], ALU.mult))
            dve.wait_ge(hist_ps, 2)
            dve.tensor_copy(zext[:, :, :, 0:2], bank[6][:, 0:64].rearrange("p (k b c) -> p k b c", k=4, b=NB)
                            ).then_inc(hist_done, 1)
            dve.wait_ge(hist_done, 2)
            for k in range(4):
                link(dve.tensor_copy(zext[:, k, :, 2:10], pk[:, 4 + k, SEQ:N].rearrange("p (b c) -> p b c", b=NB)))
            dve.tensor_copy(dummy[:, :], cc("ones")[:, 0:1]).then_inc(pm_ready, 1)
            for k in range(4):
                w = [gains[:, G_CONV + 4 * j + k:G_CONV + 4 * j + k + 1] for j in range(3)]
                z, y = pk[:, 4 + k, :], cv[:, N * k:N * k + N]
                ys = y[:, SEQ:N].rearrange("p (b c) -> p b c", b=NB)
                link(dve.tensor_scalar(y, z, w[2], None, ALU.mult))
                for j in (1, 0):
                    d = 2 - j
                    dve.scalar_tensor_tensor(out=ys, in0=zext[:, k, :, j:j + 8], scalar=w[j], in1=ys, op0=ALU.mult,
                                             op1=ALU.add)
                    link(dve.scalar_tensor_tensor(out=y[:, d:SEQ], in0=z[:, 0:SEQ - d], scalar=w[j], in1=y[:, d:SEQ],
                                                  op0=ALU.mult, op1=ALU.add))
                dve.tensor_tensor(y, y, pk[:, k, :], ALU.mult).then_inc(sub_t, 1)
            dve.wait_ge(rows_ps, 2)
            dve.tensor_copy(e2[0][:, :], bank[7]).then_inc(rows_done, 1)

            def group_maximum(g, n, scores):
                c, par, its = units1[g][n]
                d = neg1[:, g, c, 4 * par:4 * par + 4]
                for k, it in enumerate(its):
                    dve.wait_ge(p1_s, it + 1)
                    sv = scores(it).rearrange("p (h n) -> p h n", h=4)
                    link(dve.tensor_tensor(sv, sv, cc(items1[it][4]).unsqueeze(1).broadcast_to([P, 4, P]), ALU.add))
                    ins = dve.tensor_reduce(d if k == 0 else negp[:, c, 4 * par:4 * par + 4], sv, AX.X, ALU.max,
                                            negate=True)
                    if len(its) == 1:
                        ins.then_inc(p1_m, 1)
                    else:
                        link(ins)
                if len(its) == 2:
                    dve.tensor_tensor(d, d, negp[:, c, 4 * par:4 * par + 4], ALU.min).then_inc(p1_m, 1)

            def group_output(g, n, bk):
                dve.wait_ge(p1_pv, 8 * g + n + 1)
                src = bk.rearrange("p (i n) -> p i n", i=4)
                og = tiles(o_g[g], 4)
                for i in range(4):
                    dst, sr = tok_cols(og[:, i, 0:SEQ], g, units1[g][n][0]), src[:, i, :]
                    if g == 2:
                        sr = sr.rearrange("p (r l) -> p r l", r=4)
                    last = dve.tensor_copy(dst, sr)
                last.then_inc(p1_o, 1)

            for g in range(3):
                if g:
                    dve.wait_ge(qs_saved, 2 * (g + 1))
                if g < 2:
                    dense(lambda i: i + (T_CD // 4 + 3 + 3 * g), 3, to_proj())
                    for k in range(4 if g == 0 else 0):
                        dve.wait_ge(bhi_ready, 40 + k + 1)
                        dve.tensor_tensor(blk[:, k, :], cv[:, N * k:N * k + N], bhk[:, k, :].bitcast(F32),
                                          ALU.subtract).then_inc(b_ready, 1)
                    if g == 0:
                        dve.wait_ge(b_ready, 44)
                else:
                    dense(lambda i: i + (T_CD // 4 + 9), 2, to_proj_streams())
                    dense(lambda i: i + (T_CD // 4 + 11), 1, to_proj_streams(2), last=True)
                dve.wait_ge(acc_free, 2 + T_CD + 12 * (g + 2))
                dve.tensor_scalar(proj[:, 0:4 * N], proj[:, 0:4 * N], 0.125, None, ALU.mult).then_inc(q_scaled, 1)
                token_major(1 + g, g)
                if g == 0:
                    dve.wait_ge(rows_out, 80)
                for s in range(8 + 3 if g < 2 else 0):
                    if s < 8:
                        group_maximum(g, s, lambda it: bank[it % 4])
                    if s >= 4 and s % 2 == 0:
                        group_output(g, s - 3, bank[6 + (8 * g + s - 3) // 2 % 2])

            low = e2[0][0:8, :]

            def total_sums():
                dve.wait_ge(p1_e, len(items1))
                s0 = sum1[:, 0, 1:4, :]
                dve.tensor_tensor(s0, s0, sump[:, 1:4, :], ALU.add).then_inc(cb_t, 1)

            def statistics(n):
                dve.wait_ge(cb_d, n + 1)
                if n == 0:
                    dve.wait_ge(p1_pv, 24)
                    dve.wait_ge(vout, 16 * V_STORES[3])
                    for i in range(2):
                        dve.wait_ge(kout[i], 16 * K_STORES[i])
                dst = (nm, sm)[n]
                for g in range(3):
                    src = CB_BANKS[g][0:8, :].rearrange("p (c n) -> p c n", c=4)
                    for c in range(4):
                        d, s_ = tok_cols(dst[g][0:8, :], g, c), src[:, c, :]
                        if g == 2:
                            s_ = s_.rearrange("p (r l) -> p r l", r=4)
                        last = dve.tensor_copy(d, s_)
                last.then_inc(cb_v, 1)

            def relative():
                dve.wait_ge(cb_v, 2)
                link(dve.tensor_tensor(low, nm[0][0:8, :], nm[1][0:8, :], ALU.min))
                link(dve.tensor_tensor(low, low, nm[2][0:8, :], ALU.min))
                for g in range(3):
                    last = dve.tensor_tensor(nm[g][0:8, :], low, nm[g][0:8, :], ALU.subtract)
                last.then_inc(cb_x, 1)

            def group_factors():
                dve.wait_ge(cb_e, 3)
                for g in range(3):
                    last = dve.tensor_tensor(sm[g][0:8, :], sm[g][0:8, :], nm[g][0:8, :], ALU.mult)
                link(last)
                link(dve.tensor_tensor(low, sm[0][0:8, :], sm[1][0:8, :], ALU.add))
                link(dve.tensor_tensor(low, low, sm[2][0:8, :], ALU.add))
                link(dve.reciprocal(low, low))
                for g in range(3):
                    last = dve.tensor_tensor(nm[g][0:8, :], nm[g][0:8, :], low, ALU.mult)
                last.then_inc(cb_c, 1)

            of1 = tiles(o_g[0], 4)

            def combine(t):
                dve.wait_ge(cb_ps, t + 1)
                for g in range(3):
                    o = tiles(o_g[g], 4)[:, t, 0:SEQ]
                    last = dve.tensor_tensor(o, o, CB_BANKS[g][:, :], ALU.mult)
                last.then_inc(cb_u, 1)
                dve.wait_ge(cb_u, t + 1)
                o = of1[:, t, 0:SEQ]
                link(dve.tensor_tensor(o, o, tiles(o_g[1], 4)[:, t, 0:SEQ], ALU.add))
                link(dve.tensor_tensor(o, o, tiles(o_g[2], 4)[:, t, 0:SEQ], ALU.add))

            def prompt_work(m):
                beside(m, 1, lambda s: group_maximum(2, s, lambda it: P1_SCORES), 7)
                beside(m, 6, lambda s: s % 2 or group_output(2, s + 1, P1_OUTPUT), 6)
                if m == 19:
                    total_sums()
                if m in (20, 21):
                    statistics(m - 20)
                if m == 22:
                    relative()
                if m == 24:
                    group_factors()
                beside(m, 25, combine, 3)

            dve.wait_ge(qs_saved, 8)
            sample_attention(1, orun1, samp[1], prompt_work)
            sample_finish(1, orun1, samp[1], of1)
            dve.wait_ge(SS[1]["fin_d"], 1)
            split_lo(T_OC // 4, 0)
            split_lo(T_OC // 4, 1)
            for t in range(4):
                t1 = sqbuf[:, N * (t % 2):N * (t % 2) + N]
                if t == 0:
                    dve.wait_ge(SS[1]["fin_ps"], 1)
                dve.tensor_copy(t1, of1[:, t, :]).then_inc(sub_t, 1)
                dve.wait_ge(bhi_ready, 45 + t)
                dve.tensor_tensor(blk[:, 4 + t, :], t1, bhk[:, 4 + t, :].bitcast(F32), ALU.subtract).then_inc(b_ready, 1)

            dense(lambda i: i + T_OC // 4, 2, down, fin_post(3, G_MLP + 8), static=True)
            mlp(1, T_M1)

            dve.wait_ge(ms_ready, 5)
            dve.tensor_scalar(r_tok, bank[4][:, 0:5], 1.0 / D, EPS, ALU.mult, ALU.add).then_inc(v_ready, 1)
            dve.wait_ge(sqrt_ready, 5)
            dve.reciprocal(r_tok, r_tok).then_inc(rtok_ready, 1)
            dve.wait_ge(rtok_ready, 1)
            for t in range(1, 5, 2):
                dve.wait_ge(yt_ps, t + 1)
                dve.wait_ge(yt_done, t)
                dve.tensor_scalar(y_tok[:, t, :], y_ps[t][:, :], r_tok[:, t:t + 1], None, ALU.mult).then_inc(yt_done, 1)

        @block.scalar
        def _(act):
            def split_hi(G, q, free=True):
                j = q % 2
                if j == 0:
                    act.wait_ge(raw_loaded[q // 2], G * 16 + 16)
                act.activation(whi_v[j], raw_v[q // 2][:, :, j, :], ACT.Copy).then_inc(whi_ready, 1)

            def dense(group, n_groups, post=None, peel=False, hook=None, static=False, last=False):
                def four(G, i):
                    for q in range(4):
                        act.wait_ge(tile_done, G * 4 + (q + 1))
                        if not (last and q >= 2 and i == n_groups - 1):
                            split_hi(*((G, q + 2) if q < 2 else (G + 1, q - 2)))
                        if hook and q == 0 and isinstance(i, int) and i == 0:
                            hook()
                        if post:
                            post(G, i, q)
                done = 0
                while done < n_groups and (static or n_groups - done == 1 or (peel and done == 0)):
                    four(group(done), done)
                    done += 1
                if done < n_groups:
                    with act.Fori(done, n_groups) as i:
                        four(group(i), i)

            def root(f):
                def go():
                    act.wait_ge(v_ready, f + 1)
                    act.activation(rnorm[:, :], rnorm[:, :], ACT.Sqrt).then_inc(sqrt_ready, 1)
                return go

            def up_post(s0, b0):
                def post(G, i, q):
                    act.wait_ge(sq_up, s0 + i * 4 + (q + 1))
                    act.activation(b_hi[:, ds(i * (4 * N) + q * N, N)], sqbuf[:, N * (q % 2):N * (q % 2) + N],
                                   ACT.Copy).then_inc(bhi_ready, 1)
                return post

            def fin_post(f, gcol, ready, r0, hi=True, square=True):
                def post(G, i, q):
                    k = 4 * i + q
                    act.wait_ge(ready, r0 + k + 1)
                    if hi:
                        act.activation(ahk[:, k, :], xk[:, k, :], ACT.Copy,
                                       scale=gains[:, gcol + k:gcol + k + 1]).then_inc(ahi_ready, 1)
                    if not square:
                        return
                    if 8 * f + k >= 2:
                        act.wait_ge(sqs_done, 8 * f + k - 1)
                    act.activation(zbuf[:, N * (k % 2):N * (k % 2) + N], xk[:, k, :], ACT.Square).then_inc(xsq_ready, 1)
                return post

            def mlp(L, t0):
                G0, fb = t0 // 4, (8, 48)[L]
                dense(lambda i: i + G0, 2, up_post(32 * L, fb), peel=True, hook=root(1 + 2 * L))
                dense(lambda i: i + (G0 + 2), 2)
                with act.Fori(1, 3) as c:
                    dense(lambda i: c * 4 + (i + G0), 2, up_post(c * 8 + 32 * L, fb))
                    dense(lambda i: c * 4 + (i + (G0 + 2)), 2)
                dense(lambda i: i + (G0 + 12), 2, up_post(24 + 32 * L, fb))
                dense(lambda i: i + (G0 + 14), 2,
                      fin_post(2 + 2 * L, G_MIX + 8, acc_free, 2 + t0 + 56, hi=(L == 0)), static=True, last=(L == 1))

            def token_major(T):
                for c in range(5):
                    n = 5 * T + c
                    act.wait_ge(tk_ps, n + 1)
                    if K_BEFORE[n]:
                        act.wait_ge(kout[n % 2], 16 * K_BEFORE[n])
                    rows = P if c < 4 else NS
                    act.activation(k_tok[n % 2][0:rows, :], bank[4 + c % 2][0:rows, :], ACT.Copy).then_inc(tk_done, 1)

            def sample_attention(L, pt, stat, other_work):
                B, S, nb = BLK[L], SS[L], BLK[L]["nb"]

                def keys(b, i, pages):
                    for p in pages:
                        if p >= B["pages"][i]:
                            continue
                        act.wait_ge(S["kt_ps"], b * B["pn"] + (4 * i + p + 1))
                        act.activation(kt_sa[L][i % 2][:, :, p, :], bank[0].rearrange("p (i n) -> p i n", i=4),
                                       ACT.Copy).then_inc(S["kt_a"], 1)

                keys(0, 0, (0, 2))
                for b in range(NB):
                    for i in range(nb):
                        keys_beside(L, b, i, keys, (0,))
                        neg, w = stat[:, S_NEG + i:S_NEG + i + 1], B["cols"][i]
                        act.wait_ge(S["neg"], b * nb + (i + 1))
                        at_least(act, S["pt_ps"], b * nb + i)
                        act.activation(e_sa[L][i % 2][:, 0:w], SCORES[:, 0:w], ACT.Exp, bias=neg,
                                       accum_out=stat[:, S_SUM + i:S_SUM + i + 1]).then_inc(S["e"], 1)
                        if i:
                            act.activation(stat[:, S_ALPHA + i:S_ALPHA + i + 1],
                                           stat[:, S_NEG + i - 1:S_NEG + i], ACT.Exp, bias=neg, scale=-1.0)
                        keys_beside(L, b, i, keys, (2,))
                        act.wait_ge(S["pt_ps"], b * nb + (i + 1))
                        n, rows = len(chunks(B, i)), P if i < 4 else NS
                        act.activation(pt[i % 2][0:rows, 0:P * n], WEIGHTS[0:rows, 0:P * n],
                                       ACT.Copy).then_inc(S["pt"], 1)
                        other_work(nb * b + i)

            act.wait_ge(gain_ready, 1)
            for k in range(KT_N + 2):
                if k < KT_N:
                    fin_post(0, G_MIX, x_ready, 0, square=False)(0, 0, k)
                if k in (4, 6):
                    split_hi(0, k // 2 - 2)
                if k >= 2:
                    fin_post(0, G_MIX, x_ready, 0, hi=False)(0, 0, k - 2)
            act.wait_ge(lam_d, 1)
            act.activation(lam_t[:, 130:132], lam_t[:, 128:130], ACT.Exp).then_inc(lam_e, 1)

            dense(lambda i: i, 4, peel=True, hook=root(0))
            token_major(0)

            def prompt_stage(s):
                if s < 16:
                    qt, u = s % 4, s % 2
                    nk = P * (qt + 1)
                    act.wait_ge(p0_m, s + 1)
                    if s >= 2:
                        act.wait_ge(p0_t, s - 1)
                    for m in range(2):
                        last = act.activation(e4[u][m][:, 0:nk], P0_SCORES[:, 512 * m:512 * m + nk], ACT.Exp,
                                              bias=neg0[:, u, m:m + 1], accum_out=sum0[:, u, m:m + 1])
                    last.then_inc(p0_e, 1)
                if s >= 1:
                    n = s - 1
                    nk = P * (n % 4 + 1)
                    act.wait_ge(p0_t, n + 1)
                    if n >= 2:
                        act.wait_ge(p0_pv, n - 1)
                    act.activation(pt_p0[n % 2][:, 0:nk], P0_WEIGHTS[:, 0:nk], ACT.Copy).then_inc(p0_at, 1)

            def prompt_work(m):
                beside(m, 1, prompt_stage, 16)
                if 35 <= m < 39:
                    g = m - 35
                    act.wait_ge(mix_ps, g + 1)
                    act.activation(pk[:, g, :].rearrange("p (h c) -> p h c", h=2), halves[2], ACT.Copy,
                                   scale=gains[:, G_SCALE + g:G_SCALE + g + 1]).then_inc(mix_done, 1)

            sample_attention(0, pt_l0, samp[0], prompt_work)
            act.wait_ge(SS[0]["o_ps"], 5 * NB)
            act.wait_ge(mix_done, 4)
            for g in range(4):
                act.activation(bhk[:, g, :], pk[:, g, :], ACT.Copy).then_inc(bhi_ready, 1)
            of0 = tiles(o_feat0, 4)
            act.wait_ge(SS[0]["fin_d"], 1)
            for h in range(4):
                if h >= 2:
                    act.wait_ge(sub_ms, h - 1)
                act.activation(zbuf[:, N * (h % 2):N * (h % 2) + N], of0[:, h, :], ACT.Square).then_inc(sub_sq, 1)
            act.wait_ge(sub_v, 1)
            act.activation(r_head, r_head, ACT.Sqrt).then_inc(sub_r, 1)
            for h in range(4):
                act.wait_ge(sub_t, h + 1)
                act.activation(bhk[:, 4 + h, :], zbuf[:, N * (h % 2):N * (h % 2) + N], ACT.Copy).then_inc(bhi_ready, 1)
            dense(lambda i: i + T_OA // 4, 2, fin_post(1, G_MLP, acc_free, 2 + T_OA), static=True)
            mlp(0, T_M0)

            dense(lambda i: i + T_CD // 4, 3, peel=True, hook=root(2))

            def group_exp(g, n, scores):
                c, par, its = units1[g][n]
                act.wait_ge(p1_m, 8 * g + n + 1)
                for k, it in enumerate(its):
                    if it >= 3:
                        act.wait_ge(p1_t, it - 2)
                    for t in range(4):
                        h = 4 * par + t
                        dst = sum1[:, g, c, h:h + 1] if k == 0 else sump[:, c, h:h + 1]
                        last = act.activation(e_p1[it % 3][:, P * t:P * t + P], scores(it)[:, P * t:P * t + P], ACT.Exp,
                                              bias=neg1[:, g, c, h:h + 1], accum_out=dst)
                    last.then_inc(p1_e, 1)

            def group_weights(g, n, weights):
                for it in units1[g][n][2]:
                    act.wait_ge(p1_t, it + 1)
                    if it >= 2:
                        act.wait_ge(p1_pv, UNIT_OF[it - 2] + 1)
                    act.activation(pt_l1[it % 2][:, :], weights(it)[:, :], ACT.Copy).then_inc(p1_pt, 1)

            for g in range(3):
                if g < 2:
                    dense(lambda i: i + (T_CD // 4 + 3 + 3 * g), 3)
                    for k in range(4 if g == 0 else 0):
                        act.wait_ge(sub_t, 4 + k + 1)
                        act.activation(bhk[:, k, :], cv[:, N * k:N * k + N], ACT.Copy).then_inc(bhi_ready, 1)
                    if g == 0:
                        act.wait_ge(b_ready, 44)
                else:
                    dense(lambda i: i + (T_CD // 4 + 9), 2)
                    dense(lambda i: i + (T_CD // 4 + 11), 1, last=True)
                token_major(1 + g)
                for s in range(8 + 2 if g < 2 else 0):
                    if s >= 2:
                        group_weights(g, s - 2, lambda it: bank[4 + it % 2])
                    if s < 8:
                        group_exp(g, s, lambda it: bank[it % 4])

            def prompt_stage(s):
                if s < 8:
                    group_exp(2, s, lambda it: P1_SCORES)
                if s >= 1:
                    group_weights(2, s - 1, lambda it: P1_WEIGHTS)

            def relative():
                act.wait_ge(cb_x, 1)
                for g in range(3):
                    act.activation(nm[g][0:8, :], nm[g][0:8, :], ACT.Exp).then_inc(cb_e, 1)

            def prompt_work(m):
                beside(m, 1, prompt_stage, 8)
                if m == 23:
                    relative()

            act.wait_ge(qs_saved, 8)
            sample_attention(1, pt_s1, samp[1], prompt_work)
            act.wait_ge(SS[1]["fin_ps"], 1)
            split_hi(T_OC // 4, 0)
            split_hi(T_OC // 4, 1)
            for t in range(4):
                act.wait_ge(sub_t, 8 + t + 1)
                act.activation(bhk[:, 4 + t, :], sqbuf[:, N * (t % 2):N * (t % 2) + N], ACT.Copy).then_inc(bhi_ready, 1)
            dense(lambda i: i + T_OC // 4, 2, fin_post(3, G_MLP + 8, acc_free, 2 + T_OC), static=True)
            mlp(1, T_M1)

            act.wait_ge(v_ready, 5)
            act.activation(r_tok, r_tok, ACT.Sqrt).then_inc(sqrt_ready, 1)
            act.wait_ge(rtok_ready, 1)
            for t in range(0, 5, 2):
                rows = P if t < 4 else NS
                act.wait_ge(yt_ps, t + 1)
                if t:
                    act.wait_ge(yt_done, t)
                act.activation(y_tok[0:rows, t, :], y_ps[t][0:rows, :], ACT.Copy,
                               scale=r_tok[0:rows, t:t + 1]).then_inc(yt_done, 1)

        @block.gpsimd
        def _(pool):
            steps = Tally()

            def link(ins):
                ins.then_inc(pool_step, 1)
                pool.wait_ge(pool_step, steps.add())

            def sum_squares(f):
                for k in range(KT_N):
                    pool.wait_ge(xsq_ready, 8 * f + k + 1)
                    src = zbuf[:, N * (k % 2):N * (k % 2) + N]
                    if k == 0:
                        if f:
                            pool.wait_ge(ms_ready, f)
                        pool.tensor_copy(sqsum[:, :], src).then_inc(sqs_done, 1)
                    else:
                        pool.wait_ge(sqs_done, 8 * f + k)
                        pool.tensor_tensor(sqsum[:, :], sqsum[:, :], src, ALU.add).then_inc(sqs_done, 1)

            def save_samples(n, g, qb):
                pool.wait_ge(q_scaled, n)
                pool.tensor_copy(q_s[:, g, :, :], pk[:, qb:qb + 4, SEQ:N]).then_inc(qs_saved, 1)
                pool.tensor_copy(k_s[:, g, :, :], pk[:, qb + 4:qb + 8, SEQ:N]).then_inc(qs_saved, 1)

            def stage_queries(L, groups):
                S = SS[L]
                pool.wait_ge(qs_saved, (2, 8)[L])

                def stage(b):
                    if b >= 2:
                        pool.wait_ge(S["s"], BLK[L]["nb"] * (b - 1))
                    for hf in range(2):
                        if b or hf:
                            pool.wait_ge(S["q"], b * 2 + hf)
                        pool.tensor_copy(staged[L][b % 2][64 * hf:64 * hf + 64, 0:groups, :, 8 * hf:8 * hf + 8],
                                         q_s[64 * hf:64 * hf + 64, 0:groups, :, 8 * b:8 * b + 8]).then_inc(S["q"], 1)

                def values(b, i):
                    load_block(pool, 0, 1, b, i, 0)
                    load_block(pool, 0, 1, b, i, 1)

                stage(0)
                if L == 0:
                    pool.wait_ge(tile_done, T_AB + 16)
                for b in range(NB):
                    if L == 0 and b:
                        values(b, 0)
                    if L == 0:
                        values(b, 1)
                    if b < NB - 1:
                        stage(b + 1)
                    if L == 0:
                        values(b, 2)
                        values(b, 3)
                pool.wait_ge(S["q"], 2 * NB)

            def copy(dst, src):
                pool.dma_start(dst, src).then_inc(outs[3], 16)

            pool.memset(q_st, 0.0).then_inc(q_zero, 1)
            pool.wait_ge(q_zero, 1)
            copy(a["new_pool_sample"][0][:, 0:7, :], a["state_a_pool"][0][:, 8:15, :])
            sum_squares(0)
            pool.wait_ge(s_page, 16)
            load_block(pool, 0, 1, 0, 0, 0)
            load_block(pool, 0, 1, 0, 0, 1)
            link(pool.memset(pool_a[:, :, 0:16], 0.0))

            pool.wait_ge(hist_done, 1)
            pool.wait_ge(rows_ps, 1)
            for g in range(4):
                w = 2 << g
                u = pk[:, g, 0:SEQ]
                us = pk[:, g, SEQ:N].rearrange("p (b c) -> p b c", b=NB)
                if g:
                    pool.wait_ge(pm_ready, g)
                pool.tensor_copy(pool_s[:, 0, :, 0:15], hist_f[:, g, :, :])
                pool.tensor_copy(pool_s[:, 0, :, 15:23], us)
                link(pool.tensor_copy(pool_a[:, 0, 16:528], u))
                for j in range(g + 1):
                    d, s, k = pool_a[:, (j + 1) % 2, :], pool_a[:, j % 2, :], 1 << j
                    ss_, sd = pool_s[:, j % 2, :, :], pool_s[:, (j + 1) % 2, :, :]
                    pool.tensor_tensor(sd[:, :, 2 * k - 1:23], ss_[:, :, 2 * k - 1:23], ss_[:, :, k - 1:23 - k], ALU.add)
                    link(pool.tensor_tensor(d[:, 16:528], s[:, 16:528], s[:, 16 - k:528 - k], ALU.add))
                m, ms = pool_a[:, (g + 1) % 2, :], pool_s[:, (g + 1) % 2, :, 15:23]
                pool.tensor_tensor(m[:, 16:16 + w - 1], m[:, 16:16 + w - 1], cc("rtab")[:, 0:w - 1], ALU.mult)
                pool.tensor_scalar(ms, ms, 1.0 / w, None, ALU.mult)
                link(pool.tensor_scalar(m[:, 16 + w - 1:528], m[:, 16 + w - 1:528], 1.0 / w, None, ALU.mult))
                pool.tensor_tensor(us, ms, us, ALU.subtract)
                pool.tensor_tensor(u, m[:, 16:528], u, ALU.subtract).then_inc(pm_ready, 1)
            save_samples(1, 0, 4)
            pool.wait_ge(pm_ready, 4)
            stage_queries(0, 1)
            sum_squares(1)

            def kept(g):
                return (a[f"new_d{g}_sample"][0].rearrange("b t v h e -> b t (v h e)"),
                        a[f"cache_d{g}_kv"][0].rearrange("b t v h e -> b t (v h e)"))

            def piece(g, b, row, rows, cut):
                dst, src = kept(g)
                f = lambda v, r: (v[ds(b, 1), ds(r, rows), :].rearrange("o t f -> (o t f)")
                                  .rearrange("(p q) -> p q", q=cut))
                copy(f(dst, row), f(src, row + TS))

            QROWS = (WIN[2] - TS) // 4
            with pool.Fori(0, NB - 1) as b:
                for q in range(4):
                    pool.wait_ge(tile_done, b * 8 + (T_M0 + 2 * q + 1))
                    piece(2, b, QROWS * q, QROWS, QROWS * 1024 // 32)
            sum_squares(2)

            for g in range(3):
                save_samples(2 + g, g, 0)
            pool.wait_ge(tile_done, T_CD + 48)
            pool.memset(q_st1, 0.0).then_inc(q_zero, 1)
            pool.wait_ge(q_zero, 2)
            stage_queries(1, 3)
            sum_squares(3)
            for q in range(4):
                pool.wait_ge(tile_done, T_M1 + 2 * q + 1)
                piece(2, NB - 1, QROWS * q, QROWS, QROWS * 1024 // 32)
            with pool.Fori(0, NB) as b:
                pool.wait_ge(tile_done, b * 2 + (T_M1 + 9))
                piece(1, b, 0, WIN[1] - TS, (WIN[1] - TS) * 1024 // 32)
            for b in range(0, NB, 4):
                pool.wait_ge(tile_done, T_M1 + 25 + b // 2)
                dst, src = kept(0)
                copy(dst[b:b + 4, 0:WIN[0] - TS, :], src[b:b + 4, TS:WIN[0], :])
            sum_squares(4)
            pool.wait_ge(outs[3], 16 * (1 + 32 + 8 + 2))


_SHAPES = [("y_prompt", (1, SEQ, D)), ("y_sample", (NB, TS, D)), ("new_pool_prompt", (1, 1, 15, 512)),
           ("new_pool_sample", (1, NB, 15, 512)), ("new_bkv_prompt", (1, 1, SEQ, 2, 4, 128)),
           ("new_bkv_sample", (1, NB, TS, 2, 4, 128)), ("new_conv_prompt", (1, 1, 2, 512)),
           ("new_conv_sample", (1, NB, 2, 512))]
for _g in range(3):
    _SHAPES += [(f"new_d{_g}_prompt", (1, 1, min(WIN[_g], SEQ), 2, 8, 64)),
                (f"new_d{_g}_sample", (1, NB, WIN[_g], 2, 8, 64))]


def kernel(**inputs):
    import concourse.bacc as bacc
    from concourse.bass_utils import run_bass_kernel_spmd

    nc = bacc.Bacc("TRN2", target_bir_lowering=False, num_devices=1)
    arrays = {name: np.ascontiguousarray(v) for name, v in inputs.items()}
    arrays["consts"] = constants()
    arrays = {f"in_{name}": v for name, v in arrays.items()}
    aps = {name[3:]: nc.dram_tensor(name, v.shape, mybir.dt.from_np(v.dtype), kind="ExternalInput").ap()
           for name, v in arrays.items()}
    for name, shape in _SHAPES:
        aps[name] = nc.dram_tensor(f"out_{name}", shape, F32, kind="ExternalOutput").ap()
    build(nc, aps)
    r = run_bass_kernel_spmd(nc, [arrays], core_ids=[0])
    return tuple(r.results[0][f"out_{name}"] for name, _ in _SHAPES)
```
